# Optimizing a Trainium2 kernel written in Bass

```python
import jax, jax.numpy as jnp
from jax import lax
import numpy as np

D_MODEL = 1024
BATCH = 1
SEQ = 1024
DEPTH = 1

N_META = 16
EPS = 1e-6
MLA_HEADS = 8
MLA_NOPE = 64
MLA_ROPE = 32
MLA_V = 64
Q_LORA = 384
KV_LORA = 256
ROPE_BASE = 10000.0
Q_BLOCK = 128
MLA_WIDTH = MLA_HEADS * MLA_V
HG_HEADS = 4
HG_DK = 128
HG_DV = 128
HG_CHUNK = 64
HG_FWIDTH = HG_HEADS * HG_DK
HG_WIDTH = HG_HEADS * HG_DV
N_GROUPS = 8
EXPERTS_PER_GROUP = 8
N_EXPERTS = N_GROUPS * EXPERTS_PER_GROUP
TOP_K = 2
D_EXPERT = 256
MOE_BLOCK = 128
IN_SIZES = (Q_LORA, KV_LORA, MLA_ROPE, HG_FWIDTH, HG_FWIDTH, HG_WIDTH, HG_WIDTH, D_MODEL, D_MODEL)
D_IN = sum(IN_SIZES)

kernel_name = 'hybrid_mla_hgrn2_hiermoe_block'

def rmsnorm(x, g):
    x32 = x.astype(jnp.float32)
    y = x32 * lax.rsqrt(jnp.mean(x32 * x32, axis=-1, keepdims=True) + EPS)
    return (y * g.astype(jnp.float32)).astype(x.dtype)

def rope_tables(L):
    inv = ROPE_BASE ** (-jnp.arange(0, MLA_ROPE, 2, dtype=jnp.float32) / MLA_ROPE)
    ang = jnp.arange(L, dtype=jnp.float32)[:, None] * inv[None, :]
    return jnp.cos(ang), jnp.sin(ang)

def apply_rope(x, cos, sin):
    x1, x2 = jnp.split(x.astype(jnp.float32), 2, axis=-1)
    return jnp.concatenate([x1 * cos - x2 * sin, x2 * cos + x1 * sin], axis=-1).astype(x.dtype)

def mla_branch(c_q, c_kv, k_pe, q_norm, w_uq, kv_norm, w_ukv, cos, sin):
    B, L, _ = c_q.shape
    q = (rmsnorm(c_q, q_norm) @ w_uq).reshape(B, L, MLA_HEADS, MLA_NOPE + MLA_ROPE)
    q_nope, q_pe = q[..., :MLA_NOPE], q[..., MLA_NOPE:]
    q_pe = apply_rope(q_pe, cos[:, None, :], sin[:, None, :])
    kv = (rmsnorm(c_kv, kv_norm) @ w_ukv).reshape(B, L, MLA_HEADS, MLA_NOPE + MLA_V)
    k_nope, v = kv[..., :MLA_NOPE], kv[..., MLA_NOPE:]
    k_pe = apply_rope(k_pe, cos, sin)
    k_idx = jnp.arange(L)
    scale = (MLA_NOPE + MLA_ROPE) ** -0.5

    def attend(qn, qp, q_idx):
        s = jnp.einsum('bqhd,bkhd->bhqk', qn, k_nope) + jnp.einsum('bqhd,bkd->bhqk', qp, k_pe)
        s = s.astype(jnp.float32) * scale
        s = jnp.where(k_idx[None, :] <= q_idx[:, None], s, -jnp.inf)
        p = jax.nn.softmax(s, axis=-1).astype(v.dtype)
        return jnp.einsum('bhqk,bkhd->bqhd', p, v)

    o_meta = attend(q_nope[:, :N_META], q_pe[:, :N_META], k_idx[:N_META])
    n_blk = (L - N_META) // Q_BLOCK

    def to_blocks(t):
        return jnp.moveaxis(t[:, N_META:].reshape(B, n_blk, Q_BLOCK, *t.shape[2:]), 1, 0)

    idx_blocks = jnp.arange(N_META, L).reshape(n_blk, Q_BLOCK)
    o_blocks = lax.map(lambda a: attend(*a), (to_blocks(q_nope), to_blocks(q_pe), idx_blocks))
    o_real = jnp.moveaxis(o_blocks, 0, 1).reshape(B, L - N_META, MLA_HEADS, MLA_V)
    return jnp.concatenate([o_meta, o_real], axis=1).reshape(B, L, MLA_WIDTH)

def hgrn2_branch(q_raw, f_raw, i_raw, g_raw, lb, hg_norm):
    B, L, _ = q_raw.shape
    f32 = jnp.float32
    f = lb.astype(f32) + (1.0 - lb.astype(f32)) * jax.nn.sigmoid(f_raw.astype(f32))
    log_f = jnp.log(f)
    k = 1.0 - f
    q = jax.nn.silu(q_raw.astype(f32))
    v = i_raw.astype(f32)
    pad = HG_CHUNK - N_META
    n_c = (L + pad) // HG_CHUNK

    def heads(t, d):
        t = t.reshape(B, L, HG_HEADS, d).transpose(0, 2, 1, 3)
        t = jnp.pad(t, ((0, 0), (0, 0), (pad, 0), (0, 0)))
        return jnp.moveaxis(t.reshape(B, HG_HEADS, n_c, HG_CHUNK, d), 2, 0)

    qc, kc, vc, lfc = heads(q, HG_DK), heads(k, HG_DK), heads(v, HG_DV), heads(log_f, HG_DK)
    causal = jnp.tril(jnp.ones((HG_CHUNK, HG_CHUNK), dtype=bool))

    def chunk_step(S, inp):
        q_c, k_c, v_c, lf_c = inp
        b = jnp.cumsum(lf_c, axis=2)
        o_inter = jnp.einsum('bhtk,bhkv->bhtv', q_c * jnp.exp(b), S)
        rel = b[:, :, :, None, :] - b[:, :, None, :, :]
        decay = jnp.exp(jnp.where(causal[:, :, None], rel, -jnp.inf))
        A = jnp.einsum('bhtk,bhsk,bhtsk->bhts', q_c, k_c, decay)
        o_c = o_inter + jnp.einsum('bhts,bhsv->bhtv', A, v_c)
        b_end = b[:, :, -1:, :]
        S_new = jnp.exp(b_end[:, :, 0, :, None]) * S + jnp.einsum(
            'bhsk,bhsv->bhkv', k_c * jnp.exp(b_end - b), v_c)
        return S_new, o_c

    S0 = jnp.zeros((B, HG_HEADS, HG_DK, HG_DV), f32)
    _, o = lax.scan(chunk_step, S0, (qc, kc, vc, lfc))
    o = jnp.moveaxis(o, 0, 2).reshape(B, HG_HEADS, n_c * HG_CHUNK, HG_DV)[:, :, pad:]
    o = o.transpose(0, 2, 1, 3)
    o = o * lax.rsqrt(jnp.mean(o * o, axis=-1, keepdims=True) + EPS)
    o = o.reshape(B, L, HG_WIDTH) * hg_norm.astype(f32) * jax.nn.silu(g_raw.astype(f32))
    return o.astype(q_raw.dtype)

def hier_moe(xf, w_group, b_group, w_route, b_route, w1, w3, w2):
    N, D = xf.shape
    g_logits = (xf @ w_group + b_group).astype(jnp.float32)
    p_group = jax.nn.softmax(g_logits, axis=-1)
    g_sel = jnp.argmax(g_logits, axis=-1)
    p_sel = jnp.take_along_axis(p_group, g_sel[:, None], axis=-1)
    e_logits = (xf @ w_route + b_route).astype(jnp.float32).reshape(N, N_GROUPS, EXPERTS_PER_GROUP)
    e_in_group = jnp.take_along_axis(e_logits, g_sel[:, None, None], axis=1)[:, 0]
    top_val, top_idx = lax.top_k(e_in_group, TOP_K)
    gate = (p_sel * jax.nn.softmax(top_val, axis=-1)).astype(xf.dtype)
    expert = g_sel[:, None] * EXPERTS_PER_GROUP + top_idx

    A = N * TOP_K
    flat_e = expert.reshape(A)
    flat_tok = jnp.broadcast_to(jnp.arange(N, dtype=jnp.int32)[:, None], (N, TOP_K)).reshape(A)
    flat_w = gate.reshape(A)
    order = jnp.argsort(flat_e)
    e_sorted = flat_e[order]
    counts = jnp.bincount(flat_e, length=N_EXPERTS)
    start = jnp.cumsum(counts) - counts
    padded = (counts + MOE_BLOCK - 1) // MOE_BLOCK * MOE_BLOCK
    p_end = jnp.cumsum(padded)
    p_start = p_end - padded
    dest = p_start[e_sorted] + (jnp.arange(A) - start[e_sorted])
    n_blocks = -(-A // MOE_BLOCK) + N_EXPERTS
    R = n_blocks * MOE_BLOCK
    buf_tok = jnp.full((R,), N, dtype=jnp.int32).at[dest].set(flat_tok[order])
    buf_w = jnp.zeros((R,), xf.dtype).at[dest].set(flat_w[order])
    blk_expert = jnp.minimum(
        jnp.searchsorted(p_end, jnp.arange(n_blocks) * MOE_BLOCK, side='right'), N_EXPERTS - 1)
    x_pad = jnp.concatenate([xf, jnp.zeros((1, D), xf.dtype)], axis=0)

    def expert_block(args):
        tok, e = args
        xb = x_pad[tok]
        hdn = jax.nn.silu(xb @ w1[e]) * (xb @ w3[e])
        return hdn @ w2[e]

    y = lax.map(expert_block, (buf_tok.reshape(n_blocks, MOE_BLOCK), blk_expert))
    y = y.reshape(R, D) * buf_w[:, None]
    return jnp.zeros((N + 1, D), xf.dtype).at[buf_tok].add(y)[:N]

def setup_inputs(seed: int = 0) -> dict:
    key = jax.random.key(seed)
    ks = jax.random.split(key, 24)
    f32 = jnp.float32

    def nrm(k, shape, scale):
        return jax.random.normal(k, shape, f32) * scale

    def gain(k, shape):
        return 1.0 + 0.02 * jax.random.normal(k, shape, f32)

    return {
        'x': nrm(ks[0], (BATCH, SEQ, D_MODEL), 1.0),
        'meta_tokens': nrm(ks[1], (N_META, D_MODEL), 1.0),
        'attn_norm': gain(ks[2], (DEPTH, D_MODEL)),
        'w_in': nrm(ks[3], (DEPTH, D_MODEL, D_IN), D_MODEL ** -0.5),
        'q_norm': gain(ks[4], (DEPTH, Q_LORA)),
        'w_uq': nrm(ks[5], (DEPTH, Q_LORA, MLA_HEADS * (MLA_NOPE + MLA_ROPE)), Q_LORA ** -0.5),
        'kv_norm': gain(ks[6], (DEPTH, KV_LORA)),
        'w_ukv': nrm(ks[7], (DEPTH, KV_LORA, MLA_HEADS * (MLA_NOPE + MLA_V)), KV_LORA ** -0.5),
        'lb_table': nrm(ks[8], (DEPTH + 1, HG_FWIDTH), 0.5),
        'hg_norm': gain(ks[9], (DEPTH, HG_WIDTH)),
        'w_br_mla': nrm(ks[10], (DEPTH, MLA_WIDTH, D_MODEL), MLA_WIDTH ** -0.5),
        'w_br_hgrn': nrm(ks[11], (DEPTH, HG_WIDTH, D_MODEL), HG_WIDTH ** -0.5),
        'b_gate': nrm(ks[12], (DEPTH, 2, D_MODEL), 0.02),
        'w_out': nrm(ks[13], (DEPTH, D_MODEL, D_MODEL), D_MODEL ** -0.5),
        'ffn_norm': gain(ks[14], (DEPTH, D_MODEL)),
        'w_group': nrm(ks[15], (DEPTH, D_MODEL, N_GROUPS), D_MODEL ** -0.5),
        'b_group': nrm(ks[16], (DEPTH, N_GROUPS), 0.01),
        'w_route': nrm(ks[17], (DEPTH, D_MODEL, N_EXPERTS), D_MODEL ** -0.5),
        'b_route': nrm(ks[18], (DEPTH, N_EXPERTS), 0.01),
        'w1': nrm(ks[19], (DEPTH, N_EXPERTS, D_MODEL, D_EXPERT), D_MODEL ** -0.5),
        'w3': nrm(ks[20], (DEPTH, N_EXPERTS, D_MODEL, D_EXPERT), D_MODEL ** -0.5),
        'w2': nrm(ks[21], (DEPTH, N_EXPERTS, D_EXPERT, D_MODEL), D_EXPERT ** -0.5),
        'final_norm': gain(ks[22], (D_MODEL,)),
    }

def reference(x, meta_tokens, attn_norm, w_in, q_norm, w_uq, kv_norm, w_ukv, lb_table, hg_norm,
              w_br_mla, w_br_hgrn, b_gate, w_out, ffn_norm, w_group, b_group, w_route, b_route,
              w1, w3, w2, final_norm):
    B, S, D = x.shape
    L = S + N_META
    h = jnp.concatenate([jnp.broadcast_to(meta_tokens[None].astype(x.dtype), (B, N_META, D)), x], axis=1)
    cos, sin = rope_tables(L)
    lbs = jnp.cumsum(jax.nn.softmax(lb_table.astype(jnp.float32), axis=0), axis=0)
    split_idx = [int(c) for c in np.cumsum(IN_SIZES)[:-1]]
    for l in range(DEPTH):
        u = rmsnorm(h, attn_norm[l])
        proj = u @ w_in[l]
        c_q, c_kv, k_pe, hq, hf, hi, hg, gm, gh = jnp.split(proj, split_idx, axis=-1)
        o_mla = mla_branch(c_q, c_kv, k_pe, q_norm[l], w_uq[l], kv_norm[l], w_ukv[l], cos, sin)
        o_hg = hgrn2_branch(hq, hf, hi, hg, lbs[l], hg_norm[l])
        gate_m = jax.nn.sigmoid(gm + b_gate[l, 0])
        gate_h = jax.nn.sigmoid(gh + b_gate[l, 1])
        merged = gate_m * (o_mla @ w_br_mla[l]) + gate_h * (o_hg @ w_br_hgrn[l])
        h = h + merged @ w_out[l]
        u = rmsnorm(h, ffn_norm[l])
        h = h + hier_moe(u.reshape(B * L, D), w_group[l], b_group[l], w_route[l], b_route[l],
                         w1[l], w3[l], w2[l]).reshape(B, L, D)
    return rmsnorm(h, final_norm)[:, N_META:]


_drawn_inputs = setup_inputs


def setup_inputs(seed=0):
    import zlib

    import numpy as np

    out = dict(_drawn_inputs(seed))
    spreads = {}
    factors = {'attn_norm': 3.287,
     'q_norm': 8.0,
     'kv_norm': 8.0,
     'hg_norm': 15.547,
     'b_gate': 6.649,
     'b_group': 36.88,
     'b_route': 39.944,
     'final_norm': 7.975,
     'ffn_norm': 8.0,
     'w_group': 2.729,
     'w_route': 2.915,
     'w1': 2.715}
    for name, (base, spread) in spreads.items():
        noise = np.random.default_rng([zlib.crc32(name.encode()), seed]).standard_normal(out[name].shape)
        drawn = base * np.exp(spread * noise) if base else spread * noise
        out[name] = __import__('jax').numpy.asarray(drawn.astype(out[name].dtype))
    for name, factor in factors.items():
        out[name] = (out[name] * factor).astype(out[name].dtype)
    return out
```

```python
from contextlib import ExitStack

import numpy as np
import concourse.bass as bass
from concourse import mybir

F32 = mybir.dt.float32
F32R = mybir.dt.float32r
I32 = mybir.dt.int32
U32 = mybir.dt.uint32
ACT = mybir.ActivationFunctionType
ALU = mybir.AluOpType
AX = mybir.AxisListType

P = 128
D = 1024
DK = D // P
SEQ = 1024
TT = SEQ // P
META = 16
NT = SEQ + META
EPS = 1e-6
QL, KVL, ROPE = 384, 256, 32
NOPE, VD, HEADS = 64, 64, 8
QH = NOPE + ROPE
HG = 4
CH = 32
SCALE = QH ** -0.5
C_CQ, C_CKV = 0, QL
C_KPE = QL + KVL
C_HQ = C_KPE + ROPE
C_HF = C_HQ + 512
C_HI = C_HF + 512
C_HG = C_HI + 512
C_GM = C_HG + 512
GROUPS, PER_GROUP, EXPERTS, DE = 8, 8, 64, 256
ROWS = 4
SLOTS = 1024
CAP = 128
SKIP = 4096.0
SWAP = [(i + ROPE // 2) % ROPE for i in range(ROPE)]


class Steps:

    def __init__(self, eng, sem):
        self.eng, self.sem, self.base, self.k = eng, sem, 0, 0

    def mark(self, ins):
        ins.then_inc(self.sem, 1)
        self.k += 1

    def link(self, ins):
        self.mark(ins)
        self.eng.wait_ge(self.sem, self.base + self.k)

    def now(self):
        return self.base + self.k

    def enter(self, i, per):
        self.outer, self.per = self.base + self.k, per
        self.base, self.k = self.outer + i * per, 0

    def leave(self, n):
        assert self.k == self.per, (self.k, self.per)
        self.base, self.k = self.outer + n * self.per, 0


class Ctx:

    def __init__(self, a, out):
        self.x, self.meta_tokens, self.attn_norm, self.w_in = a["x"], a["meta_tokens"], a["attn_norm"], a["w_in"]
        self.q_norm, self.w_uq, self.kv_norm, self.w_ukv = a["q_norm"], a["w_uq"], a["kv_norm"], a["w_ukv"]
        self.lb_table, self.hg_norm, self.b_gate = a["lb_table"], a["hg_norm"], a["b_gate"]
        self.w_br_mla, self.w_br_hgrn, self.w_out = a["w_br_mla"], a["w_br_hgrn"], a["w_out"]
        self.ffn_norm, self.w_group, self.b_group = a["ffn_norm"], a["w_group"], a["b_group"]
        self.w_route, self.b_route, self.final_norm = a["w_route"], a["b_route"], a["final_norm"]
        self.w1, self.w3, self.w2 = a["w1"], a["w3"], a["w2"]
        self.rope_cos, self.rope_sin = a["rope_cos"], a["rope_sin"]
        self.out = out


def semaphores(nc, phase):
    made = []

    def clear():
        nc.clear_and_free_semaphores(made)
        nc.all_engine_barrier()

    phase.callback(clear)

    def sem(name):
        made.append(nc.alloc_semaphore(name=name))
        return made[-1]

    return sem


def settle(eng, g):
    eng.sem_inc(g.settled, 1)


def mm3(pe, out, lh, ll, rh, rl, start, stop):
    pe.matmul(out, lh, rh, start=start, stop=False)
    pe.matmul(out, lh, rl, start=False, stop=False)
    return pe.matmul(out, ll, rh, start=False, stop=stop)


def phase_norm_in(nc, g):
    with ExitStack() as ph:
        sb = lambda n, s, d=F32: ph.enter_context(nc.sbuf_tensor(n, s, d))
        sem = semaphores(nc, ph)
        x = sb("a_x", [P, 2, D])
        sq = sb("a_sq", [P, D])
        u = sb("a_u", [P, 2, D])
        gain = sb("a_gain", [P, D])
        ss = sb("a_ss", [P, 4])
        x_in = [sem("a_x_in0"), sem("a_x_in1")]
        const_in, meta_in = sem("a_const_in"), sem("a_meta_in")
        ss_done, rt_done, u_done, tr_done = sem("a_ss_done"), sem("a_rt_done"), sem("a_u_done"), sem("a_tr_done")
        hi_done, lo_done, dv, consts = sem("a_hi"), sem("a_lo"), sem("a_dv"), sem("a_consts")
        block = ph.enter_context(nc.Block())

        @block.sync
        def _(sp):
            sp.dma_start(x[0:META, 1, :], g.meta_tokens).then_inc(meta_in, 16)
            sp.dma_start(gain[:, :], g.attn_norm[0:1, :].to_broadcast([P, D])).then_inc(const_in, 16)
            sp.dma_start(x[:, 0, :], g.x[0, 0:P, :]).then_inc(x_in[0], 16)
            sp.wait_ge(u_done, 1)
            sp.dma_start(x[:, 1, :], g.x[0, P:2 * P, :]).then_inc(x_in[1], 16)
            with sp.Fori(0, TT // 2 - 1) as i:
                for b in range(2):
                    sp.wait_ge(u_done, 2 * i + b + 2)
                    t = 2 * i + b + 2
                    sp.dma_start(x[:, b, :], g.x[0, bass.ds(t * P, P), :]).then_inc(x_in[b], 16)

        @block.gpsimd
        def _(pool):
            pool.memset(g.ident[:, :], 0.0).then_inc(consts, 1)
            pool.memset(g.ones[:, :], 1.0).then_inc(consts, 1)
            pool.memset(g.eps[:, :], EPS).then_inc(consts, 1)
            pool.wait_ge(consts, 3)
            pool.affine_select(out=g.ident[:, :], in_=g.ident[:, :], compare_op=ALU.not_equal, fill=1.0,
                               base=0, pattern=[[-1, P]], channel_multiplier=1).then_inc(consts, 1)

        @block.scalar
        def _(act):
            act.wait_ge(consts, 4)

            def sums(n, xs, rows, b):
                act.activation(sq[0:rows, :], xs, ACT.Square, accum_out=ss[0:rows, b:b + 1]).then_inc(ss_done, 1)
                act.wait_ge(ss_done, n + 1)
                act.activation(ss[0:rows, 2 + b:3 + b], ss[0:rows, b:b + 1], ACT.Sqrt, scale=1.0 / D,
                               bias=g.eps[0:rows, :]).then_inc(rt_done, 1)

            def evac(n, rows, b, col):
                for q in range(2):
                    act.wait_ge(tr_done, 2 * n + q + 1)
                    settle(act, g)
                    src = g.ps[:, (2 * b + q) * 512:(2 * b + q + 1) * 512].rearrange("p (j t) -> p j t", j=4)
                    act.activation(g.uTh[:, 4 * q:4 * q + 4, bass.ds(col, rows)], src[:, :, 0:rows],
                                   ACT.Copy).then_inc(hi_done, 1)

            act.wait_ge(meta_in, 16)
            sums(0, x[0:META, 1, :], META, 1)
            evac(0, META, 1, SEQ)
            with act.Fori(0, TT // 2) as i:
                for b in range(2):
                    act.wait_ge(x_in[b], 16 * i + 16)
                    act.wait_ge(u_done, 2 * i + b + 1)
                    sums(2 * i + b + 1, x[:, b, :], P, b)
                    evac(2 * i + b + 1, P, b, (2 * i + b) * P)

        @block.vector
        def _(dve):
            v = Steps(dve, dv)

            def scaled(n, rows, b):
                dve.wait_ge(rt_done, n + 1)
                v.link(dve.reciprocal(ss[0:rows, 2 + b:3 + b], ss[0:rows, 2 + b:3 + b]))
                dve.scalar_tensor_tensor(out=u[0:rows, b, :], in0=x[0:rows, b, :], scalar=ss[0:rows, 2 + b:3 + b],
                                         in1=gain[0:rows, :], op0=ALU.mult, op1=ALU.mult).then_inc(u_done, 1)

            def low(n, rows, b, col):
                for q in range(2):
                    dve.wait_ge(hi_done, 2 * n + q + 1)
                    src = g.ps[:, (2 * b + q) * 512:(2 * b + q + 1) * 512].rearrange("p (j t) -> p j t", j=4)
                    dve.tensor_tensor(g.uTl[:, 4 * q:4 * q + 4, bass.ds(col, rows)], src[:, :, 0:rows],
                                      g.uTh[:, 4 * q:4 * q + 4, bass.ds(col, rows)].bitcast(F32),
                                      ALU.subtract).then_inc(lo_done, 1)

            dve.wait_ge(const_in, 16)
            dve.wait_ge(meta_in, 16)
            scaled(0, META, 1)
            low(0, META, 1, SEQ)
            with dve.Fori(0, TT // 2) as i:
                v.enter(i, 2)
                for b in range(2):
                    dve.wait_ge(x_in[b], 16 * i + 16)
                    scaled(2 * i + b + 1, P, b)
                    low(2 * i + b + 1, P, b, (2 * i + b) * P)
                v.leave(TT // 2)

        @block.tensor
        def _(pe):
            pe.wait_ge(consts, 4)

            def flip(n, rows, b):
                pe.wait_ge(u_done, n + 1)
                for q in range(2):
                    for j in range(4):
                        last = pe.transpose(g.ps[:, (2 * b + q) * 512 + j * P:(2 * b + q) * 512 + j * P + rows],
                                            u[0:rows, b, 4 * q + j::DK], g.ident[0:rows, 0:rows])
                    last.then_inc(tr_done, 1)

            flip(0, META, 1)
            with pe.Fori(0, TT // 2) as i:
                for b in range(2):
                    pe.wait_ge(lo_done, 4 * i + 2 * b + 1)
                    flip(2 * i + b + 1, P, b)


def phase_gates(nc, g):
    NB = 2 * DK
    with ExitStack() as ph:
        sb = lambda n, s, d=F32: ph.enter_context(nc.sbuf_tensor(n, s, d))
        sem = semaphores(nc, ph)
        w = [sb(f"g_w{b}", [P, DK, P]) for b in range(2)]
        wh = [sb(f"g_wh{b}", [P, DK, P], F32R) for b in range(2)]
        wl = [sb(f"g_wl{b}", [P, DK, P], F32R) for b in range(2)]
        sg = [sb(f"g_sg{b}", [P, SEQ]) for b in range(2)]
        bias = sb("g_bias", [P, NB])
        w_in = [sem(f"g_w_in{b}") for b in range(2)]
        out_sem = [sem(f"g_out{b}") for b in range(2)]
        bias_in, wh_done, wl_done, mm_done, sg_done = (sem("g_bias_in"), sem("g_wh_done"), sem("g_wl_done"),
                                                       sem("g_mm_done"), sem("g_sg_done"))
        block = ph.enter_context(nc.Block())
        w_src = g.w_in[0].rearrange("(p j) n -> p j n", j=DK)

        @block.sync
        def _(sp):
            with nc.allow_non_contiguous_dma(reason="a small bias turned once"):
                sp.dma_start(bias[:, :], g.b_gate[0].rearrange("a (j p) -> p (a j)", p=P)).then_inc(bias_in, 16)
            for b in range(2):
                sp.dma_start(w[b][:, :, :], w_src[:, :, C_GM + b * P:C_GM + (b + 1) * P]).then_inc(w_in[b], 16)
            with sp.Fori(0, NB // 2 - 1) as i:
                for b in range(2):
                    sp.wait_ge(wl_done, 2 * i + b + 1)
                    sp.dma_start(w[b][:, :, :], w_src[:, :, bass.ds(C_GM + (2 * i + b + 2) * P, P)]).then_inc(w_in[b], 16)

        @block.gpsimd
        def _(pool):
            with pool.Fori(0, NB // 2) as i:
                for b in range(2):
                    pool.wait_ge(sg_done, 4 * i + 2 * b + 2)
                    settle(pool, g)
                    pool.dma_start(g.gates[bass.ds((2 * i + b) * P, P), :], sg[b][:, :]).then_inc(out_sem[b], 16)
            for b in range(2):
                pool.wait_ge(out_sem[b], 16 * (NB // 2))

        @block.scalar
        def _(act):
            act.wait_ge(bias_in, 16)

            def split(b, turn):
                act.wait_ge(w_in[b], 16 * turn + 16)
                act.activation(wh[b][:, :, :], w[b][:, :, :], ACT.Copy).then_inc(wh_done, 1)

            def gate(b, n):
                for q in range(2):
                    act.wait_ge(mm_done, 2 * n + q + 1)
                    settle(act, g)
                    act.activation(sg[b][:, q * 512:(q + 1) * 512], g.ps[:, (2 * b + q) * 512:(2 * b + q + 1) * 512],
                                   ACT.Sigmoid, bias=bias[:, bass.ds(n, 1)]).then_inc(sg_done, 1)

            split(0, 0)
            split(1, 0)
            gate(0, 0)
            act.wait_ge(mm_done, 2)
            split(0, 1)
            gate(1, 1)
            with act.Fori(0, NB // 2 - 2) as i:
                for b in range(2):
                    act.wait_ge(mm_done, 4 * i + 2 * b + 4)
                    split(1 - b, i + 1 + b)
                    act.wait_ge(out_sem[b], 16 * i + 16)
                    gate(b, 2 * i + b + 2)
            act.wait_ge(mm_done, 2 * (NB - 2))
            split(1, NB // 2 - 1)
            for b in range(2):
                act.wait_ge(out_sem[b], 16 * (NB // 2 - 1))
                gate(b, NB - 2 + b)

        @block.vector
        def _(dve):
            with dve.Fori(0, NB // 2) as i:
                for b in range(2):
                    dve.wait_ge(wh_done, 2 * i + b + 1)
                    dve.tensor_tensor(wl[b][:, :, :], w[b][:, :, :], wh[b][:, :, :].bitcast(F32),
                                      ALU.subtract).then_inc(wl_done, 1)

        @block.tensor
        def _(pe):
            def project(n, b):
                pe.wait_ge(wl_done, n + 1)
                for q in range(2):
                    for j in range(DK):
                        last = mm3(pe, g.ps[:, (2 * b + q) * 512:(2 * b + q + 1) * 512], wh[b][:, j, :], wl[b][:, j, :],
                                   g.uTh[:, j, q * 512:(q + 1) * 512], g.uTl[:, j, q * 512:(q + 1) * 512],
                                   j == 0, j == DK - 1)
                    last.then_inc(mm_done, 1)

            project(0, 0)
            project(1, 1)
            with pe.Fori(1, NB // 2) as i:
                for b in range(2):
                    pe.wait_ge(sg_done, 4 * i + 2 * b - 2)
                    project(2 * i + b, b)


def phase_hgrn(nc, g):
    NCH = SEQ // CH
    with ExitStack() as ph:
        sb = lambda n, s, d=F32: ph.enter_context(nc.sbuf_tensor(n, s, d))
        sem = semaphores(nc, ph)
        w = [sb(f"h_w{b}", [P, DK, P]) for b in range(2)]
        wh = [sb(f"h_wh{b}", [P, DK, P], F32R) for b in range(2)]
        wl = [sb(f"h_wl{b}", [P, DK, P], F32R) for b in range(2)]
        lb_raw, lb, oml, hgain = sb("h_lb_raw", [P, 2, HG]), sb("h_lb", [P, HG]), sb("h_oml", [P, HG]), sb("h_hgain", [P, HG])
        lbd = sb("h_lbd", [P, HG])
        reset = sb("h_reset", [P, NT])
        causal = sb("h_causal", [P, P])
        f, k, lf, bb, d1 = sb("h_f", [P, NT]), sb("h_k", [P, NT]), sb("h_lf", [P, NT]), sb("h_b", [P, NT]), sb("h_d1", [P, SEQ])
        qs, ks, qd, kd = sb("h_qs", [P, SEQ]), sb("h_ks", [P, SEQ]), sb("h_qd", [P, SEQ]), sb("h_kd", [P, NT])
        q, vt, gt, ot = sb("h_q", [P, SEQ]), sb("h_vt", [P, NT]), sb("h_gt", [P, SEQ]), sb("h_ot", [P, SEQ])
        dec = sb("h_dec", [P, NCH])
        v = sb("h_v", [P, TT + 1, P])
        kdn = sb("h_kdn", [P, 2, P])
        kdm = sb("h_kdm", [META, P])
        at = sb("h_at", [P, 2, P])
        vb = [sb(f"h_vb{b}", [P, 4 * P]) for b in range(2)]
        S = sb("h_S", [P, 8, P])
        vb_zero, vb_ok = sem("h_vb_zero"), sem("h_vb_ok")
        cst_in, cst, lb_ok = sem("h_cst_in"), sem("h_cst"), sem("h_lb_ok")
        w_in = [sem(f"h_w_in{b}") for b in range(2)]
        wh_done, wl_done, mm_done = sem("h_wh_done"), sem("h_wl_done"), sem("h_mm_done")
        sig_f, f_ok, lf_ok, b_ok, sig_q, e_ok, kd_ok = (sem("h_sig_f"), sem("h_f_ok"), sem("h_lf_ok"), sem("h_b_ok"),
                                                        sem("h_sig_q"), sem("h_e_ok"), sem("h_kd_ok"))
        q_ok, sig_g, g_ok, vt_ok, vtr, v_ok = (sem("h_q_ok"), sem("h_sig_g"), sem("h_g_ok"), sem("h_vt_ok"),
                                               sem("h_vtr"), sem("h_v_ok"))
        ktr, kdn_ok, s0_mm, s0_ok, a_mm, a_ok, kv_mm, s_ok, o_mm, o_ok = (
            sem("h_ktr"), sem("h_kdn_ok"), sem("h_s0_mm"), sem("h_s0_ok"), sem("h_a_mm"), sem("h_a_ok"),
            sem("h_kv_mm"), sem("h_s_ok"), sem("h_o_mm"), sem("h_o_ok"))
        sq_ok, ms_mm, rt_ok, on_ok, hi_ok, lo_ok, dv = (sem("h_sq_ok"), sem("h_ms_mm"), sem("h_rt_ok"), sem("h_on_ok"),
                                                        sem("h_hi_ok"), sem("h_lo_ok"), sem("h_dv"))
        block = ph.enter_context(nc.Block())
        w_src = g.w_in[0].rearrange("(p j) n -> p j n", j=DK)
        bank = lambda i, a=0, n=512: g.ps[:, i * 512 + a:i * 512 + a + n]
        pieces = [(0, 512), (512, 512), (SEQ, META)]
        COLS = [C_HF, C_HI, C_HQ, C_HG]
        FB, VB, QB, GB = 0, 3, 0, 3
        AB, KVB, TB, OB = 0, 3, 6, [2, 5]
        chunked = lambda t: t[:, 0:SEQ].rearrange("p (c t) -> p c t", t=CH)

        @block.sync
        def _(sp):
            with nc.allow_non_contiguous_dma(reason="small vectors turned once"):
                sp.dma_start(lb_raw[:, :, :], g.lb_table.rearrange("a (h p) -> p a h", p=P)).then_inc(cst_in, 16)
                sp.dma_start(hgain[:, :], g.hg_norm[0].rearrange("(h p) -> p h", p=P)).then_inc(cst_in, 16)
            for r in range(2):
                sp.dma_start(w[r][:, :, :], w_src[:, :, COLS[r]:COLS[r] + P]).then_inc(w_in[r], 16)
            with sp.Fori(0, HG) as h:
                for r in range(4):
                    col = COLS[(r + 2) % 4] + h * P + (P if r >= 2 else 0)
                    sp.wait_ge(wl_done, 4 * h + r + 1)
                    sp.dma_start(w[r % 2][:, :, :], w_src[:, :, bass.ds(col, P)]).then_inc(w_in[r % 2], 16)
            for b in range(2):
                sp.wait_ge(w_in[b], 16 * (2 * HG + 1))

        @block.gpsimd
        def _(pool):
            pool.memset(reset[:, :], 1.0).then_inc(cst, 1)
            pool.memset(at[:, :, :], 0.0).then_inc(cst, 1)
            pool.wait_ge(cst, 2)
            pool.memset(reset[:, 0:SEQ:CH], 0.0).then_inc(cst, 1)
            pool.memset(reset[:, SEQ:SEQ + 1], 0.0).then_inc(cst, 1)
            cv = causal[:, :].rearrange("p (c t) -> p c t", t=CH)
            ov = g.ones[:, :].rearrange("p (c t) -> p c t", t=CH)
            pool.affine_select(out=cv, in_=ov, compare_op=ALU.is_ge, fill=0.0, base=0,
                               pattern=[[CH, P // CH], [1, CH]], channel_multiplier=-1).then_inc(cst, 1)
            pool.wait_ge(cst, 5)
            pool.affine_select(out=cv, in_=cv, compare_op=ALU.is_ge, fill=0.0, base=0,
                               pattern=[[-CH, P // CH], [0, CH]], channel_multiplier=1).then_inc(cst, 1)
            for b in range(2):
                pool.memset(vb[b][:, :], 0.0).then_inc(vb_zero, 1)
            pool.wait_ge(vb_zero, 2)

            def spread(h, t):
                for ci in range(4):
                    rows = slice(ci * CH, (ci + 1) * CH)
                    pool.tensor_copy(vb[t % 2][rows, ci * P:(ci + 1) * P], v[rows, t, :]).then_inc(vb_ok, 1)

            with pool.Fori(0, HG) as h:
                for t in range(TT):
                    pool.wait_ge(v_ok, 3 * h + 2)
                    if t >= 2:
                        pool.wait_ge(kv_mm, TT * h + t - 1)
                    settle(pool, g)
                    spread(h, t)

        @block.scalar
        def _(act):
            def split(b, n_in, n_mm):
                if n_mm is not None:
                    act.wait_ge(mm_done, n_mm)
                act.wait_ge(w_in[b], n_in)
                act.activation(wh[b][:, :, :], w[b][:, :, :], ACT.Copy).then_inc(wh_done, 1)

            act.wait_ge(cst_in, 32)
            split(0, 16, None)
            split(1, 16, None)
            act.wait_ge(dv, 1)
            act.activation(lb[:, :], lbd[:, :], ACT.Sigmoid).then_inc(lb_ok, 1)
            with act.Fori(0, HG) as h:
                w0 = 32 * h + 32
                for n, (c, m) in enumerate(pieces):
                    act.wait_ge(mm_done, 10 * h + n + 1)
                    act.activation(f[:, c:c + m], bank(FB + n, 0, m), ACT.Sigmoid).then_inc(sig_f, 1)
                split(0, w0, 10 * h + 3)
                for n, (c, m) in enumerate(pieces):
                    act.wait_ge(mm_done, 10 * h + n + 4)
                    act.activation(vt[:, c:c + m], bank(VB + n, 0, m), ACT.Copy).then_inc(vt_ok, 1)
                split(1, w0, 10 * h + 6)
                for n in range(2):
                    act.wait_ge(mm_done, 10 * h + n + 7)
                    act.activation(q[:, n * 512:(n + 1) * 512], bank(QB + n), ACT.Sigmoid).then_inc(sig_q, 1)
                split(0, w0 + 16, 10 * h + 8)
                for n in range(2):
                    act.wait_ge(mm_done, 10 * h + n + 9)
                    act.activation(gt[:, n * 512:(n + 1) * 512], bank(GB + n), ACT.Sigmoid).then_inc(sig_g, 1)
                split(1, w0 + 16, 10 * h + 10)
                act.wait_ge(f_ok, h + 1)
                act.activation(lf[:, :], f[:, :], ACT.Ln).then_inc(lf_ok, 1)
                act.wait_ge(b_ok, 3 * h + 3)
                act.activation(qs[:, :], d1[:, :], ACT.Exp).then_inc(e_ok, 1)
                act.activation(ks[:, :], d1[:, :], ACT.Exp, scale=-1.0).then_inc(e_ok, 1)
                act.activation(qd[:, :], bb[:, 0:SEQ], ACT.Exp).then_inc(e_ok, 1)
                act.activation(kd[:, :], lf[:, :], ACT.Exp).then_inc(e_ok, 1)
                act.activation(dec[:, :], bb[:, CH - 1:SEQ:CH], ACT.Exp).then_inc(e_ok, 1)
                for n in range(2):
                    act.wait_ge(vtr, 3 * h + n + 1)
                    act.activation(v[:, 4 * n:4 * n + 4, :], bank(6 + n).rearrange("p (t c) -> p t c", t=4),
                                   ACT.Copy).then_inc(v_ok, 1)
                act.wait_ge(vtr, 3 * h + 3)
                act.activation(v[0:META, TT, :], g.ps[0:META, 2 * 512:2 * 512 + P], ACT.Copy).then_inc(v_ok, 1)
                act.wait_ge(ktr, 9 * h + 1)
                act.activation(kdm[:, :], g.ps[0:META, 2 * 512:2 * 512 + P], ACT.Copy).then_inc(kdn_ok, 1)
                act.wait_ge(s0_mm, h + 1)
                act.activation(S[:, 0, :], bank(5, 0, P), ACT.Copy).then_inc(s0_ok, 1)

                def kd_rows(t):
                    act.wait_ge(ktr, 9 * h + t + 2)
                    act.activation(kdn[:, t % 2, :], bank(TB + t % 2, 0, P), ACT.Copy).then_inc(kdn_ok, 1)

                kd_rows(0)
                for t in range(TT):
                    if t + 1 < TT:
                        kd_rows(t + 1)
                    act.wait_ge(o_mm, TT * h + t + 1)
                    act.activation(ot[:, t * P:(t + 1) * P], bank(OB[t % 2], 0, P), ACT.Copy).then_inc(o_ok, 1)
                act.wait_ge(o_ok, TT * h + TT)
                act.activation(d1[:, :], ot[:, :], ACT.Square).then_inc(sq_ok, 1)
                for n in range(2):
                    act.wait_ge(ms_mm, 2 * h + n + 1)
                    act.activation(qs[:, n * 512:(n + 1) * 512], bank(TB + n), ACT.Sqrt, scale=1.0 / P,
                                   bias=g.eps[:, :]).then_inc(rt_ok, 1)
                act.wait_ge(on_ok, h + 1)
                settle(act, g)
                act.activation(g.ohTh[:, bass.ds(h, 1), :], ot[:, :].rearrange("p (a t) -> p a t", a=1),
                               ACT.Copy).then_inc(hi_ok, 1)

        @block.vector
        def _(dve):
            c = Steps(dve, dv)

            def low(b, n):
                dve.wait_ge(wh_done, n)
                dve.tensor_tensor(wl[b][:, :, :], w[b][:, :, :], wh[b][:, :, :].bitcast(F32),
                                  ALU.subtract).then_inc(wl_done, 1)

            dve.wait_ge(cst_in, 32)
            c.link(dve.tensor_tensor(lbd[:, :], lb_raw[:, 0, :], lb_raw[:, 1, :], ALU.subtract))
            low(0, 1)
            low(1, 2)
            dve.wait_ge(cst, 6)
            dve.wait_ge(lb_ok, 1)
            c.link(dve.tensor_scalar(oml[:, :], lb[:, :], -1.0, 1.0, ALU.mult, ALU.add))
            with dve.Fori(0, HG) as h:
                c.enter(h, 8)
                dve.wait_ge(sig_f, 3 * h + 3)
                c.link(dve.tensor_scalar(f[:, :], f[:, :], oml[:, bass.ds(h, 1)], lb[:, bass.ds(h, 1)], ALU.mult, ALU.add))
                dve.tensor_scalar(k[:, :], f[:, :], -1.0, 1.0, ALU.mult, ALU.add).then_inc(f_ok, 1)
                low(0, 4 * h + 3)
                low(1, 4 * h + 4)
                for n in range(2):
                    dve.wait_ge(sig_q, 2 * h + n + 1)
                    dve.tensor_tensor(q[:, n * 512:(n + 1) * 512], q[:, n * 512:(n + 1) * 512], bank(QB + n),
                                      ALU.mult).then_inc(q_ok, 1)
                low(0, 4 * h + 5)
                for n in range(2):
                    dve.wait_ge(sig_g, 2 * h + n + 1)
                    dve.scalar_tensor_tensor(out=gt[:, n * 512:(n + 1) * 512], in0=gt[:, n * 512:(n + 1) * 512],
                                             scalar=hgain[:, bass.ds(h, 1)], in1=bank(GB + n),
                                             op0=ALU.mult, op1=ALU.mult).then_inc(g_ok, 1)
                low(1, 4 * h + 6)
                dve.wait_ge(lf_ok, h + 1)
                dve.tensor_tensor_scan(bb[:, :], reset[:, :], lf[:, :], 0.0, ALU.mult, ALU.add).then_inc(b_ok, 1)
                dve.wait_ge(b_ok, 3 * h + 1)
                bv, dv1, dv2 = chunked(bb), chunked(d1), chunked(lf)
                c.mark(dve.tensor_tensor(dv1, bv, bv[:, :, CH // 2 - 1:CH // 2].to_broadcast([P, NCH, CH]), ALU.subtract))
                dve.tensor_tensor(dv2, bv[:, :, CH - 1:CH].to_broadcast([P, NCH, CH]), bv, ALU.subtract).then_inc(b_ok, 1)
                dve.tensor_tensor(lf[:, SEQ:NT], bb[:, NT - 1:NT].to_broadcast([P, META]), bb[:, SEQ:NT],
                                  ALU.subtract).then_inc(b_ok, 1)
                dve.wait_ge(q_ok, 2 * h + 2)
                dve.wait_ge(e_ok, 5 * h + 5)
                c.mark(dve.tensor_tensor(qs[:, :], qs[:, :], q[:, :], ALU.mult))
                c.mark(dve.tensor_tensor(ks[:, :], ks[:, :], k[:, 0:SEQ], ALU.mult))
                c.mark(dve.tensor_tensor(qd[:, :], qd[:, :], q[:, :], ALU.mult))
                dve.tensor_tensor(kd[:, :], kd[:, :], k[:, :], ALU.mult).then_inc(kd_ok, 1)
                dve.wait_ge(s0_ok, h + 1)

                def scores(t):
                    dve.wait_ge(a_mm, TT * h + t + 1)
                    settle(dve, g)
                    dve.copy_predicated(at[:, t % 2, :], causal[:, :].bitcast(U32), bank(AB + t % 2, 0, P)).then_inc(a_ok, 1)

                scores(0)
                for t in range(TT):
                    dve.wait_ge(kv_mm, TT * h + t + 1)
                    for ci in range(4):
                        n = 4 * t + ci
                        if n == 4 * TT - 1:
                            break
                        if n:
                            dve.wait_ge(s_ok, (4 * TT - 1) * h + n)
                        if ci == 3 and t >= 1:
                            dve.wait_ge(o_mm, TT * h + t)
                        dve.scalar_tensor_tensor(out=S[:, (n + 1) % 8, :], in0=S[:, n % 8, :], scalar=dec[:, n:n + 1],
                                                 in1=bank(KVB + t % 2, ci * P, P), op0=ALU.mult,
                                                 op1=ALU.add).then_inc(s_ok, 1)
                    if t + 1 < TT:
                        scores(t + 1)
                for n in range(2):
                    dve.wait_ge(rt_ok, 2 * h + n + 1)
                c.link(dve.reciprocal(qs[:, :], qs[:, :]))
                dve.wait_ge(o_ok, TT * h + TT)
                c.link(dve.tensor_tensor(ot[:, :], ot[:, :], qs[:, :], ALU.mult))
                dve.wait_ge(g_ok, 2 * h + 2)
                dve.tensor_tensor(ot[:, :], ot[:, :], gt[:, :], ALU.mult).then_inc(on_ok, 1)
                dve.wait_ge(hi_ok, h + 1)
                c.mark(dve.tensor_tensor(g.ohTl[:, bass.ds(h, 1), :], ot[:, :].rearrange("p (a t) -> p a t", a=1),
                                         g.ohTh[:, bass.ds(h, 1), :].bitcast(F32), ALU.subtract))
                c.leave(HG)

        @block.tensor
        def _(pe):
            def project(h, r, base, cols):
                pe.wait_ge(wl_done, 4 * h + r + 1)
                for n, (col, m) in enumerate(cols):
                    for j in range(DK):
                        last = mm3(pe, bank(base + n, 0, m), wh[r % 2][:, j, :], wl[r % 2][:, j, :],
                                   g.uTh[:, j, col:col + m], g.uTl[:, j, col:col + m], j == 0, j == DK - 1)
                    last.then_inc(mm_done, 1)

            def head(h, first):
                if not first:
                    pe.wait_ge(a_ok, TT * h)
                    pe.wait_ge(o_ok, TT * h)
                project(h, 0, FB, pieces)
                if not first:
                    pe.wait_ge(s_ok, (4 * TT - 1) * h)
                project(h, 1, VB, pieces)
                pe.wait_ge(sig_f, 3 * h + 3)
                project(h, 2, QB, pieces[:2])
                pe.wait_ge(vt_ok, 3 * h + 3)
                project(h, 3, GB, pieces[:2])
                if not first:
                    pe.wait_ge(rt_ok, 2 * h)
                for n in range(2):
                    for t in range(4):
                        tt = 4 * n + t
                        last = pe.transpose(bank(6 + n, t * P, P), vt[:, tt * P:(tt + 1) * P], g.ident[:, :])
                    last.then_inc(vtr, 1)
                pe.transpose(g.ps[0:META, 2 * 512:2 * 512 + P], vt[:, SEQ:NT], g.ident[:, :]).then_inc(vtr, 1)
                pe.wait_ge(kd_ok, h + 1)
                pe.wait_ge(v_ok, 3 * h + 3)
                pe.transpose(g.ps[0:META, 2 * 512:2 * 512 + P], kd[:, SEQ:NT], g.ident[:, :]).then_inc(ktr, 1)
                pe.wait_ge(kdn_ok, 9 * h + 1)
                pe.matmul(bank(5, 0, P), kdm[:, :], v[0:META, TT, :], start=True, stop=True).then_inc(s0_mm, 1)
                pe.wait_ge(g_ok, 2 * h + 2)
                pe.wait_ge(q_ok, 2 * h + 2)

                def ahead(t):
                    if t >= 2:
                        pe.wait_ge(kdn_ok, 9 * h + t)
                        pe.wait_ge(a_ok, TT * h + t - 1)
                        pe.wait_ge(s_ok, (4 * TT - 1) * h + 4 * (t - 1))
                    pe.transpose(bank(TB + t % 2, 0, P), kd[:, t * P:(t + 1) * P], g.ident[:, :]).then_inc(ktr, 1)
                    pe.matmul(bank(AB + t % 2, 0, P), ks[:, t * P:(t + 1) * P], qs[:, t * P:(t + 1) * P],
                              start=True, stop=True).then_inc(a_mm, 1)
                    pe.wait_ge(kdn_ok, 9 * h + t + 2)
                    pe.wait_ge(vb_ok, 4 * (TT * h + t + 1))
                    pe.matmul(bank(KVB + t % 2), kdn[:, t % 2, :], vb[t % 2][:, :], start=True, stop=True).then_inc(kv_mm, 1)

                ahead(0)
                pe.wait_ge(s0_ok, h + 1)
                for t in range(TT):
                    if t + 1 < TT:
                        ahead(t + 1)
                    pe.wait_ge(a_ok, TT * h + t + 1)
                    if t >= 2:
                        pe.wait_ge(o_ok, TT * h + t - 1)
                    pe.matmul(bank(OB[t % 2], 0, P), v[:, t, :], at[:, t % 2, :], start=True, stop=False)
                    for ci in range(4):
                        n = 4 * t + ci
                        if n:
                            pe.wait_ge(s_ok, (4 * TT - 1) * h + n)
                        last = pe.matmul(bank(OB[t % 2], ci * CH, CH), S[:, n % 8, :], qd[:, n * CH:(n + 1) * CH],
                                         start=False, stop=ci == 3)
                    last.then_inc(o_mm, 1)
                pe.wait_ge(sq_ok, h + 1)
                for n in range(2):
                    pe.matmul(bank(TB + n), g.ones[:, :], d1[:, n * 512:(n + 1) * 512],
                              start=True, stop=True).then_inc(ms_mm, 1)

            head(0, True)
            with pe.Fori(1, HG) as h:
                head(h, False)


def phase_latents(nc, g):
    with ExitStack() as ph:
        sb = lambda n, s, d=F32: ph.enter_context(nc.sbuf_tensor(n, s, d))
        sem = semaphores(nc, ph)
        w = [sb(f"l_w{b}", [P, DK, P]) for b in range(2)]
        wh = [sb(f"l_wh{b}", [P, DK, P], F32R) for b in range(2)]
        wl = [sb(f"l_wl{b}", [P, DK, P], F32R) for b in range(2)]
        raw = sb("l_raw", [P, 5, NT])
        sq, rt = sb("l_sq", [P, NT]), sb("l_rt", [P, NT])
        gain = sb("l_gain", [P, 5])
        cst_in, zero = sem("l_cst_in"), sem("l_zero")
        w_in = [sem(f"l_w_in{b}") for b in range(2)]
        wh_done, wl_done, mm_done, raw_ok, kpe_ok = (sem("l_wh_done"), sem("l_wl_done"), sem("l_mm_done"),
                                                     sem("l_raw_ok"), sem("l_kpe_ok"))
        sq_ok, ms_mm, rt_ok, n_ok, hi_ok, lo_ok, dv = (sem("l_sq_ok"), sem("l_ms_mm"), sem("l_rt_ok"), sem("l_n_ok"),
                                                       sem("l_hi_ok"), sem("l_lo_ok"), sem("l_dv"))
        block = ph.enter_context(nc.Block())
        w_src = g.w_in[0].rearrange("(p j) n -> p j n", j=DK)
        bank = lambda i, a=0, n=512: g.ps[:, i * 512 + a:i * 512 + a + n]
        real, full = [(0, 512), (512, 512)], [(0, 512), (512, 512), (SEQ, META)]
        BLOCKS = [(C_CQ + i * P, P, real) for i in range(3)] + [(C_CKV + i * P, P, full) for i in range(2)] \
            + [(C_KPE - NOPE, QH, full)]
        NORMS = [(range(0, 3), SEQ, QL, g.cqh, g.cql, real), (range(3, 5), NT, KVL, g.ckh, g.ckl, full)]
        mm_before = [sum(len(b[2]) for b in BLOCKS[:n]) for n in range(7)]
        fbank = lambda n: 3 * (n % 2)

        @block.sync
        def _(sp):
            with nc.allow_non_contiguous_dma(reason="small vectors turned once"):
                sp.dma_start(gain[:, 0:3], g.q_norm[0].rearrange("(j p) -> p j", p=P)).then_inc(cst_in, 16)
                sp.dma_start(gain[:, 3:5], g.kv_norm[0].rearrange("(j p) -> p j", p=P)).then_inc(cst_in, 16)
            sp.dma_start(g.cos[NOPE:QH, :], g.rope_cos).then_inc(cst_in, 16)
            sp.dma_start(g.sin[NOPE:QH, :], g.rope_sin).then_inc(cst_in, 16)
            for n, (col, m, _) in enumerate(BLOCKS):
                if n >= 2:
                    sp.wait_ge(wl_done, n - 1)
                sp.dma_start(w[n % 2][:, :, 0:m], w_src[:, :, col:col + m]).then_inc(w_in[n % 2], 16)
            sp.wait_ge(cst_in, 64)

        @block.scalar
        def _(act):
            def split(n):
                if n >= 2:
                    act.wait_ge(mm_done, mm_before[n - 1])
                m = BLOCKS[n][1]
                act.wait_ge(w_in[n % 2], 16 * (n // 2) + 16)
                act.activation(wh[n % 2][:, :, 0:m], w[n % 2][:, :, 0:m], ACT.Copy).then_inc(wh_done, 1)

            split(0)
            split(1)
            for n in range(5):
                for p, (c, m) in enumerate(BLOCKS[n][2]):
                    act.wait_ge(mm_done, mm_before[n] + p + 1)
                    act.activation(raw[:, n, c:c + m], bank(fbank(n) + p, 0, m), ACT.Copy).then_inc(raw_ok, 1)
                if n + 2 < 6:
                    split(n + 2)
            done = 0
            for z, (js, width, size, _, _, cols) in enumerate(NORMS):
                for p, (c, m) in enumerate(cols):
                    act.wait_ge(ms_mm, done + p + 1)
                    act.activation(rt[:, c:c + m], bank([6, 7, 2][p], 0, m), ACT.Sqrt, scale=1.0 / size,
                                   bias=g.eps[:, :]).then_inc(rt_ok, 1)
                done += len(cols)
                for j in js:
                    act.wait_ge(n_ok, j + 1)
                    hi = NORMS[z][3]
                    act.activation(hi[:, j - js[0], 0:width], raw[:, j, 0:width], ACT.Copy).then_inc(hi_ok, 1)

        @block.vector
        def _(dve):
            v = Steps(dve, dv)

            def low(n):
                dve.wait_ge(wh_done, n + 1)
                m = BLOCKS[n][1]
                dve.tensor_tensor(wl[n % 2][:, :, 0:m], w[n % 2][:, :, 0:m], wh[n % 2][:, :, 0:m].bitcast(F32),
                                  ALU.subtract).then_inc(wl_done, 1)

            def squares(js, width, z):
                for j in js:
                    dve.wait_ge(raw_ok, mm_before[j + 1])
                    x = raw[:, j, 0:width]
                    if j == js[0]:
                        v.link(dve.tensor_tensor(sq[:, 0:width], x, x, ALU.mult))
                    else:
                        v.link(dve.tensor_tensor(rt[:, 0:width], x, x, ALU.mult))
                        ins = dve.tensor_tensor(sq[:, 0:width], sq[:, 0:width], rt[:, 0:width], ALU.add)
                        if j == js[-1]:
                            ins.then_inc(sq_ok, 1)
                        else:
                            v.link(ins)
                    if j + 2 < 6:
                        low(j + 2)

            def normed(z):
                js, width, _, hi, lo, cols = NORMS[z]
                dve.wait_ge(rt_ok, 2 if z == 0 else 5)
                v.link(dve.reciprocal(rt[:, 0:width], rt[:, 0:width]))
                for j in js:
                    dve.scalar_tensor_tensor(out=raw[:, j, 0:width], in0=raw[:, j, 0:width], scalar=gain[:, j:j + 1],
                                             in1=rt[:, 0:width], op0=ALU.mult, op1=ALU.mult).then_inc(n_ok, 1)
                for j in js:
                    dve.wait_ge(hi_ok, j + 1)
                    dve.tensor_tensor(lo[:, j - js[0], 0:width], raw[:, j, 0:width],
                                      hi[:, j - js[0], 0:width].bitcast(F32), ALU.subtract).then_inc(lo_ok, 1)

            low(0)
            low(1)
            dve.wait_ge(cst_in, 64)
            squares(range(0, 3), SEQ, 0)
            normed(0)
            squares(range(3, 5), NT, 1)
            normed(1)
            rows = slice(NOPE, QH)
            for p, (c, m) in enumerate(full):
                dve.wait_ge(mm_done, mm_before[5] + p + 1)
                b = g.ps[rows, (3 + p) * 512:(3 + p) * 512 + m]
                v.link(dve.stream_shuffle(out=sq[rows, c:c + m], in_=b, mask=SWAP))
                dve.tensor_tensor(g.KT[0][rows, c:c + m], b, g.cos[rows, c:c + m], ALU.mult).then_inc(kpe_ok, 1)
            dve.wait_ge(kpe_ok, 3)
            v.link(dve.tensor_tensor(sq[rows, :], sq[rows, :], g.sin[rows, :], ALU.mult))
            v.link(dve.tensor_tensor(g.KT[0][rows, :], g.KT[0][rows, :], sq[rows, :], ALU.add))

        @block.tensor
        def _(pe):
            def project(n):
                pe.wait_ge(wl_done, n + 1)
                if n >= 2:
                    pe.wait_ge(raw_ok, mm_before[n - 1])
                m = BLOCKS[n][1]
                for p, (col, k) in enumerate(BLOCKS[n][2]):
                    for j in range(DK):
                        last = mm3(pe, g.ps[0:m, (fbank(n) + p) * 512:(fbank(n) + p) * 512 + k], wh[n % 2][:, j, 0:m],
                                   wl[n % 2][:, j, 0:m], g.uTh[:, j, col:col + k], g.uTl[:, j, col:col + k],
                                   j == 0, j == DK - 1)
                    last.then_inc(mm_done, 1)

            def sums(z, cols):
                pe.wait_ge(sq_ok, z + 1)
                for p, (c, m) in enumerate(cols):
                    pe.matmul(bank([6, 7, 2][p], 0, m), g.ones[:, :], sq[:, c:c + m], start=True, stop=True).then_inc(ms_mm, 1)

            for n in range(4):
                project(n)
            sums(0, real)
            project(4)
            pe.wait_ge(raw_ok, mm_before[4])
            project(5)
            pe.wait_ge(rt_ok, 2)
            pe.wait_ge(raw_ok, mm_before[5])
            sums(1, full)


def phase_attention(nc, g):
    with ExitStack() as ph:
        sb = lambda n, s, d=F32: ph.enter_context(nc.sbuf_tensor(n, s, d))
        sem = semaphores(nc, ph)
        wq_all, wkv_all = sb("t_wq_all", [P, 3, HEADS * QH]), sb("t_wkv_all", [P, 2, D])
        wqh = [sb(f"t_wqh{b}", [P, 3, QH], F32R) for b in range(2)]
        wql = [sb(f"t_wql{b}", [P, 3, QH], F32R) for b in range(2)]
        wkh = [sb(f"t_wkh{b}", [P, 2, P], F32R) for b in range(2)]
        wkl = [sb(f"t_wkl{b}", [P, 2, P], F32R) for b in range(2)]
        QT = [sb(f"t_QT{b}", [QH, SEQ]) for b in range(2)]
        KT = [g.KT[0], sb("t_KT1", [QH, NT])]
        KVT = sb("t_KVT", [P, NT])
        V = [sb(f"t_V{b}", [P, TT + 1, VD]) for b in range(2)]
        pr = [sb(f"t_p{b}", [P, NT]) for b in range(2)]
        PT = [sb(f"t_PT{b}", [P, TT + 1, P]) for b in range(2)]
        rot = sb("t_rot", [QH, SEQ])
        mask = sb("t_mask", [P, P])
        oall = sb("t_oall", [P, TT, HEADS * VD])
        st = sb("t_stat", [P, 8])
        w_in, cst, kt_pe = sem("t_w_in"), sem("t_cst"), sem("t_kt_pe")
        wh_ok, wl_ok, q_mm, kv_mm = sem("t_wh_ok"), sem("t_wl_ok"), sem("t_q_mm"), sem("t_kv_mm")
        qn_ok, qp_ok, kvt_ok, kt_ok = sem("t_qn_ok"), sem("t_qp_ok"), sem("t_kvt_ok"), sem("t_kt_ok")
        v_tr, v_ok = sem("t_v_tr"), sem("t_v_ok")
        s_mm, mx_ok, exp_ok, p_tr, pa_ok, pd_ok, o_mm, o_ok, dv = (
            sem("t_s_mm"), sem("t_mx_ok"), sem("t_exp_ok"), sem("t_p_tr"), sem("t_pa_ok"), sem("t_pd_ok"),
            sem("t_o_mm"), sem("t_o_ok"), sem("t_dv"))
        ot_tr, oh_ok, ol_ok = sem("t_ot_tr"), sem("t_oh_ok"), sem("t_ol_ok")
        block = ph.enter_context(nc.Block())
        bank = lambda i, a=0, n=512: g.ps[:, i * 512 + a:i * 512 + a + n]
        pieces = [(0, 512), (512, 512), (SEQ, META)]
        tiles = lambda i: list(range(i + 1)) + [TT]
        groups = lambda i: [tiles(i)[a:a + 4] for a in range(0, i + 2, 4)]
        before = [sum(len(groups(m)) for m in range(i)) for i in range(TT + 1)]
        NG = before[TT]
        assert NG % 2 == 0
        HALF = NG // 2
        sbank = lambda i: 3 * (i % 2)

        def taken(i, grp, b):
            real = [t for t in grp if t != TT]
            out = []
            if real:
                out.append((PT[i % 2][:, real[0]:real[0] + len(real), :],
                            g.ps[:, b * 512:b * 512 + len(real) * P].rearrange("p (t c) -> p t c", c=P)))
            if TT in grp:
                at = b * 512 + len(real) * P
                out.append((PT[i % 2][0:META, TT, :], g.ps[0:META, at:at + P]))
            return out

        @block.sync
        def _(sp):
            sp.dma_start(wq_all[:, :, :], g.w_uq[0].rearrange("(j p) n -> p j n", p=P)).then_inc(w_in, 16)
            sp.dma_start(wkv_all[:, :, :], g.w_ukv[0].rearrange("(j p) n -> p j n", p=P)).then_inc(w_in, 16)

        @block.gpsimd
        def _(pool):
            pool.memset(mask[:, :], 0.0).then_inc(cst, 1)
            pool.wait_ge(cst, 1)
            pool.affine_select(out=mask[:, :], in_=mask[:, :], compare_op=ALU.is_ge, fill=-1e30, base=0,
                               pattern=[[-1, P]], channel_multiplier=1).then_inc(cst, 1)
            pool.wait_ge(cst, 2)
            pool.tensor_copy(KT[1][NOPE:QH, :], KT[0][NOPE:QH, :]).then_inc(kt_pe, 1)
            pool.wait_ge(kt_pe, 1)

            def keys(h, b, used):
                pool.wait_ge(kvt_ok, 3 * h + 3)
                if used:
                    pool.wait_ge(s_mm, TT * (h - 1))
                settle(pool, g)
                pool.tensor_copy(KT[b][0:NOPE, :], KVT[0:NOPE, :]).then_inc(kt_ok, 1)

            keys(0, 0, False)
            keys(1, 1, False)
            with pool.Fori(1, HEADS // 2) as i:
                for b in range(2):
                    keys(2 * i + b, b, True)

        @block.scalar
        def _(act):
            def split(h, b):
                settle(act, g)
                act.activation(wqh[b][:, :, :], wq_all[:, :, bass.ds(h * QH, QH)], ACT.Copy).then_inc(wh_ok, 1)
                act.activation(wkh[b][:, :, :], wkv_all[:, :, bass.ds(h * P, P)], ACT.Copy).then_inc(wh_ok, 1)

            def evac(h, b, first):
                for n in range(2):
                    act.wait_ge(q_mm, 2 * h + n + 1)
                    act.activation(QT[b][0:NOPE, n * 512:(n + 1) * 512], g.ps[0:NOPE, n * 512:(n + 1) * 512],
                                   ACT.Copy).then_inc(qn_ok, 1)
                for n, (c, m) in enumerate(pieces):
                    act.wait_ge(kv_mm, 3 * h + n + 1)
                    if n == 0 and not first:
                        act.wait_ge(kt_ok, h)
                        act.wait_ge(v_tr, 3 * h)
                    act.activation(KVT[:, c:c + m], bank(3 + n, 0, m), ACT.Copy).then_inc(kvt_ok, 1)

            def values(h, b):
                for n in range(2):
                    act.wait_ge(v_tr, 3 * h + n + 1)
                    act.activation(V[b][:, 4 * n:4 * n + 4, :], bank(6 + n).rearrange("p (t c) -> p t c", t=4)[:, :, NOPE:P],
                                   ACT.Copy).then_inc(v_ok, 1)
                act.wait_ge(v_tr, 3 * h + 3)
                act.activation(V[b][0:META, TT, :], g.ps[0:META, 6 * 512 + NOPE:6 * 512 + P], ACT.Copy).then_inc(v_ok, 1)

            def expo(h, i):
                act.wait_ge(mx_ok, TT * h + i + 1)
                s, n = i % 2, META + P * (i + 1)
                act.activation(pr[s][:, 0:n], g.ps[:, sbank(i) * 512:sbank(i) * 512 + n], ACT.Exp, scale=SCALE,
                               bias=st[:, 2 + s:3 + s], accum_out=st[:, 4 + s:5 + s]).then_inc(exp_ok, 1)

            def attend(h, b, nxt, ahead):
                if nxt:
                    evac(h + 1, 1 - b, False)
                expo(h, 0)
                for i in range(TT):
                    if i + 1 < TT:
                        expo(h, i + 1)
                    for gi, grp in enumerate(groups(i)):
                        n = before[i] + gi
                        if n % 2 == 0:
                            act.wait_ge(p_tr, NG * h + n + 1)
                            for dst, src in taken(i, grp, 6):
                                ins = act.activation(dst, src, ACT.Copy)
                            ins.then_inc(pa_ok, 1)
                    if i == 2 and nxt:
                        values(h + 1, 1 - b)
                    if i == 3 and ahead:
                        split(h + 2, b)

            act.wait_ge(w_in, 32)
            split(0, 0)
            split(1, 1)
            evac(0, 0, True)
            values(0, 0)
            with act.Fori(0, HEADS // 2 - 1) as i:
                for b in range(2):
                    attend(2 * i + b, b, True, True)
            attend(HEADS - 2, 0, True, False)
            attend(HEADS - 1, 1, False, False)
            for t in range(TT):
                act.wait_ge(ot_tr, t + 1)
                act.activation(g.omTh[:, :, t * P:(t + 1) * P], bank(t % 4).rearrange("p (c t) -> p c t", c=4),
                               ACT.Copy).then_inc(oh_ok, 1)

        @block.vector
        def _(dve):
            c = Steps(dve, dv)

            def low(n, b):
                for x, (raw, hi, lo) in enumerate([(wq_all, wqh, wql), (wkv_all, wkh, wkl)]):
                    m = [QH, P][x]
                    dve.wait_ge(wh_ok, 2 * n + x + 1)
                    dve.tensor_tensor(lo[b][:, :, :], raw[:, :, bass.ds(n * m, m)], hi[b][:, :, :].bitcast(F32),
                                      ALU.subtract).then_inc(wl_ok, 1)

            def rotate(h, b):
                rows = slice(NOPE, QH)
                for n in range(2):
                    dve.wait_ge(q_mm, 2 * h + n + 1)
                    src = g.ps[rows, n * 512:(n + 1) * 512]
                    cols = slice(n * 512, (n + 1) * 512)
                    settle(dve, g)
                    c.mark(dve.stream_shuffle(out=rot[rows, cols], in_=src, mask=SWAP))
                    c.link(dve.tensor_tensor(QT[b][rows, cols], src, g.cos[rows, cols], ALU.mult))
                c.link(dve.tensor_tensor(rot[rows, :], rot[rows, :], g.sin[rows, 0:SEQ], ALU.mult))
                dve.tensor_tensor(QT[b][rows, :], QT[b][rows, :], rot[rows, :], ALU.add).then_inc(qp_ok, 1)

            def stats(h, i):
                s, n = i % 2, META + P * (i + 1)
                dve.wait_ge(s_mm, TT * h + i + 1)
                diag = g.ps[:, sbank(i) * 512 + P * i:sbank(i) * 512 + P * (i + 1)]
                c.link(dve.tensor_tensor(diag, diag, mask[:, :], ALU.add))
                c.link(dve.tensor_reduce(out=st[:, s:s + 1], in_=g.ps[:, sbank(i) * 512:sbank(i) * 512 + n], axis=AX.X,
                                         op=ALU.max, negate=True))
                dve.tensor_scalar(st[:, 2 + s:3 + s], st[:, s:s + 1], SCALE, None, ALU.mult).then_inc(mx_ok, 1)

            def attend(h, b, nxt, ahead):
                if nxt:
                    rotate(h + 1, 1 - b)
                stats(h, 0)
                for i in range(TT):
                    if i + 1 < TT:
                        stats(h, i + 1)
                    for gi, grp in enumerate(groups(i)):
                        n = before[i] + gi
                        if n % 2 == 1:
                            dve.wait_ge(p_tr, NG * h + n + 1)
                            for dst, src in taken(i, grp, 7):
                                ins = dve.tensor_copy(dst, src)
                            ins.then_inc(pd_ok, 1)
                    s = i % 2
                    dve.wait_ge(exp_ok, TT * h + i + 1)
                    c.link(dve.reciprocal(st[:, 6 + s:7 + s], st[:, 4 + s:5 + s]))
                    dve.wait_ge(o_mm, TT * h + i + 1)
                    dve.tensor_scalar(oall[:, i, bass.ds(h * VD, VD)], bank(sbank(i) + 2, 512 - VD, VD),
                                      st[:, 6 + s:7 + s], None, ALU.mult).then_inc(o_ok, 1)
                    if i == 3 and ahead:
                        low(h + 2, b)

            dve.wait_ge(w_in, 32)
            low(0, 0)
            low(1, 1)
            rotate(0, 0)
            dve.wait_ge(cst, 2)
            with dve.Fori(0, HEADS // 2 - 1) as i:
                c.enter(i, 2 * (5 + 3 * TT))
                for b in range(2):
                    attend(2 * i + b, b, True, True)
                c.leave(HEADS // 2 - 1)
            attend(HEADS - 2, 0, True, False)
            attend(HEADS - 1, 1, False, False)
            for t in range(TT):
                dve.wait_ge(oh_ok, t + 1)
                dve.tensor_tensor(g.omTl[:, :, t * P:(t + 1) * P], bank(t % 4).rearrange("p (c t) -> p c t", c=4),
                                  g.omTh[:, :, t * P:(t + 1) * P].bitcast(F32), ALU.subtract).then_inc(ol_ok, 1)

        @block.tensor
        def _(pe):
            def project(h, b):
                pe.wait_ge(wl_ok, 2 * h + 2)
                for n in range(2):
                    for j in range(3):
                        last = mm3(pe, g.ps[0:QH, n * 512:(n + 1) * 512], wqh[b][:, j, :], wql[b][:, j, :],
                                   g.cqh[:, j, n * 512:(n + 1) * 512], g.cql[:, j, n * 512:(n + 1) * 512], j == 0, j == 2)
                    last.then_inc(q_mm, 1)
                for n, (col, m) in enumerate(pieces):
                    for j in range(2):
                        last = mm3(pe, bank(3 + n, 0, m), wkh[b][:, j, :], wkl[b][:, j, :],
                                   g.ckh[:, j, col:col + m], g.ckl[:, j, col:col + m], j == 0, j == 1)
                    last.then_inc(kv_mm, 1)

            def values(h, b):
                pe.wait_ge(kvt_ok, 3 * h + 3)
                for n in range(2):
                    for t in range(4):
                        last = pe.transpose(bank(6 + n, t * P, P), KVT[:, (4 * n + t) * P:(4 * n + t + 1) * P], g.ident[:, :])
                    last.then_inc(v_tr, 1)
                pe.wait_ge(v_ok, 3 * h + 1)
                pe.transpose(g.ps[0:META, 6 * 512:6 * 512 + P], KVT[:, SEQ:NT], g.ident[:, :]).then_inc(v_tr, 1)

            def scores(h, b, i):
                if i >= 2:
                    pe.wait_ge(exp_ok, TT * h + i - 1)
                if i == TT - 1:
                    pe.wait_ge(o_ok, TT * h + i - 1)
                base = sbank(i) * 512
                q = QT[b][:, i * P:(i + 1) * P]
                n = P * (i + 1)
                for c in range(0, n, 512):
                    m = min(512, n - c)
                    pe.matmul(g.ps[:, base + c:base + c + m], q, KT[b][:, c:c + m], start=True, stop=True)
                pe.matmul(g.ps[:, base + n:base + n + META], q, KT[b][:, SEQ:NT], start=True, stop=True).then_inc(s_mm, 1)

            def taken_by(n, h):
                pe.wait_ge(pa_ok if n % 2 == 0 else pd_ok, HALF * h + n // 2 + 1)

            def attend(h, b, nxt, first, last_head):
                if nxt:
                    pe.wait_ge(qn_ok, 2 * h + 2)
                    pe.wait_ge(qp_ok, h + 1)
                    pe.wait_ge(kvt_ok, 3 * h + 3)
                if not first:
                    pe.wait_ge(exp_ok, TT * h)
                    pe.wait_ge(o_ok, TT * h)
                if nxt:
                    project(h + 1, 1 - b)
                    pe.wait_ge(qn_ok, 2 * h + 4)
                    pe.wait_ge(qp_ok, h + 2)
                else:
                    pe.wait_ge(qn_ok, 2 * h + 2)
                    pe.wait_ge(qp_ok, h + 1)
                pe.wait_ge(kt_ok, h + 1)
                scores(h, b, 0)
                if nxt:
                    pe.wait_ge(kvt_ok, 3 * h + 6)
                pe.wait_ge(v_ok, 3 * h + 3)
                for i in range(TT):
                    if i + 1 < TT:
                        scores(h, b, i + 1)
                    pe.wait_ge(exp_ok, TT * h + i + 1)
                    s, gs = i % 2, groups(i)
                    if i == 3 and nxt:
                        pe.wait_ge(v_ok, 3 * h + 6)
                    done = 0

                    def weighted(gi):
                        n = before[i] + gi
                        taken_by(n, h)
                        for t in gs[gi]:
                            k = META if t == TT else P
                            ins = pe.matmul(bank(sbank(i) + 2, 512 - VD, VD), PT[s][0:k, t, :], V[b][0:k, t, :],
                                            start=t == 0, stop=t == TT)
                        return ins

                    for gi, grp in enumerate(gs):
                        n = before[i] + gi
                        if n >= 2:
                            taken_by(n - 2, h)
                        elif not first:
                            pe.wait_ge(pa_ok if n % 2 == 0 else pd_ok, HALF * h)
                        for x, t in enumerate(grp):
                            if t == TT:
                                last = pe.transpose(g.ps[0:META, (6 + n % 2) * 512 + x * P:(6 + n % 2) * 512 + (x + 1) * P],
                                                    pr[s][:, P * (i + 1):P * (i + 1) + META], g.ident[:, :])
                            else:
                                last = pe.transpose(bank(6 + n % 2, x * P, P), pr[s][:, t * P:(t + 1) * P], g.ident[:, :])
                        last.then_inc(p_tr, 1)
                        if gi == 1 and i >= 2:
                            pe.wait_ge(o_ok, TT * h + i - 1)
                        if gi >= 1:
                            weighted(gi - 1)
                    if len(gs) == 1 and i >= 2:
                        pe.wait_ge(o_ok, TT * h + i - 1)
                    weighted(len(gs) - 1).then_inc(o_mm, 1)
                    if i == 2 and nxt:
                        values(h + 1, 1 - b)

            project(0, 0)
            values(0, 0)
            pe.wait_ge(cst, 2)
            pe.wait_ge(kt_pe, 1)
            pe.wait_ge(v_ok, 3)
            attend(0, 0, True, True, False)
            attend(1, 1, True, False, False)
            with pe.Fori(1, HEADS // 2 - 1) as i:
                for b in range(2):
                    attend(2 * i + b, b, True, False, False)
            attend(HEADS - 2, 0, True, False, False)
            attend(HEADS - 1, 1, False, False, True)
            pe.wait_ge(exp_ok, TT * HEADS)
            pe.wait_ge(o_ok, TT * HEADS)
            for t in range(TT):
                if t >= 4:
                    pe.wait_ge(ol_ok, t - 3)
                for x in range(4):
                    last = pe.transpose(bank(t % 4, x * P, P), oall[:, t, x * P:(x + 1) * P], g.ident[:, :])
                last.then_inc(ot_tr, 1)


def expert_loaders(g):
    up = [a[0].rearrange("e (p j) f -> p e j f", j=DK) for a in (g.w1, g.w3)]
    down = g.w2[0].rearrange("e (p j) n -> p e j n", j=2)

    def load_up(eng, e, b):
        for r in range(2):
            eng.dma_start(g.r13[b][:, r, :, :], up[r][:, bass.ds(e, 1), :, :].rearrange("p a j f -> p (a j) f")
                          ).then_inc(g.w_up_in[b], 16)

    def load_down(eng, e, b):
        eng.dma_start(g.r2[b][:, :, :], down[:, bass.ds(e, 1), :, :].rearrange("p a j n -> p (a j) n")
                      ).then_inc(g.w_down_in[b], 16)

    return load_up, load_down


def phase_merge(nc, g):
    with ExitStack() as ph:
        sb = lambda n, s, d=F32: ph.enter_context(nc.sbuf_tensor(n, s, d))
        sem = semaphores(nc, ph)
        w = [sb(f"e_w{b}", [P, 2, 4, P]) for b in range(2)]
        wh = [sb(f"e_wh{b}", [P, 2, 4, P], F32R) for b in range(2)]
        wl = [sb(f"e_wl{b}", [P, 2, 4, P], F32R) for b in range(2)]
        gate = [sb(f"e_gate{b}", [P, 2, SEQ]) for b in range(2)]
        m = [sb(f"e_m{b}", [P, SEQ]) for b in range(2)]
        w_in = [sem(f"e_w_in{b}") for b in range(2)]
        gate_in = [sem(f"e_gate_in{b}") for b in range(2)]
        stored = [sem(f"e_stored{b}") for b in range(2)]
        wh_ok, wl_ok, mm_ok, m_ok, dv = sem("e_wh_ok"), sem("e_wl_ok"), sem("e_mm_ok"), sem("e_m_ok"), sem("e_dv")
        block = ph.enter_context(nc.Block())
        bank = lambda i: g.ps[:, i * 512:(i + 1) * 512]
        br = [a[0].rearrange("(j p) n -> p j n", p=P) for a in (g.w_br_mla, g.w_br_hgrn)]

        @block.sync
        def _(sp):
            def load(n, b):
                for r in range(2):
                    sp.dma_start(w[b][:, r, :, :], br[r][:, :, bass.ds(n * P, P)]).then_inc(w_in[b], 16)
                    sp.dma_start(gate[b][:, r, :], g.gates[bass.ds(n * P + r * D, P), :]).then_inc(gate_in[b], 16)

            def store(n, b):
                sp.wait_ge(m_ok, n + 1)
                sp.dma_start(g.merged[bass.ds(n * P, P), :], m[b][:, :]).then_inc(stored[b], 16)

            load(0, 0)
            load(1, 1)
            with sp.Fori(0, DK // 2 - 1) as i:
                for b in range(2):
                    store(2 * i + b, b)
                    load(2 * i + b + 2, b)
            for b in range(2):
                store(DK - 2 + b, b)
                sp.wait_ge(stored[b], 16 * (DK // 2))

        @block.scalar
        def _(act):
            for b in range(2):
                act.wait_ge(w_in[b], 32)
                act.activation(wh[b][:, :, :, :], w[b][:, :, :, :], ACT.Copy).then_inc(wh_ok, 1)
            with act.Fori(1, DK // 2) as i:
                for b in range(2):
                    act.wait_ge(mm_ok, 4 * (2 * i + b - 1))
                    act.wait_ge(w_in[b], 32 * i + 32)
                    act.activation(wh[b][:, :, :, :], w[b][:, :, :, :], ACT.Copy).then_inc(wh_ok, 1)

        @block.vector
        def _(dve):
            c = Steps(dve, dv)

            def low(n, b):
                dve.wait_ge(wh_ok, n + 1)
                dve.tensor_tensor(wl[b][:, :, :, :], w[b][:, :, :, :], wh[b][:, :, :, :].bitcast(F32),
                                  ALU.subtract).then_inc(wl_ok, 1)

            def merge(n, b, turn, first):
                dve.wait_ge(gate_in[b], 32 * turn + 32)
                if not first:
                    dve.wait_ge(stored[b], 16 * turn)
                for r in range(2):
                    for q in range(2):
                        dve.wait_ge(mm_ok, 4 * n + 2 * r + q + 1)
                        cols = slice(q * 512, (q + 1) * 512)
                        c.mark(dve.tensor_tensor((m[b] if r == 0 else gate[b][:, 1, :])[:, cols], gate[b][:, r, cols],
                                                 bank(4 * b + 2 * r + q), ALU.mult))
                dve.wait_ge(dv, c.now())
                dve.tensor_tensor(m[b][:, :], m[b][:, :], gate[b][:, 1, :], ALU.add).then_inc(m_ok, 1)

            low(0, 0)
            low(1, 1)
            for b in range(2):
                merge(b, b, 0, True)
            with dve.Fori(1, DK // 2) as i:
                c.outer, c.per, c.base, c.k = 0, 8, i * 8, 0
                for b in range(2):
                    low(2 * i + b, b)
                for b in range(2):
                    merge(2 * i + b, b, i, False)

        @block.tensor
        def _(pe):
            def products(n, b):
                pe.wait_ge(wl_ok, n + 1)
                for r, (oh, ol) in enumerate([(g.omTh, g.omTl), (g.ohTh, g.ohTl)]):
                    for q in range(2):
                        cols = slice(q * 512, (q + 1) * 512)
                        for j in range(4):
                            last = mm3(pe, bank(4 * b + 2 * r + q), wh[b][:, r, j, :], wl[b][:, r, j, :],
                                       oh[:, j, cols], ol[:, j, cols], j == 0, j == 3)
                        last.then_inc(mm_ok, 1)

            for b in range(2):
                products(b, b)
            with pe.Fori(1, DK // 2) as i:
                for b in range(2):
                    pe.wait_ge(m_ok, 2 * i + b - 1)
                    products(2 * i + b, b)


def phase_output(nc, g):
    with ExitStack() as ph:
        sb = lambda n, s, d=F32: ph.enter_context(nc.sbuf_tensor(n, s, d))
        sem = semaphores(nc, ph)
        w = [sb(f"f_w{b}", [P, 2, D]) for b in range(2)]
        woh, wol = sb("f_woh", [P, DK, D], F32R), sb("f_wol", [P, DK, D], F32R)
        m = [sb(f"f_m{b}", [P, DK, P]) for b in range(2)]
        mh = [sb(f"f_mh{b}", [P, DK, P], F32R) for b in range(2)]
        ml = [sb(f"f_ml{b}", [P, DK, P], F32R) for b in range(2)]
        x = [sb(f"f_x{b}", [P, D]) for b in range(2)]
        u = [sb(f"f_u{b}", [P, D]) for b in range(2)]
        junk, gain, uT = sb("f_junk", [P, D]), sb("f_gain", [P, D]), sb("f_uT", [P, DK, P])
        R = GROUPS + EXPERTS
        wr, br = sb("f_wr", [P, DK, R]), sb("f_br", [P, R])
        st = sb("f_stat", [P, 4])
        lg, top, idx, ex8, oh8, sel, es = (sb("f_lg", [P, R]), sb("f_top", [P, 2, 8]), sb("f_idx", [P, 2, 8], U32),
                                           sb("f_ex8", [P, 8]), sb("f_oh8", [P, 8]), sb("f_sel", [P, 8, 8]), sb("f_es", [P, 8]))
        sc = sb("f_sc", [P, 16])
        M = [sb(f"f_M{b}", [P, 3, EXPERTS]) for b in range(2)]
        Mcum, R2, tmp = sb("f_Mcum", [P, EXPERTS]), sb("f_R2", [P, EXPERTS]), sb("f_tmp", [P, EXPERTS])
        slot = [sb(f"f_slot{b}", [P, 2], I32) for b in range(2)]
        slotf = sb("f_slotf", [P, 2])
        rec = [sb(f"f_rec{b}", [P, 2, ROWS]) for b in range(2)]
        io8, io64, off64, tok, upper = (sb("f_io8", [P, 8]), sb("f_io64", [P, EXPERTS]), sb("f_off64", [P, EXPERTS]),
                                        sb("f_tok", [P, 1]), sb("f_upper", [P, P]))
        fill = sb("f_fill", [P, EXPERTS * SLOTS * ROWS // P])
        rec_z = sem("f_rec_z")
        cst_in, cst, filled, wh_ok, wl_ok = sem("f_cst_in"), sem("f_cst"), sem("f_filled"), sem("f_wh_ok"), sem("f_wl_ok")
        w_in = [sem(f"f_w_in{b}") for b in range(2)]
        m_in = [sem(f"f_m_in{b}") for b in range(2)]
        x_in = [sem(f"f_x_in{b}") for b in range(2)]
        h_out = [sem(f"f_h_out{b}") for b in range(2)]
        u_out = [sem(f"f_u_out{b}") for b in range(2)]
        rec_out = sem("f_rec_out")
        mh_ok, ml_ok, w_mm, h_ok, ss_ok, rt_ok, u_ok = (sem("f_mh_ok"), sem("f_ml_ok"), sem("f_w_mm"), sem("f_h_ok"),
                                                        sem("f_ss_ok"), sem("f_rt_ok"), sem("f_u_ok"))
        u_tr, uT_ok, lg_mm, lg_ok, eg_ok, d_ok, ed_ok, M_ok, rk_mm, cum_ok, dv = (
            sem("f_u_tr"), sem("f_uT_ok"), sem("f_lg_mm"), sem("f_lg_ok"), sem("f_eg_ok"), sem("f_d_ok"), sem("f_ed_ok"),
            sem("f_M_ok"), sem("f_rk_mm"), sem("f_cum_ok"), sem("f_dv"))
        block = ph.enter_context(nc.Block())
        bank = lambda i, a=0, n=512: g.ps[:, i * 512 + a:i * 512 + a + n]
        w_src = g.w_out[0].rearrange("(j p) n -> p j n", p=P)
        m_src = g.merged.rearrange("(j p) t -> p j t", p=P)

        def tiles(body, eng):
            body(0, 0, True, False)
            with eng.Fori(0, TT // 2 - 1) as i:
                for b in (1, 0):
                    body(2 * i + 2 - b, b, False, False, i)
            body(TT - 1, 1, False, True)

        def turn(t, b, i):
            if isinstance(t, int):
                return t // 2
            return i if b else i + 1

        @block.sync
        def _(sp):
            sp.dma_start(gain[:, :], g.ffn_norm[0:1, :].to_broadcast([P, D])).then_inc(cst_in, 16)
            sp.dma_start(wr[:, :, 0:GROUPS], g.w_group[0].rearrange("(j p) n -> p j n", p=P)).then_inc(cst_in, 16)
            sp.dma_start(wr[:, :, GROUPS:R], g.w_route[0].rearrange("(j p) n -> p j n", p=P)).then_inc(cst_in, 16)
            sp.dma_start(br[:, 0:GROUPS], g.b_group[0:1, :].to_broadcast([P, GROUPS])).then_inc(cst_in, 16)
            sp.dma_start(br[:, GROUPS:R], g.b_route[0:1, :].to_broadcast([P, EXPERTS])).then_inc(cst_in, 16)
            for n in range(2):
                sp.dma_start(w[n][:, :, :], w_src[:, 2 * n:2 * n + 2, :]).then_inc(w_in[n], 16)
            for b in range(2):
                sp.dma_start(m[b][:, :, :], m_src[:, :, b * P:(b + 1) * P]).then_inc(m_in[b], 16)
                sp.dma_start(x[b][:, :], g.x[0, b * P:(b + 1) * P, :]).then_inc(x_in[b], 16)
            for n in range(2, 4):
                sp.wait_ge(wl_ok, n - 1)
                sp.dma_start(w[n % 2][:, :, :], w_src[:, 2 * n:2 * n + 2, :]).then_inc(w_in[n % 2], 16)
            sp.wait_ge(cst, 8)
            sp.dma_start(g.table.rearrange("(p s) r -> p (s r)", p=P), fill[:, :]).then_inc(filled, 16)
            for b in range(2):
                g.load_up(sp, b, b)
                g.load_down(sp, b, b)

            def body(t, b, first, last, i=None):
                n = turn(t, b, i)
                sp.wait_ge(h_ok, t + 1)
                sp.dma_start(g.h[bass.ds(t * P, P), :], x[b][:, :]).then_inc(h_out[b], 16)
                sp.wait_ge(u_ok, t + 1)
                sp.dma_start(g.u2[bass.ds(t * P, P), :], u[b][:, :]).then_inc(u_out[b], 16)

            def loads(t, b, i):
                sp.wait_ge(ml_ok, t - 1)
                sp.dma_start(m[b][:, :, :], m_src[:, :, bass.ds(t * P, P)]).then_inc(m_in[b], 16)
                sp.wait_ge(h_out[b], 16 * (i + 1))
                sp.dma_start(x[b][:, :], g.x[0, bass.ds(t * P, P), :]).then_inc(x_in[b], 16)

            with sp.Fori(0, TT // 2 - 1) as i:
                for b in range(2):
                    body(2 * i + b, b, False, False, i if b else i)
                    loads(2 * i + b + 2, b, i)
            for b in range(2):
                body(TT - 2 + b, b, False, True)
                sp.wait_ge(h_out[b], 16 * (TT // 2))
                sp.wait_ge(u_out[b], 16 * (TT // 2 + b))

        @block.gpsimd
        def _(pool):
            pool.sem_inc(u_out[1], 16)
            pool.iota(io8[:, :], pattern=[[1, 8]], base=0, channel_multiplier=0,
                      allow_small_or_imprecise_dtypes=True).then_inc(cst, 1)
            pool.iota(io64[:, :], pattern=[[1, EXPERTS]], base=0, channel_multiplier=0,
                      allow_small_or_imprecise_dtypes=True).then_inc(cst, 1)
            pool.iota(off64[:, :], pattern=[[SLOTS, EXPERTS]], base=0, channel_multiplier=0,
                      allow_small_or_imprecise_dtypes=True).then_inc(cst, 1)
            pool.iota(tok[:, :], pattern=[[0, 1]], base=0, channel_multiplier=1,
                      allow_small_or_imprecise_dtypes=True).then_inc(cst, 1)
            pool.memset(Mcum[:, :], 0.0).then_inc(cst, 1)
            pool.affine_select(out=upper[:, :], in_=g.ones[:, :], compare_op=ALU.is_gt, fill=0.0, base=0,
                               pattern=[[1, P]], channel_multiplier=-1).then_inc(cst, 1)
            for b in range(2):
                pool.memset(rec[b][:, :, :], 0.0).then_inc(rec_z, 1)
            pool.memset(fill[:, 0:SLOTS], SKIP).then_inc(cst, 1)
            pool.memset(fill[:, SLOTS:], SKIP).then_inc(cst, 1)

            pool.wait_ge(filled, 16)
            with pool.Fori(0, TT // 2) as i:
                for b in range(2):
                    pool.wait_ge(cum_ok, 2 * i + b + 1)
                    settle(pool, g)
                    for c in range(2):
                        pool.indirect_dma_start(out=g.table, out_offset=bass.IndirectOffsetOnAxis(ap=slot[b][:, c:c + 1], axis=0),
                                                in_=rec[b][:, c, :], in_offset=None).then_inc(rec_out, 16)
            pool.wait_ge(rec_out, 32 * TT)

        @block.scalar
        def _(act):
            def split(t, b, n):
                act.wait_ge(m_in[b], 16 * n + 16)
                act.activation(mh[b][:, :, :], m[b][:, :, :], ACT.Copy).then_inc(mh_ok, 1)

            def body(t, b, first, last, i=None):
                if not last:
                    nxt = turn(t + 1, 1 - b, i) if isinstance(t, int) else (i + 1)
                    if not first:
                        act.wait_ge(w_mm, t)
                    split(t + 1, 1 - b, nxt)
                act.wait_ge(h_ok, t + 1)
                act.activation(junk[:, :], x[b][:, :], ACT.Square, accum_out=st[:, b:b + 1]).then_inc(ss_ok, 1)
                act.wait_ge(ss_ok, t + 1)
                act.activation(st[:, 2 + b:3 + b], st[:, b:b + 1], ACT.Sqrt, scale=1.0 / D, bias=g.eps[:, :]).then_inc(rt_ok, 1)
                for q in range(2):
                    act.wait_ge(u_tr, 2 * t + q + 1)
                    act.activation(uT[:, 4 * q:4 * q + 4, :], bank(4 + q).rearrange("p (j t) -> p j t", j=4),
                                   ACT.Copy).then_inc(uT_ok, 1)
                act.wait_ge(lg_ok, t + 1)
                act.activation(ex8[:, :], lg[:, 0:8], ACT.Exp, bias=sc[:, 0:1], accum_out=sc[:, 1:2]).then_inc(eg_ok, 1)
                act.wait_ge(d_ok, t + 1)
                act.activation(sc[:, 7:8], sc[:, 6:7], ACT.Exp).then_inc(ed_ok, 1)

            for n in range(4):
                act.wait_ge(w_in[n % 2], 16 * (n // 2) + 16)
                act.activation(woh[:, 2 * n:2 * n + 2, :], w[n % 2][:, :, :], ACT.Copy).then_inc(wh_ok, 1)
            split(0, 0, 0)
            tiles(body, act)

        @block.vector
        def _(dve):
            c = Steps(dve, dv)

            def low(t, b):
                dve.wait_ge(mh_ok, t + 1)
                dve.tensor_tensor(ml[b][:, :, :], m[b][:, :, :], mh[b][:, :, :].bitcast(F32), ALU.subtract).then_inc(ml_ok, 1)

            def choose(t, b):
                dve.wait_ge(lg_mm, t + 1)
                c.link(dve.tensor_tensor(lg[:, :], bank(6, 0, R), br[:, :], ALU.add))
                settle(dve, g)
                c.link(dve.max(out=top[:, 0, :], in_=lg[:, 0:8]))
                dve.tensor_scalar(sc[:, 0:1], top[:, 0, 0:1], -1.0, None, ALU.mult).then_inc(lg_ok, 1)
                settle(dve, g)
                c.link(dve.max_index(out=idx[:, 0, :], in_max=top[:, 0, :], in_values=lg[:, 0:8]))
                c.link(dve.tensor_copy(sc[:, 2:3], idx[:, 0, 0:1]))
                c.link(dve.tensor_scalar(oh8[:, :], io8[:, :], sc[:, 2:3], None, ALU.is_equal))
                c.link(dve.tensor_tensor(sel[:, :, :], lg[:, 8:R].rearrange("p (g e) -> p g e", g=8),
                                         oh8[:, :].rearrange("p (g a) -> p g a", a=1).to_broadcast([P, 8, 8]), ALU.mult))
                c.link(dve.tensor_reduce(out=es[:, :], in_=sel[:, :, :].rearrange("p g e -> p e g"), axis=AX.X, op=ALU.add))
                settle(dve, g)
                c.link(dve.max(out=top[:, 1, :], in_=es[:, :]))
                dve.tensor_tensor(sc[:, 6:7], top[:, 1, 1:2], top[:, 1, 0:1], ALU.subtract).then_inc(d_ok, 1)
                settle(dve, g)
                c.link(dve.max_index(out=idx[:, 1, :], in_max=top[:, 1, :], in_values=es[:, :]))
                c.link(dve.tensor_copy(sc[:, 4:6], idx[:, 1, 0:2]))
                c.link(dve.tensor_scalar(sc[:, 3:4], sc[:, 2:3], 8.0, None, ALU.mult))
                c.link(dve.tensor_scalar(sc[:, 4:6], sc[:, 4:6], sc[:, 3:4], None, ALU.add))
                for k in range(2):
                    c.link(dve.tensor_scalar(M[b][:, k, :], io64[:, :], sc[:, 4 + k:5 + k], None, ALU.is_equal))
                dve.tensor_tensor(M[b][:, 2, :], M[b][:, 0, :], M[b][:, 1, :], ALU.add).then_inc(M_ok, 1)
                dve.wait_ge(eg_ok, t + 1)
                c.link(dve.reciprocal(sc[:, 8:9], sc[:, 1:2]))
                dve.wait_ge(ed_ok, t + 1)
                c.link(dve.tensor_scalar(sc[:, 9:10], sc[:, 7:8], 1.0, None, ALU.add))
                c.link(dve.reciprocal(sc[:, 9:10], sc[:, 9:10]))
                c.link(dve.tensor_tensor(sc[:, 10:11], sc[:, 8:9], sc[:, 9:10], ALU.mult))
                c.link(dve.tensor_tensor(sc[:, 11:12], sc[:, 10:11], sc[:, 7:8], ALU.mult))

            def place(t, b, n, first):
                dve.wait_ge(rk_mm, t + 1)
                c.link(dve.tensor_tensor(R2[:, :], bank(7, 0, EXPERTS), off64[:, :], ALU.add))
                for k in range(2):
                    c.link(dve.scalar_tensor_tensor(out=tmp[:, :], in0=M[b][:, k, :], scalar=1.0, in1=R2[:, :], op0=ALU.mult,
                                                    op1=ALU.mult, accum_out=slotf[:, k:k + 1]))
                if not first:
                    dve.wait_ge(rec_out, 32 * t)
                c.link(dve.tensor_copy(slot[b][:, :], slotf[:, :]))
                for k in range(2):
                    c.link(dve.tensor_scalar(rec[b][:, k, 0:1], tok[:, :], 2.0, float(k), ALU.mult, ALU.add))
                    c.link(dve.tensor_copy(rec[b][:, k, 1:2], sc[:, 10 + k:11 + k]))
                    c.link(dve.tensor_copy(rec[b][:, k, 2:3], tok[:, :]))
                c.link(dve.tensor_scalar(tok[:, :], tok[:, :], float(P), None, ALU.add))
                dve.tensor_tensor(Mcum[:, :], Mcum[:, :], M[b][:, 2, :], ALU.add).then_inc(cum_ok, 1)

            def body(t, b, first, last, i=None):
                if not last:
                    low(t + 1, 1 - b)
                n = turn(t, b, i)
                dve.wait_ge(x_in[b], 16 * n + 16)
                for q in range(2):
                    dve.wait_ge(w_mm, t + 1)
                    ins = dve.tensor_tensor(x[b][:, q * 512:(q + 1) * 512], x[b][:, q * 512:(q + 1) * 512],
                                            bank(2 * b + q), ALU.add)
                ins.then_inc(h_ok, 1)
                dve.wait_ge(rt_ok, t + 1)
                c.link(dve.reciprocal(st[:, 2 + b:3 + b], st[:, 2 + b:3 + b]))
                if not first:
                    dve.wait_ge(u_out[b], 16 * (n + b))
                dve.scalar_tensor_tensor(out=u[b][:, :], in0=x[b][:, :], scalar=st[:, 2 + b:3 + b], in1=gain[:, :],
                                         op0=ALU.mult, op1=ALU.mult).then_inc(u_ok, 1)
                choose(t, b)
                place(t, b, n, first)

            for n in range(4):
                dve.wait_ge(wh_ok, n + 1)
                dve.tensor_tensor(wol[:, 2 * n:2 * n + 2, :], w[n % 2][:, :, :], woh[:, 2 * n:2 * n + 2, :].bitcast(F32),
                                  ALU.subtract).then_inc(wl_ok, 1)
            low(0, 0)
            dve.wait_ge(cst_in, 80)
            dve.wait_ge(cst, 8)
            dve.wait_ge(rec_z, 2)
            per = 31
            body(0, 0, True, False)
            with dve.Fori(0, TT // 2 - 1) as i:
                c.enter(i, 2 * per)
                for b in (1, 0):
                    body(2 * i + 2 - b, b, False, False, i)
                c.leave(TT // 2 - 1)
            body(TT - 1, 1, False, True)
            dve.wait_ge(rk_mm, TT + 1)
            c.link(dve.tensor_reduce(out=sc[:, 12:13], in_=bank(7, 0, EXPERTS), axis=AX.X, op=ALU.max))
            c.link(dve.tensor_copy(g.most[:, :], sc[:, 12:13]))

        @block.tensor
        def _(pe):
            pe.wait_ge(wl_ok, 4)

            def times_out(t, b, first):
                pe.wait_ge(ml_ok, t + 1)
                for q in range(2):
                    for j in range(DK):
                        last = mm3(pe, bank(2 * b + q), mh[b][:, j, :], ml[b][:, j, :], woh[:, j, q * 512:(q + 1) * 512],
                                   wol[:, j, q * 512:(q + 1) * 512], j == 0, j == DK - 1)
                last.then_inc(w_mm, 1)

            def body(t, b, first, last, i=None):
                if not last:
                    if not first:
                        pe.wait_ge(h_ok, t)
                    times_out(t + 1, 1 - b, first)
                pe.wait_ge(u_ok, t + 1)
                for q in range(2):
                    for j in range(4):
                        last_i = pe.transpose(bank(4 + q, j * P, P), u[b][:, (4 * q + j) * P:(4 * q + j + 1) * P], g.ident[:, :])
                    last_i.then_inc(u_tr, 1)
                pe.wait_ge(uT_ok, 2 * t + 2)
                for j in range(DK):
                    ins = pe.matmul(bank(6, 0, R), uT[:, j, :], wr[:, j, :], start=j == 0, stop=j == DK - 1)
                ins.then_inc(lg_mm, 1)
                pe.wait_ge(M_ok, t + 1)
                if not first:
                    pe.wait_ge(cum_ok, t)
                pe.matmul(bank(7, 0, EXPERTS), upper[:, :], M[b][:, 2, :], start=True, stop=False)
                pe.matmul(bank(7, 0, EXPERTS), g.ones[:, :], Mcum[:, :], start=False, stop=True).then_inc(rk_mm, 1)

            pe.wait_ge(cst_in, 80)
            pe.wait_ge(cst, 8)
            times_out(0, 0, True)
            tiles(body, pe)
            pe.wait_ge(cum_ok, TT)
            pe.matmul(bank(7, 0, EXPERTS), g.ones[:, :], Mcum[:, :], start=True, stop=True).then_inc(rk_mm, 1)


def inside(e, d=0):
    return not isinstance(e, int) or 0 <= e + d < EXPERTS


def each_expert(eng, body):
    for e in (-2, -1, 0, 1, 2):
        body(e, e // 2, e % 2)
    with eng.Fori(0, (EXPERTS - 8) // 2) as i:
        body(2 * i + 3, i + 1, 1)
        body(2 * i + 4, i + 2, 0)
    for e in range(EXPERTS - 5, EXPERTS + 1):
        body(e, e // 2, e % 2)


def wait(eng, sem, value):
    if not isinstance(value, int) or value > 0:
        eng.wait_ge(sem, value)


def phase_experts(nc, g):
    with ExitStack() as ph:
        sb = lambda n, s, d=F32: ph.enter_context(nc.sbuf_tensor(n, s, d))
        sem = semaphores(nc, ph)
        up_h = [sb(f"m_up_h{b}", [P, 2, DK, DE], F32R) for b in range(2)]
        up_l = [sb(f"m_up_l{b}", [P, 2, DK, DE], F32R) for b in range(2)]
        dn_h = [sb(f"m_dn_h{b}", [P, 2, D], F32R) for b in range(2)]
        dn_l = [sb(f"m_dn_l{b}", [P, 2, D], F32R) for b in range(2)]
        x = [sb(f"m_x{b}", [CAP, D]) for b in range(2)]
        xT_h, xT_l = sb("m_xT_h", [P, DK, CAP], F32R), sb("m_xT_l", [P, DK, CAP], F32R)
        sig, prod, hid = sb("m_sig", [CAP, DE]), sb("m_prod", [CAP, DE]), sb("m_hid", [CAP, DE])
        hT_h, hT_l = sb("m_hT_h", [P, 2, CAP], F32R), sb("m_hT_l", [P, 2, CAP], F32R)
        y = [sb(f"m_y{b}", [CAP, D]) for b in range(2)]
        tab = sb("m_tab", [EXPERTS, CAP * ROWS])
        rows = sb("m_rows", [CAP, 2, EXPERTS], I32)
        gate = sb("m_gate", [CAP, EXPERTS])
        src_row = [sb(f"m_src_row{b}", [CAP, 1], I32) for b in range(2)]
        dst_row = [sb(f"m_dst_row{b}", [CAP, 1], I32) for b in range(2)]
        tab_in, tab_tr, rows_ok, x_zero = sem("m_tab_in"), sem("m_tab_tr"), sem("m_rows_ok"), sem("m_x_zero")
        x_in = [sem(f"m_x_in{b}") for b in range(2)]
        y_out = [sem(f"m_y_out{b}") for b in range(2)]
        row_ok = sem("m_row_ok")
        up_h_ok, up_l_ok, dn_h_ok, dn_l_ok = sem("m_up_h_ok"), sem("m_up_l_ok"), sem("m_dn_h_ok"), sem("m_dn_l_ok")
        x_tr, xh_ok, xl_ok, up_mm, sig_ok, prod_ok, hid_ok = (sem("m_x_tr"), sem("m_xh_ok"), sem("m_xl_ok"), sem("m_up_mm"),
                                                              sem("m_sig_ok"), sem("m_prod_ok"), sem("m_hid_ok"))
        h_tr, hh_ok, hl_ok, dn_mm, y_ok = sem("m_h_tr"), sem("m_hh_ok"), sem("m_hl_ok"), sem("m_dn_mm"), sem("m_y_ok")
        block = ph.enter_context(nc.Block())
        bank = lambda i, a=0, n=512, rows=P: g.ps[0:rows, i * 512 + a:i * 512 + a + n]
        turned = lambda i, n: bank(i, 0, n * CAP).rearrange("p (j t) -> p j t", j=n)
        X_BANK, UP_BANK, Y_BANK, H_BANK = 0, 2, 4, 6

        @block.sync
        def _(sp):
            sp.dma_start(tab[:, :], g.table.rearrange("(e s) r -> e s r", e=EXPERTS)[:, 0:CAP, :]
                         .rearrange("e s r -> e (s r)")).then_inc(tab_in, 16)

            def body(e, n, b):
                if inside(e, 4):
                    wait(sp, up_l_ok, 2 * e + 6)
                    g.load_up(sp, e + 4, b)
                if inside(e, 3) and (not isinstance(e, int) or e > -2):
                    wait(sp, dn_l_ok, e + 2)
                    g.load_down(sp, e + 3, 1 - b)

            each_expert(sp, body)

        @block.gpsimd
        def _(pool):
            k = [0]
            for b in range(2):
                pool.memset(x[b][:, :], 0.0).then_inc(x_zero, 1)
            pool.wait_ge(x_zero, 2)
            pool.wait_ge(rows_ok, 3)

            def body(e, n, b):
                before = k[0] if isinstance(e, int) else 2 * e + 1
                if inside(e, 2):
                    wait(pool, x_tr, 2 * e + 2)
                    settle(pool, g)
                    pool.tensor_copy(src_row[b][:, :], rows[:, 1, bass.ds(e + 2, 1)]).then_inc(row_ok, 1)
                    pool.wait_ge(row_ok, before + 1)
                    settle(pool, g)
                    pool.indirect_dma_start(out=x[b][:, :], out_offset=None, in_=g.u2,
                                            in_offset=bass.IndirectOffsetOnAxis(ap=src_row[b][:, 0:1], axis=0),
                                            bounds_check=SEQ - 1, oob_is_err=False).then_inc(x_in[b], 16)
                    before = before + 1
                if inside(e, -1):
                    pool.wait_ge(y_ok, 2 * e)
                    settle(pool, g)
                    pool.tensor_copy(dst_row[1 - b][:, :], rows[:, 0, bass.ds(e - 1, 1)]).then_inc(row_ok, 1)
                    pool.wait_ge(row_ok, before + 1)
                    settle(pool, g)
                    pool.indirect_dma_start(out=g.y, out_offset=bass.IndirectOffsetOnAxis(ap=dst_row[1 - b][:, 0:1], axis=0),
                                            in_=y[1 - b][:, :], in_offset=None,
                                            bounds_check=2 * SEQ - 1, oob_is_err=False).then_inc(y_out[1 - b], 16)
                    before = before + 1
                k[0] = before if isinstance(e, int) else 2 * (EXPERTS - 5) + 1

            each_expert(pool, body)
            for b in range(2):
                pool.wait_ge(y_out[b], 16 * (EXPERTS // 2))

        @block.scalar
        def _(act):
            act.wait_ge(rows_ok, 3)

            def body(e, n, b):
                if inside(e):
                    act.wait_ge(up_mm, e + 1)
                    act.activation(sig[:, :], bank(UP_BANK + b, 0, DE, CAP), ACT.Sigmoid).then_inc(sig_ok, 1)
                if inside(e, 1):
                    for q in range(2):
                        act.wait_ge(x_tr, 2 * e + q + 3)
                        act.activation(xT_h[:, 4 * q:4 * q + 4, :], turned(X_BANK + q, 4), ACT.Copy).then_inc(xh_ok, 1)
                if inside(e):
                    act.wait_ge(h_tr, e + 1)
                    act.activation(hT_h[:, :, :], turned(H_BANK + b, 2), ACT.Copy).then_inc(hh_ok, 1)
                if inside(e, -1):
                    if inside(e, -3):
                        act.wait_ge(y_out[1 - b], 16 * (n - 1 if b == 0 else n))
                    for q in range(2):
                        act.wait_ge(dn_mm, 2 * e + q - 1)
                        settle(act, g)
                        act.activation(y[1 - b][:, q * 512:(q + 1) * 512], bank(Y_BANK + q, rows=CAP), ACT.Copy,
                                       scale=gate[:, bass.ds(e - 1, 1)]).then_inc(y_ok, 1)
                if inside(e, 2):
                    act.wait_ge(g.w_up_in[b], 32 * (n + 2))
                    for r in range(2):
                        act.activation(up_h[b][:, r, :, :], g.r13[b][:, r, :, :], ACT.Copy).then_inc(up_h_ok, 1)
                if inside(e, 1):
                    act.wait_ge(g.w_down_in[1 - b], 16 * (n + 1 + b))
                    act.activation(dn_h[1 - b][:, :, :], g.r2[1 - b][:, :, :], ACT.Copy).then_inc(dn_h_ok, 1)

            each_expert(act, body)

        @block.vector
        def _(dve):
            dve.wait_ge(tab_tr, 1)
            for c in range(2):
                dve.tensor_copy(rows[:, c, :], bank(H_BANK + 1, 2 * c * EXPERTS, EXPERTS, CAP)).then_inc(rows_ok, 1)
            dve.tensor_copy(gate[:, :], bank(H_BANK + 1, EXPERTS, EXPERTS, CAP)).then_inc(rows_ok, 1)

            def body(e, n, b):
                if inside(e):
                    dve.wait_ge(sig_ok, e + 1)
                    dve.tensor_tensor(prod[:, :], sig[:, :], bank(UP_BANK + b, 0, DE, CAP), ALU.mult).then_inc(prod_ok, 1)
                    dve.wait_ge(prod_ok, e + 1)
                    dve.tensor_tensor(hid[:, :], prod[:, :], bank(UP_BANK + b, DE, DE, CAP), ALU.mult).then_inc(hid_ok, 1)
                if inside(e, 1):
                    for q in range(2):
                        dve.wait_ge(xh_ok, 2 * e + q + 3)
                        dve.tensor_tensor(xT_l[:, 4 * q:4 * q + 4, :], turned(X_BANK + q, 4),
                                          xT_h[:, 4 * q:4 * q + 4, :].bitcast(F32), ALU.subtract).then_inc(xl_ok, 1)
                if inside(e):
                    dve.wait_ge(hh_ok, e + 1)
                    dve.tensor_tensor(hT_l[:, :, :], turned(H_BANK + b, 2), hT_h[:, :, :].bitcast(F32),
                                      ALU.subtract).then_inc(hl_ok, 1)
                if inside(e, 2):
                    for r in range(2):
                        dve.wait_ge(up_h_ok, 2 * e + r + 5)
                        dve.tensor_tensor(up_l[b][:, r, :, :], g.r13[b][:, r, :, :], up_h[b][:, r, :, :].bitcast(F32),
                                          ALU.subtract).then_inc(up_l_ok, 1)
                if inside(e, 1):
                    dve.wait_ge(dn_h_ok, e + 2)
                    dve.tensor_tensor(dn_l[1 - b][:, :, :], g.r2[1 - b][:, :, :], dn_h[1 - b][:, :, :].bitcast(F32),
                                      ALU.subtract).then_inc(dn_l_ok, 1)

            each_expert(dve, body)

        @block.tensor
        def _(pe):
            pe.wait_ge(tab_in, 16)
            for c in range(3):
                ins = pe.transpose(bank(H_BANK + 1, c * EXPERTS, EXPERTS, CAP), tab[:, c::ROWS], g.ident[0:EXPERTS, 0:EXPERTS])
            ins.then_inc(tab_tr, 1)
            pe.wait_ge(rows_ok, 3)

            def body(e, n, b):
                if inside(e):
                    pe.wait_ge(up_l_ok, 2 * e + 2)
                    pe.wait_ge(xl_ok, 2 * e + 2)
                    for j in range(DK):
                        ins = mm3(pe, bank(UP_BANK + b, rows=CAP).rearrange("p (r f) -> p r f", r=2), xT_h[:, j, :], xT_l[:, j, :],
                                  up_h[b][:, :, j, :], up_l[b][:, :, j, :], j == 0, j == DK - 1)
                    ins.then_inc(up_mm, 1)
                if inside(e, 1):
                    pe.wait_ge(x_in[1 - b], 16 * (n + 1 + b))
                    for q in range(2):
                        for j in range(4):
                            ins = pe.transpose(bank(X_BANK + q, j * CAP, CAP), x[1 - b][:, 4 * q + j::DK], g.ident[0:CAP, 0:CAP])
                        ins.then_inc(x_tr, 1)
                if inside(e, -1):
                    pe.wait_ge(hl_ok, e)
                    pe.wait_ge(dn_l_ok, e)
                    if inside(e, -2):
                        pe.wait_ge(y_ok, 2 * e - 2)
                    for q in range(2):
                        for j in range(2):
                            ins = mm3(pe, bank(Y_BANK + q, rows=CAP), hT_h[:, j, :], hT_l[:, j, :],
                                      dn_h[1 - b][:, j, q * 512:(q + 1) * 512], dn_l[1 - b][:, j, q * 512:(q + 1) * 512],
                                      j == 0, j == 1)
                        ins.then_inc(dn_mm, 1)
                if inside(e):
                    pe.wait_ge(hid_ok, e + 1)
                    for j in range(2):
                        ins = pe.transpose(bank(H_BANK + b, j * CAP, CAP), hid[:, j::2], g.ident[0:CAP, 0:CAP])
                    ins.then_inc(h_tr, 1)

            each_expert(pe, body)


def phase_overflow(nc, g):
    BLOCKS = (SLOTS // CAP - 1) * EXPERTS
    with ExitStack() as ph:
        sb = lambda n, s, d=F32: ph.enter_context(nc.sbuf_tensor(n, s, d))
        sem = semaphores(nc, ph)
        x, xT = sb("v_x", [CAP, D]), sb("v_xT", [P, DK, CAP])
        sig, prod, hid, hT = sb("v_sig", [CAP, DE]), sb("v_prod", [CAP, DE]), sb("v_hid", [CAP, DE]), sb("v_hT", [P, 2, CAP])
        y = sb("v_y", [CAP, D])
        rec, rows = sb("v_rec", [CAP, ROWS]), sb("v_rows", [CAP, ROWS], I32)
        up_in, down_in, rec_in, x_zero = sem("v_up_in"), sem("v_down_in"), sem("v_rec_in"), sem("v_x_zero")
        rows_ok, x_in, x_tr, xT_ok, up_mm = sem("v_rows_ok"), sem("v_x_in"), sem("v_x_tr"), sem("v_xT_ok"), sem("v_up_mm")
        sig_ok, prod_ok, hid_ok, h_tr, hT_ok = sem("v_sig_ok"), sem("v_prod_ok"), sem("v_hid_ok"), sem("v_h_tr"), sem("v_hT_ok")
        dn_mm, y_ok, y_out, turn = sem("v_dn_mm"), sem("v_y_ok"), sem("v_y_out"), sem("v_turn")
        block = ph.enter_context(nc.Block())
        bank = lambda i, a=0, n=512, rows=P: g.ps[0:rows, i * 512 + a:i * 512 + a + n]
        turned = lambda i, n: bank(i, 0, n * CAP).rearrange("p (j t) -> p j t", j=n)
        X_BANK, UP_BANK, Y_BANK, H_BANK = 0, 2, 4, 6

        def blocks(eng, body):
            most = eng.value_load(g.most[0:1, 0:1], min_val=0, max_val=SLOTS)
            with eng.If(most > CAP):
                with eng.Fori(1, SLOTS // CAP) as c:
                    with eng.Fori(0, EXPERTS) as e:
                        body((c - 1) * EXPERTS + e, e, c)
                eng.sem_inc(g.settled, 1)
            with eng.Else():
                eng.sem_inc(g.settled, 1)

        @block.sync
        def _(sp):
            table = g.table.rearrange("(e b s) r -> e b s r", e=EXPERTS, s=CAP)
            up = [a[0].rearrange("e (p j) f -> p e j f", j=DK) for a in (g.w1, g.w3)]
            down = g.w2[0].rearrange("e (p j) n -> p e j n", j=2)

            def body(k, e, c):
                sp.wait_ge(turn, k + 1)
                sp.dma_start(rec[:, :], table[bass.ds(e, 1), bass.ds(c, 1), :, :].rearrange("a b s r -> (a b s) r")
                             ).then_inc(rec_in, 16)
                for r in range(2):
                    sp.dma_start(g.r13[0][:, r, :, :], up[r][:, bass.ds(e, 1), :, :].rearrange("p a j f -> p (a j) f")
                                 ).then_inc(up_in, 16)
                sp.dma_start(g.r2[0][:, :, :], down[:, bass.ds(e, 1), :, :].rearrange("p a j n -> p (a j) n")
                             ).then_inc(down_in, 16)

            blocks(sp, body)

        @block.gpsimd
        def _(pool):
            pool.memset(x[:, :], 0.0).then_inc(x_zero, 1)
            pool.sem_inc(turn, 1)
            pool.wait_ge(x_zero, 1)

            def body(k, e, c):
                pool.wait_ge(rows_ok, k + 1)
                settle(pool, g)
                pool.indirect_dma_start(out=x[:, :], out_offset=None, in_=g.u2,
                                        in_offset=bass.IndirectOffsetOnAxis(ap=rows[:, 2:3], axis=0),
                                        bounds_check=SEQ - 1, oob_is_err=False).then_inc(x_in, 16)
                pool.wait_ge(y_ok, 2 * k + 2)
                settle(pool, g)
                pool.indirect_dma_start(out=g.y, out_offset=bass.IndirectOffsetOnAxis(ap=rows[:, 0:1], axis=0),
                                        in_=y[:, :], in_offset=None,
                                        bounds_check=2 * SEQ - 1, oob_is_err=False).then_inc(y_out, 16)
                pool.wait_ge(y_out, 16 * k + 16)
                pool.sem_inc(turn, 1)

            blocks(pool, body)

        @block.scalar
        def _(act):
            def body(k, e, c):
                for q in range(2):
                    act.wait_ge(x_tr, 2 * k + q + 1)
                    act.activation(xT[:, 4 * q:4 * q + 4, :], turned(X_BANK + q, 4), ACT.Copy).then_inc(xT_ok, 1)
                act.wait_ge(up_mm, k + 1)
                act.activation(sig[:, :], bank(UP_BANK, 0, DE, CAP), ACT.Sigmoid).then_inc(sig_ok, 1)
                act.wait_ge(h_tr, k + 1)
                act.activation(hT[:, :, :], turned(H_BANK, 2), ACT.Copy).then_inc(hT_ok, 1)
                for q in range(2):
                    act.wait_ge(dn_mm, 2 * k + q + 1)
                    act.activation(y[:, q * 512:(q + 1) * 512], bank(Y_BANK + q, rows=CAP), ACT.Copy,
                                   scale=rec[:, 1:2]).then_inc(y_ok, 1)

            blocks(act, body)

        @block.vector
        def _(dve):
            def body(k, e, c):
                dve.wait_ge(rec_in, 16 * k + 16)
                dve.tensor_copy(rows[:, :], rec[:, :]).then_inc(rows_ok, 1)
                dve.wait_ge(sig_ok, k + 1)
                dve.tensor_tensor(prod[:, :], sig[:, :], bank(UP_BANK, 0, DE, CAP), ALU.mult).then_inc(prod_ok, 1)
                dve.wait_ge(prod_ok, k + 1)
                dve.tensor_tensor(hid[:, :], prod[:, :], bank(UP_BANK, DE, DE, CAP), ALU.mult).then_inc(hid_ok, 1)

            blocks(dve, body)

        @block.tensor
        def _(pe):
            def body(k, e, c):
                pe.wait_ge(x_in, 16 * k + 16)
                for q in range(2):
                    for j in range(4):
                        ins = pe.transpose(bank(X_BANK + q, j * CAP, CAP), x[:, 4 * q + j::DK], g.ident[0:CAP, 0:CAP])
                    ins.then_inc(x_tr, 1)
                pe.wait_ge(up_in, 32 * k + 32)
                pe.wait_ge(xT_ok, 2 * k + 2)
                for j in range(DK):
                    ins = pe.matmul(bank(UP_BANK, rows=CAP).rearrange("p (r f) -> p r f", r=2), xT[:, j, :],
                                    g.r13[0][:, :, j, :], start=j == 0, stop=j == DK - 1)
                ins.then_inc(up_mm, 1)
                pe.wait_ge(hid_ok, k + 1)
                for j in range(2):
                    ins = pe.transpose(bank(H_BANK, j * CAP, CAP), hid[:, j::2], g.ident[0:CAP, 0:CAP])
                ins.then_inc(h_tr, 1)
                pe.wait_ge(down_in, 16 * k + 16)
                pe.wait_ge(hT_ok, k + 1)
                for q in range(2):
                    for j in range(2):
                        ins = pe.matmul(bank(Y_BANK + q, rows=CAP), hT[:, j, :], g.r2[0][:, j, q * 512:(q + 1) * 512],
                                        start=j == 0, stop=j == 1)
                    ins.then_inc(dn_mm, 1)

            blocks(pe, body)


def phase_final(nc, g):
    with ExitStack() as ph:
        sb = lambda n, s, d=F32: ph.enter_context(nc.sbuf_tensor(n, s, d))
        sem = semaphores(nc, ph)
        NB = 4
        h = [sb(f"z_h{b}", [P, D]) for b in range(NB)]
        y = [sb(f"z_y{b}", [P, 2, D]) for b in range(NB)]
        o = [sb(f"z_o{b}", [P, D]) for b in range(NB)]
        gain, junk = sb("z_gain", [P, D]), sb("z_junk", [P, D])
        st = [sb(f"z_stat{b}", [P, 2]) for b in range(NB)]
        gain_in = sem("z_gain_in")
        t_in = [sem(f"z_t_in{b}") for b in range(NB)]
        stored = [sem(f"z_stored{b}") for b in range(NB)]
        s0_ok, s1_ok, ss_ok, rt_ok, rc_ok, o_ok = (sem("z_s0_ok"), sem("z_s1_ok"), sem("z_ss_ok"), sem("z_rt_ok"),
                                                   sem("z_rc_ok"), sem("z_o_ok"))
        block = ph.enter_context(nc.Block())
        y_src = g.y.rearrange("(t c) d -> t c d", c=2)

        def rounds(eng, body):
            with eng.Fori(0, TT // NB) as i:
                for b in range(NB):
                    body(NB * i + b, b, i)

        @block.sync
        def _(sp):
            def load(t, b):
                sp.dma_start(h[b][:, :], g.h[bass.ds(t * P, P), :]).then_inc(t_in[b], 16)
                sp.dma_start(y[b][:, :, :], y_src[bass.ds(t * P, P), :, :]).then_inc(t_in[b], 16)

            load(0, 0)
            sp.dma_start(gain[:, :], g.final_norm[None, :].to_broadcast([P, D])).then_inc(gain_in, 16)
            for b in range(1, NB):
                load(b, b)
            with sp.Fori(0, TT // NB - 1) as i:
                for b in range(NB):
                    sp.wait_ge(o_ok, NB * i + b + 1)
                    load(NB * i + NB + b, b)

        @block.gpsimd
        def _(pool):
            def body(t, b, i):
                pool.wait_ge(o_ok, t + 1)
                settle(pool, g)
                pool.dma_start(g.out[0, bass.ds(t * P, P), :], o[b][:, :]).then_inc(stored[b], 16)

            rounds(pool, body)
            for b in range(NB):
                pool.wait_ge(stored[b], 16 * (TT // NB))

        @block.scalar
        def _(act):
            def body(t, b, i):
                act.wait_ge(s1_ok, t + 1)
                act.activation(junk[:, :], h[b][:, :], ACT.Square, accum_out=st[b][:, 0:1]).then_inc(ss_ok, 1)
                act.wait_ge(ss_ok, t + 1)
                act.activation(st[b][:, 1:2], st[b][:, 0:1], ACT.Sqrt, scale=1.0 / D, bias=g.eps[:, :]).then_inc(rt_ok, 1)

            rounds(act, body)

        @block.vector
        def _(dve):
            dve.wait_ge(gain_in, 16)

            def body(t, b, i):
                dve.wait_ge(t_in[b], 32 * i + 32)
                for c, done in ((0, s0_ok), (1, s1_ok)):
                    dve.tensor_tensor(h[b][:, :], h[b][:, :], y[b][:, c, :], ALU.add).then_inc(done, 1)
                    dve.wait_ge(done, t + 1)
                dve.wait_ge(rt_ok, t + 1)
                dve.reciprocal(st[b][:, 1:2], st[b][:, 1:2]).then_inc(rc_ok, 1)
                dve.wait_ge(rc_ok, t + 1)
                wait(dve, stored[b], 16 * i)
                dve.scalar_tensor_tensor(out=o[b][:, :], in0=h[b][:, :], scalar=st[b][:, 1:2], in1=gain[:, :],
                                         op0=ALU.mult, op1=ALU.mult).then_inc(o_ok, 1)

            for b in range(NB):
                body(b, b, 0)
            with dve.Fori(1, TT // NB) as i:
                for b in range(NB):
                    body(NB * i + b, b, i)


def program(nc, a, out):
    g = Ctx(a, out)
    g.gates = nc.dram_tensor("gates", [2 * D, SEQ], F32, kind="Internal").ap()
    g.merged = nc.dram_tensor("merged", [D, SEQ], F32, kind="Internal").ap()
    g.h = nc.dram_tensor("h_mid", [SEQ, D], F32, kind="Internal").ap()
    g.u2 = nc.dram_tensor("u_moe", [SEQ, D], F32, kind="Internal").ap()
    g.y = nc.dram_tensor("y_moe", [2 * SEQ, D], F32, kind="Internal").ap()
    g.table = nc.dram_tensor("slots", [EXPERTS * SLOTS, ROWS], F32, kind="Internal").ap()
    with ExitStack() as keep:
        g.most = keep.enter_context(nc.sbuf_tensor("most", [P, 1], I32))
        g.ident = keep.enter_context(nc.sbuf_tensor("ident", [P, P], F32))
        g.ones = keep.enter_context(nc.sbuf_tensor("ones", [P, P], F32))
        g.eps = keep.enter_context(nc.sbuf_tensor("eps", [P, 1], F32))
        g.settled = keep.enter_context(nc.semaphore("settled"))
        g.ps = keep.enter_context(nc.psum_tensor("ps", [P, 8 * 512], F32))
        left = lambda st, n, sh, d=F32: st.enter_context(nc.sbuf_tensor(n, sh, d))
        oh = ExitStack()
        g.ohTh, g.ohTl = left(oh, "ohTh", [P, HG, SEQ], F32R), left(oh, "ohTl", [P, HG, SEQ], F32R)
        with ExitStack() as ust:
            g.uTh = ust.enter_context(nc.sbuf_tensor("uTh", [P, DK, NT], F32R, side="right"))
            g.uTl = ust.enter_context(nc.sbuf_tensor("uTl", [P, DK, NT], F32R, side="right"))
            phase_norm_in(nc, g)
            phase_gates(nc, g)
            phase_hgrn(nc, g)
            lat = ExitStack()
            g.cqh, g.cql = left(lat, "cqh", [P, 3, SEQ], F32R), left(lat, "cql", [P, 3, SEQ], F32R)
            g.ckh, g.ckl = left(lat, "ckh", [P, 2, NT], F32R), left(lat, "ckl", [P, 2, NT], F32R)
            g.KT = [left(lat, "KT0", [QH, NT])]
            g.cos, g.sin = left(lat, "cos", [QH, NT]), left(lat, "sin", [QH, NT])
            phase_latents(nc, g)
        om = ExitStack()
        g.omTh = om.enter_context(nc.sbuf_tensor("omTh", [P, 4, SEQ], F32R, side="right"))
        g.omTl = om.enter_context(nc.sbuf_tensor("omTl", [P, 4, SEQ], F32R, side="right"))
        phase_attention(nc, g)
        lat.close()
        phase_merge(nc, g)
        om.close()
        oh.close()
        wraw = ExitStack()
        g.r13 = [wraw.enter_context(nc.sbuf_tensor(f"r13_{b}", [P, 2, DK, DE], F32, side="right")) for b in range(2)]
        g.r2 = [wraw.enter_context(nc.sbuf_tensor(f"r2_{b}", [P, 2, D], F32, side="right")) for b in range(2)]
        g.w_up_in = [keep.enter_context(nc.semaphore(f"w_up_in{b}")) for b in range(2)]
        g.w_down_in = [keep.enter_context(nc.semaphore(f"w_down_in{b}")) for b in range(2)]
        g.load_up, g.load_down = expert_loaders(g)
        phase_output(nc, g)
        phase_experts(nc, g)
        phase_overflow(nc, g)
        wraw.close()
        phase_final(nc, g)

_INPUTS = ["x", "meta_tokens", "attn_norm", "w_in", "q_norm", "w_uq", "kv_norm", "w_ukv", "lb_table", "hg_norm",
           "w_br_mla", "w_br_hgrn", "b_gate", "w_out", "ffn_norm", "w_group", "b_group", "w_route", "b_route",
           "w1", "w3", "w2", "final_norm"]


def rotary():
    inv = (np.float32(10000.0) ** (-np.arange(0, ROPE, 2, dtype=np.float32) / np.float32(ROPE))).astype(np.float32)
    pos = np.concatenate([np.arange(META, META + SEQ), np.arange(META)]).astype(np.float32)
    ang = (inv[:, None] * pos[None, :]).astype(np.float32)
    cos, sin = np.cos(ang), np.sin(ang)
    return (np.concatenate([cos, cos], 0).astype(np.float32), np.concatenate([-sin, sin], 0).astype(np.float32))


def kernel(**inputs):
    import concourse.bacc as bacc
    from concourse.bass_utils import run_bass_kernel_spmd

    nc = bacc.Bacc("TRN2", target_bir_lowering=False, num_devices=1)
    arrays, aps = {}, {}
    cos, sin = rotary()
    for name in _INPUTS + ["rope_cos", "rope_sin"]:
        a = cos if name == "rope_cos" else sin if name == "rope_sin" else np.ascontiguousarray(inputs[name])
        arrays["in_" + name] = a
        aps[name] = nc.dram_tensor("in_" + name, a.shape, mybir.dt.from_np(a.dtype), kind="ExternalInput").ap()
    out = nc.dram_tensor("out_0", (1, SEQ, D), F32, kind="ExternalOutput").ap()
    program(nc, aps, out)
    r = run_bass_kernel_spmd(nc, [arrays], core_ids=[0])
    return r.results[0]["out_0"]
```

```python
from contextlib import ExitStack

import numpy as np
import concourse.bass as bass
from concourse import mybir

F32 = mybir.dt.float32
F32R = mybir.dt.float32r
I32 = mybir.dt.int32
U32 = mybir.dt.uint32
ACT = mybir.ActivationFunctionType
ALU = mybir.AluOpType
AX = mybir.AxisListType

P = 128
D = 1024
DK = D // P
SEQ = 1024
TT = SEQ // P
META = 16
NT = SEQ + META
EPS = 1e-6
QL, KVL, ROPE = 384, 256, 32
NOPE, VD, HEADS = 64, 64, 8
QH = NOPE + ROPE
HG = 4
CH = 32
SCALE = QH ** -0.5
C_CQ, C_CKV = 0, QL
C_KPE = QL + KVL
C_HQ = C_KPE + ROPE
C_HF = C_HQ + 512
C_HI = C_HF + 512
C_HG = C_HI + 512
C_GM = C_HG + 512
GROUPS, PER_GROUP, EXPERTS, DE = 8, 8, 64, 256
ROWS = 4
SLOTS = 1024
CAP = 64
WIDE = 96
SKIP = 4096.0
SWAP = [(i + ROPE // 2) % ROPE for i in range(ROPE)]


class Steps:

    def __init__(self, eng, sem):
        self.eng, self.sem, self.base, self.k = eng, sem, 0, 0

    def mark(self, ins):
        ins.then_inc(self.sem, 1)
        self.k += 1

    def link(self, ins):
        self.mark(ins)
        self.eng.wait_ge(self.sem, self.base + self.k)

    def now(self):
        return self.base + self.k

    def enter(self, i, per):
        self.outer, self.per = self.base + self.k, per
        self.base, self.k = self.outer + i * per, 0

    def leave(self, n):
        assert self.k == self.per, (self.k, self.per)
        self.base, self.k = self.outer + n * self.per, 0


class Ctx:

    def __init__(self, a, out):
        self.x, self.meta_tokens, self.attn_norm, self.w_in = a["x"], a["meta_tokens"], a["attn_norm"], a["w_in"]
        self.q_norm, self.w_uq, self.kv_norm, self.w_ukv = a["q_norm"], a["w_uq"], a["kv_norm"], a["w_ukv"]
        self.lb_table, self.hg_norm, self.b_gate = a["lb_table"], a["hg_norm"], a["b_gate"]
        self.w_br_mla, self.w_br_hgrn, self.w_out = a["w_br_mla"], a["w_br_hgrn"], a["w_out"]
        self.ffn_norm, self.w_group, self.b_group = a["ffn_norm"], a["w_group"], a["b_group"]
        self.w_route, self.b_route, self.final_norm = a["w_route"], a["b_route"], a["final_norm"]
        self.w1, self.w3, self.w2 = a["w1"], a["w3"], a["w2"]
        self.rope_cos, self.rope_sin = a["rope_cos"], a["rope_sin"]
        self.out = out


def semaphores(nc, phase):
    made = []

    def clear():
        nc.clear_and_free_semaphores(made)
        nc.all_engine_barrier()

    phase.callback(clear)

    def sem(name):
        made.append(nc.alloc_semaphore(name=name))
        return made[-1]

    return sem


def settle(eng, g):
    eng.sem_inc(g.settled, 1)


def mm3(pe, out, lh, ll, rh, rl, start, stop):
    pe.matmul(out, lh, rh, start=start, stop=False)
    pe.matmul(out, lh, rl, start=False, stop=False)
    return pe.matmul(out, ll, rh, start=False, stop=stop)


def phase_norm_in(nc, g):
    with ExitStack() as ph:
        sb = lambda n, s, d=F32: ph.enter_context(nc.sbuf_tensor(n, s, d))
        sem = semaphores(nc, ph)
        x = sb("a_x", [P, 2, D])
        sq = sb("a_sq", [P, D])
        u = sb("a_u", [P, 2, D])
        gain = sb("a_gain", [P, D])
        ss = sb("a_ss", [P, 4])
        x_in = [sem("a_x_in0"), sem("a_x_in1")]
        const_in, meta_in = sem("a_const_in"), sem("a_meta_in")
        ss_done, rt_done, u_done, tr_done = sem("a_ss_done"), sem("a_rt_done"), sem("a_u_done"), sem("a_tr_done")
        hi_done, lo_done, dv, consts = sem("a_hi"), sem("a_lo"), sem("a_dv"), sem("a_consts")
        block = ph.enter_context(nc.Block())

        @block.sync
        def _(sp):
            sp.dma_start(x[0:META, 1, :], g.meta_tokens).then_inc(meta_in, 16)
            sp.dma_start(gain[:, :], g.attn_norm[0:1, :].to_broadcast([P, D])).then_inc(const_in, 16)
            sp.dma_start(x[:, 0, :], g.x[0, 0:P, :]).then_inc(x_in[0], 16)
            sp.wait_ge(u_done, 1)
            sp.dma_start(x[:, 1, :], g.x[0, P:2 * P, :]).then_inc(x_in[1], 16)
            with sp.Fori(0, TT // 2 - 1) as i:
                for b in range(2):
                    sp.wait_ge(u_done, 2 * i + b + 2)
                    t = 2 * i + b + 2
                    sp.dma_start(x[:, b, :], g.x[0, bass.ds(t * P, P), :]).then_inc(x_in[b], 16)

        @block.gpsimd
        def _(pool):
            pool.memset(g.ident[:, :], 0.0).then_inc(consts, 1)
            pool.memset(g.ones[:, :], 1.0).then_inc(consts, 1)
            pool.memset(g.eps[:, :], EPS).then_inc(consts, 1)
            pool.wait_ge(consts, 3)
            pool.affine_select(out=g.ident[:, :], in_=g.ident[:, :], compare_op=ALU.not_equal, fill=1.0,
                               base=0, pattern=[[-1, P]], channel_multiplier=1).then_inc(consts, 1)

        @block.scalar
        def _(act):
            act.wait_ge(consts, 4)

            def sums(n, xs, rows, b):
                act.activation(sq[0:rows, :], xs, ACT.Square, accum_out=ss[0:rows, b:b + 1]).then_inc(ss_done, 1)
                act.wait_ge(ss_done, n + 1)
                act.activation(ss[0:rows, 2 + b:3 + b], ss[0:rows, b:b + 1], ACT.Sqrt, scale=1.0 / D,
                               bias=g.eps[0:rows, :]).then_inc(rt_done, 1)

            def evac(n, rows, b, col):
                for q in range(2):
                    act.wait_ge(tr_done, 2 * n + q + 1)
                    settle(act, g)
                    src = g.ps[:, (2 * b + q) * 512:(2 * b + q + 1) * 512].rearrange("p (j t) -> p j t", j=4)
                    act.activation(g.uTh[:, 4 * q:4 * q + 4, bass.ds(col, rows)], src[:, :, 0:rows],
                                   ACT.Copy).then_inc(hi_done, 1)

            act.wait_ge(meta_in, 16)
            sums(0, x[0:META, 1, :], META, 1)
            evac(0, META, 1, SEQ)
            with act.Fori(0, TT // 2) as i:
                for b in range(2):
                    act.wait_ge(x_in[b], 16 * i + 16)
                    act.wait_ge(u_done, 2 * i + b + 1)
                    sums(2 * i + b + 1, x[:, b, :], P, b)
                    evac(2 * i + b + 1, P, b, (2 * i + b) * P)

        @block.vector
        def _(dve):
            v = Steps(dve, dv)

            def scaled(n, rows, b):
                dve.wait_ge(rt_done, n + 1)
                v.link(dve.reciprocal(ss[0:rows, 2 + b:3 + b], ss[0:rows, 2 + b:3 + b]))
                dve.scalar_tensor_tensor(out=u[0:rows, b, :], in0=x[0:rows, b, :], scalar=ss[0:rows, 2 + b:3 + b],
                                         in1=gain[0:rows, :], op0=ALU.mult, op1=ALU.mult).then_inc(u_done, 1)

            def low(n, rows, b, col):
                for q in range(2):
                    dve.wait_ge(hi_done, 2 * n + q + 1)
                    src = g.ps[:, (2 * b + q) * 512:(2 * b + q + 1) * 512].rearrange("p (j t) -> p j t", j=4)
                    dve.tensor_tensor(g.uTl[:, 4 * q:4 * q + 4, bass.ds(col, rows)], src[:, :, 0:rows],
                                      g.uTh[:, 4 * q:4 * q + 4, bass.ds(col, rows)].bitcast(F32),
                                      ALU.subtract).then_inc(lo_done, 1)

            dve.wait_ge(const_in, 16)
            dve.wait_ge(meta_in, 16)
            scaled(0, META, 1)
            low(0, META, 1, SEQ)
            with dve.Fori(0, TT // 2) as i:
                v.enter(i, 2)
                for b in range(2):
                    dve.wait_ge(x_in[b], 16 * i + 16)
                    scaled(2 * i + b + 1, P, b)
                    low(2 * i + b + 1, P, b, (2 * i + b) * P)
                v.leave(TT // 2)

        @block.tensor
        def _(pe):
            pe.wait_ge(consts, 4)

            def flip(n, rows, b):
                pe.wait_ge(u_done, n + 1)
                for q in range(2):
                    for j in range(4):
                        last = pe.transpose(g.ps[:, (2 * b + q) * 512 + j * P:(2 * b + q) * 512 + j * P + rows],
                                            u[0:rows, b, 4 * q + j::DK], g.ident[0:rows, 0:rows])
                    last.then_inc(tr_done, 1)

            flip(0, META, 1)
            with pe.Fori(0, TT // 2) as i:
                for b in range(2):
                    pe.wait_ge(lo_done, 4 * i + 2 * b + 1)
                    flip(2 * i + b + 1, P, b)


def phase_gates(nc, g):
    NB = 2 * DK
    with ExitStack() as ph:
        sb = lambda n, s, d=F32: ph.enter_context(nc.sbuf_tensor(n, s, d))
        sem = semaphores(nc, ph)
        w = [sb(f"g_w{b}", [P, DK, P]) for b in range(2)]
        wh = [sb(f"g_wh{b}", [P, DK, P], F32R) for b in range(2)]
        wl = [sb(f"g_wl{b}", [P, DK, P], F32R) for b in range(2)]
        sg = [sb(f"g_sg{b}", [P, SEQ]) for b in range(2)]
        bias = sb("g_bias", [P, NB])
        w_in = [sem(f"g_w_in{b}") for b in range(2)]
        out_sem = [sem(f"g_out{b}") for b in range(2)]
        bias_in, wh_done, wl_done, mm_done, sg_done = (sem("g_bias_in"), sem("g_wh_done"), sem("g_wl_done"),
                                                       sem("g_mm_done"), sem("g_sg_done"))
        block = ph.enter_context(nc.Block())
        w_src = g.w_in[0].rearrange("(p j) n -> p j n", j=DK)

        @block.sync
        def _(sp):
            with nc.allow_non_contiguous_dma(reason="a small bias turned once"):
                sp.dma_start(bias[:, :], g.b_gate[0].rearrange("a (j p) -> p (a j)", p=P)).then_inc(bias_in, 16)
            for b in range(2):
                sp.dma_start(w[b][:, :, :], w_src[:, :, C_GM + b * P:C_GM + (b + 1) * P]).then_inc(w_in[b], 16)
            with sp.Fori(0, NB // 2 - 1) as i:
                for b in range(2):
                    sp.wait_ge(wl_done, 2 * i + b + 1)
                    sp.dma_start(w[b][:, :, :], w_src[:, :, bass.ds(C_GM + (2 * i + b + 2) * P, P)]).then_inc(w_in[b], 16)

        @block.gpsimd
        def _(pool):
            with pool.Fori(0, NB // 2) as i:
                for b in range(2):
                    pool.wait_ge(sg_done, 4 * i + 2 * b + 2)
                    settle(pool, g)
                    pool.dma_start(g.gates[bass.ds((2 * i + b) * P, P), :], sg[b][:, :]).then_inc(out_sem[b], 16)
            for b in range(2):
                pool.wait_ge(out_sem[b], 16 * (NB // 2))

        @block.scalar
        def _(act):
            act.wait_ge(bias_in, 16)

            def split(b, turn):
                act.wait_ge(w_in[b], 16 * turn + 16)
                act.activation(wh[b][:, :, :], w[b][:, :, :], ACT.Copy).then_inc(wh_done, 1)

            def gate(b, n):
                for q in range(2):
                    act.wait_ge(mm_done, 2 * n + q + 1)
                    settle(act, g)
                    act.activation(sg[b][:, q * 512:(q + 1) * 512], g.ps[:, (2 * b + q) * 512:(2 * b + q + 1) * 512],
                                   ACT.Sigmoid, bias=bias[:, bass.ds(n, 1)]).then_inc(sg_done, 1)

            split(0, 0)
            split(1, 0)
            gate(0, 0)
            act.wait_ge(mm_done, 2)
            split(0, 1)
            gate(1, 1)
            with act.Fori(0, NB // 2 - 2) as i:
                for b in range(2):
                    act.wait_ge(mm_done, 4 * i + 2 * b + 4)
                    split(1 - b, i + 1 + b)
                    act.wait_ge(out_sem[b], 16 * i + 16)
                    gate(b, 2 * i + b + 2)
            act.wait_ge(mm_done, 2 * (NB - 2))
            split(1, NB // 2 - 1)
            for b in range(2):
                act.wait_ge(out_sem[b], 16 * (NB // 2 - 1))
                gate(b, NB - 2 + b)

        @block.vector
        def _(dve):
            with dve.Fori(0, NB // 2) as i:
                for b in range(2):
                    dve.wait_ge(wh_done, 2 * i + b + 1)
                    dve.tensor_tensor(wl[b][:, :, :], w[b][:, :, :], wh[b][:, :, :].bitcast(F32),
                                      ALU.subtract).then_inc(wl_done, 1)

        @block.tensor
        def _(pe):
            def project(n, b):
                pe.wait_ge(wl_done, n + 1)
                for q in range(2):
                    for j in range(DK):
                        last = mm3(pe, g.ps[:, (2 * b + q) * 512:(2 * b + q + 1) * 512], wh[b][:, j, :], wl[b][:, j, :],
                                   g.uTh[:, j, q * 512:(q + 1) * 512], g.uTl[:, j, q * 512:(q + 1) * 512],
                                   j == 0, j == DK - 1)
                    last.then_inc(mm_done, 1)

            project(0, 0)
            project(1, 1)
            with pe.Fori(1, NB // 2) as i:
                for b in range(2):
                    pe.wait_ge(sg_done, 4 * i + 2 * b - 2)
                    project(2 * i + b, b)


def phase_hgrn(nc, g):
    NCH = SEQ // CH
    with ExitStack() as ph:
        sb = lambda n, s, d=F32: ph.enter_context(nc.sbuf_tensor(n, s, d))
        sem = semaphores(nc, ph)
        w = [sb(f"h_w{b}", [P, DK, P]) for b in range(2)]
        wh = [sb(f"h_wh{b}", [P, DK, P], F32R) for b in range(2)]
        wl = [sb(f"h_wl{b}", [P, DK, P], F32R) for b in range(2)]
        lb_raw, lb, oml, hgain = sb("h_lb_raw", [P, 2, HG]), sb("h_lb", [P, HG]), sb("h_oml", [P, HG]), sb("h_hgain", [P, HG])
        lbd = sb("h_lbd", [P, HG])
        reset = sb("h_reset", [P, NT])
        causal = sb("h_causal", [P, P])
        f, k, lf, bb, d1 = sb("h_f", [P, NT]), sb("h_k", [P, NT]), sb("h_lf", [P, NT]), sb("h_b", [P, NT]), sb("h_d1", [P, SEQ])
        qs, ks, qd, kd = sb("h_qs", [P, SEQ]), sb("h_ks", [P, SEQ]), sb("h_qd", [P, SEQ]), sb("h_kd", [P, NT])
        q, vt, gt, ot = sb("h_q", [P, SEQ]), sb("h_vt", [P, NT]), sb("h_gt", [P, SEQ]), sb("h_ot", [P, SEQ])
        dec = sb("h_dec", [P, NCH])
        v = sb("h_v", [P, TT + 1, P])
        kdn = sb("h_kdn", [P, 2, P])
        kdm = sb("h_kdm", [META, P])
        at = sb("h_at", [P, 2, P])
        vb = [sb(f"h_vb{b}", [P, 4 * P]) for b in range(2)]
        S = sb("h_S", [P, 8, P])
        vb_zero, vb_ok = sem("h_vb_zero"), sem("h_vb_ok")
        cst_in, cst, lb_ok = sem("h_cst_in"), sem("h_cst"), sem("h_lb_ok")
        w_in = [sem(f"h_w_in{b}") for b in range(2)]
        wh_done, wl_done, mm_done = sem("h_wh_done"), sem("h_wl_done"), sem("h_mm_done")
        sig_f, f_ok, lf_ok, b_ok, sig_q, e_ok, kd_ok = (sem("h_sig_f"), sem("h_f_ok"), sem("h_lf_ok"), sem("h_b_ok"),
                                                        sem("h_sig_q"), sem("h_e_ok"), sem("h_kd_ok"))
        q_ok, sig_g, g_ok, vt_ok, vtr, v_ok = (sem("h_q_ok"), sem("h_sig_g"), sem("h_g_ok"), sem("h_vt_ok"),
                                               sem("h_vtr"), sem("h_v_ok"))
        ktr, kdn_ok, s0_mm, s0_ok, a_mm, a_ok, kv_mm, s_ok, o_mm, o_ok = (
            sem("h_ktr"), sem("h_kdn_ok"), sem("h_s0_mm"), sem("h_s0_ok"), sem("h_a_mm"), sem("h_a_ok"),
            sem("h_kv_mm"), sem("h_s_ok"), sem("h_o_mm"), sem("h_o_ok"))
        sq_ok, ms_mm, rt_ok, on_ok, hi_ok, lo_ok, dv = (sem("h_sq_ok"), sem("h_ms_mm"), sem("h_rt_ok"), sem("h_on_ok"),
                                                        sem("h_hi_ok"), sem("h_lo_ok"), sem("h_dv"))
        block = ph.enter_context(nc.Block())
        w_src = g.w_in[0].rearrange("(p j) n -> p j n", j=DK)
        bank = lambda i, a=0, n=512: g.ps[:, i * 512 + a:i * 512 + a + n]
        pieces = [(0, 512), (512, 512), (SEQ, META)]
        COLS = [C_HF, C_HI, C_HQ, C_HG]
        FB, VB, QB, GB = 0, 3, 0, 3
        AB, KVB, TB, OB = 0, 3, 6, [2, 5]
        chunked = lambda t: t[:, 0:SEQ].rearrange("p (c t) -> p c t", t=CH)

        @block.sync
        def _(sp):
            with nc.allow_non_contiguous_dma(reason="small vectors turned once"):
                sp.dma_start(lb_raw[:, :, :], g.lb_table.rearrange("a (h p) -> p a h", p=P)).then_inc(cst_in, 16)
                sp.dma_start(hgain[:, :], g.hg_norm[0].rearrange("(h p) -> p h", p=P)).then_inc(cst_in, 16)
            for r in range(2):
                sp.dma_start(w[r][:, :, :], w_src[:, :, COLS[r]:COLS[r] + P]).then_inc(w_in[r], 16)
            with sp.Fori(0, HG) as h:
                for r in range(4):
                    col = COLS[(r + 2) % 4] + h * P + (P if r >= 2 else 0)
                    sp.wait_ge(wl_done, 4 * h + r + 1)
                    sp.dma_start(w[r % 2][:, :, :], w_src[:, :, bass.ds(col, P)]).then_inc(w_in[r % 2], 16)
            for b in range(2):
                sp.wait_ge(w_in[b], 16 * (2 * HG + 1))

        @block.gpsimd
        def _(pool):
            pool.memset(reset[:, :], 1.0).then_inc(cst, 1)
            pool.memset(at[:, :, :], 0.0).then_inc(cst, 1)
            pool.wait_ge(cst, 2)
            pool.memset(reset[:, 0:SEQ:CH], 0.0).then_inc(cst, 1)
            pool.memset(reset[:, SEQ:SEQ + 1], 0.0).then_inc(cst, 1)
            cv = causal[:, :].rearrange("p (c t) -> p c t", t=CH)
            ov = g.ones[:, :].rearrange("p (c t) -> p c t", t=CH)
            pool.affine_select(out=cv, in_=ov, compare_op=ALU.is_ge, fill=0.0, base=0,
                               pattern=[[CH, P // CH], [1, CH]], channel_multiplier=-1).then_inc(cst, 1)
            pool.wait_ge(cst, 5)
            pool.affine_select(out=cv, in_=cv, compare_op=ALU.is_ge, fill=0.0, base=0,
                               pattern=[[-CH, P // CH], [0, CH]], channel_multiplier=1).then_inc(cst, 1)
            for b in range(2):
                pool.memset(vb[b][:, :], 0.0).then_inc(vb_zero, 1)
            pool.wait_ge(vb_zero, 2)

            def spread(h, t):
                for ci in range(4):
                    rows = slice(ci * CH, (ci + 1) * CH)
                    pool.tensor_copy(vb[t % 2][rows, ci * P:(ci + 1) * P], v[rows, t, :]).then_inc(vb_ok, 1)

            with pool.Fori(0, HG) as h:
                for t in range(TT):
                    pool.wait_ge(v_ok, 3 * h + 2)
                    if t >= 2:
                        pool.wait_ge(kv_mm, TT * h + t - 1)
                    settle(pool, g)
                    spread(h, t)

        @block.scalar
        def _(act):
            def split(b, n_in, n_mm):
                if n_mm is not None:
                    act.wait_ge(mm_done, n_mm)
                act.wait_ge(w_in[b], n_in)
                act.activation(wh[b][:, :, :], w[b][:, :, :], ACT.Copy).then_inc(wh_done, 1)

            act.wait_ge(cst_in, 32)
            split(0, 16, None)
            split(1, 16, None)
            act.wait_ge(dv, 1)
            act.activation(lb[:, :], lbd[:, :], ACT.Sigmoid).then_inc(lb_ok, 1)
            with act.Fori(0, HG) as h:
                w0 = 32 * h + 32
                for n, (c, m) in enumerate(pieces):
                    act.wait_ge(mm_done, 10 * h + n + 1)
                    act.activation(f[:, c:c + m], bank(FB + n, 0, m), ACT.Sigmoid).then_inc(sig_f, 1)
                split(0, w0, 10 * h + 3)
                for n, (c, m) in enumerate(pieces):
                    act.wait_ge(mm_done, 10 * h + n + 4)
                    act.activation(vt[:, c:c + m], bank(VB + n, 0, m), ACT.Copy).then_inc(vt_ok, 1)
                split(1, w0, 10 * h + 6)
                for n in range(2):
                    act.wait_ge(mm_done, 10 * h + n + 7)
                    act.activation(q[:, n * 512:(n + 1) * 512], bank(QB + n), ACT.Sigmoid).then_inc(sig_q, 1)
                split(0, w0 + 16, 10 * h + 8)
                for n in range(2):
                    act.wait_ge(mm_done, 10 * h + n + 9)
                    act.activation(gt[:, n * 512:(n + 1) * 512], bank(GB + n), ACT.Sigmoid).then_inc(sig_g, 1)
                split(1, w0 + 16, 10 * h + 10)
                act.wait_ge(f_ok, h + 1)
                act.activation(lf[:, :], f[:, :], ACT.Ln).then_inc(lf_ok, 1)
                act.wait_ge(b_ok, 3 * h + 3)
                act.activation(qs[:, :], d1[:, :], ACT.Exp).then_inc(e_ok, 1)
                act.activation(ks[:, :], d1[:, :], ACT.Exp, scale=-1.0).then_inc(e_ok, 1)
                act.activation(qd[:, :], bb[:, 0:SEQ], ACT.Exp).then_inc(e_ok, 1)
                act.activation(kd[:, :], lf[:, :], ACT.Exp).then_inc(e_ok, 1)
                act.activation(dec[:, :], bb[:, CH - 1:SEQ:CH], ACT.Exp).then_inc(e_ok, 1)
                for n in range(2):
                    act.wait_ge(vtr, 3 * h + n + 1)
                    act.activation(v[:, 4 * n:4 * n + 4, :], bank(6 + n).rearrange("p (t c) -> p t c", t=4),
                                   ACT.Copy).then_inc(v_ok, 1)
                act.wait_ge(vtr, 3 * h + 3)
                act.activation(v[0:META, TT, :], g.ps[0:META, 2 * 512:2 * 512 + P], ACT.Copy).then_inc(v_ok, 1)
                act.wait_ge(ktr, 9 * h + 1)
                act.activation(kdm[:, :], g.ps[0:META, 2 * 512:2 * 512 + P], ACT.Copy).then_inc(kdn_ok, 1)
                act.wait_ge(s0_mm, h + 1)
                act.activation(S[:, 0, :], bank(5, 0, P), ACT.Copy).then_inc(s0_ok, 1)

                def kd_rows(t):
                    act.wait_ge(ktr, 9 * h + t + 2)
                    act.activation(kdn[:, t % 2, :], bank(TB + t % 2, 0, P), ACT.Copy).then_inc(kdn_ok, 1)

                kd_rows(0)
                for t in range(TT):
                    if t + 1 < TT:
                        kd_rows(t + 1)
                    act.wait_ge(o_mm, TT * h + t + 1)
                    act.activation(ot[:, t * P:(t + 1) * P], bank(OB[t % 2], 0, P), ACT.Copy).then_inc(o_ok, 1)
                act.wait_ge(o_ok, TT * h + TT)
                act.activation(d1[:, :], ot[:, :], ACT.Square).then_inc(sq_ok, 1)
                for n in range(2):
                    act.wait_ge(ms_mm, 2 * h + n + 1)
                    act.activation(qs[:, n * 512:(n + 1) * 512], bank(TB + n), ACT.Sqrt, scale=1.0 / P,
                                   bias=g.eps[:, :]).then_inc(rt_ok, 1)
                act.wait_ge(on_ok, h + 1)
                settle(act, g)
                act.activation(g.ohTh[:, bass.ds(h, 1), :], ot[:, :].rearrange("p (a t) -> p a t", a=1),
                               ACT.Copy).then_inc(hi_ok, 1)

        @block.vector
        def _(dve):
            c = Steps(dve, dv)

            def low(b, n):
                dve.wait_ge(wh_done, n)
                dve.tensor_tensor(wl[b][:, :, :], w[b][:, :, :], wh[b][:, :, :].bitcast(F32),
                                  ALU.subtract).then_inc(wl_done, 1)

            dve.wait_ge(cst_in, 32)
            c.link(dve.tensor_tensor(lbd[:, :], lb_raw[:, 0, :], lb_raw[:, 1, :], ALU.subtract))
            low(0, 1)
            low(1, 2)
            dve.wait_ge(cst, 6)
            dve.wait_ge(lb_ok, 1)
            c.link(dve.tensor_scalar(oml[:, :], lb[:, :], -1.0, 1.0, ALU.mult, ALU.add))
            with dve.Fori(0, HG) as h:
                c.enter(h, 8)
                dve.wait_ge(sig_f, 3 * h + 3)
                c.link(dve.tensor_scalar(f[:, :], f[:, :], oml[:, bass.ds(h, 1)], lb[:, bass.ds(h, 1)], ALU.mult, ALU.add))
                dve.tensor_scalar(k[:, :], f[:, :], -1.0, 1.0, ALU.mult, ALU.add).then_inc(f_ok, 1)
                low(0, 4 * h + 3)
                low(1, 4 * h + 4)
                for n in range(2):
                    dve.wait_ge(sig_q, 2 * h + n + 1)
                    dve.tensor_tensor(q[:, n * 512:(n + 1) * 512], q[:, n * 512:(n + 1) * 512], bank(QB + n),
                                      ALU.mult).then_inc(q_ok, 1)
                low(0, 4 * h + 5)
                for n in range(2):
                    dve.wait_ge(sig_g, 2 * h + n + 1)
                    dve.scalar_tensor_tensor(out=gt[:, n * 512:(n + 1) * 512], in0=gt[:, n * 512:(n + 1) * 512],
                                             scalar=hgain[:, bass.ds(h, 1)], in1=bank(GB + n),
                                             op0=ALU.mult, op1=ALU.mult).then_inc(g_ok, 1)
                low(1, 4 * h + 6)
                dve.wait_ge(lf_ok, h + 1)
                dve.tensor_tensor_scan(bb[:, :], reset[:, :], lf[:, :], 0.0, ALU.mult, ALU.add).then_inc(b_ok, 1)
                dve.wait_ge(b_ok, 3 * h + 1)
                bv, dv1, dv2 = chunked(bb), chunked(d1), chunked(lf)
                c.mark(dve.tensor_tensor(dv1, bv, bv[:, :, CH // 2 - 1:CH // 2].to_broadcast([P, NCH, CH]), ALU.subtract))
                dve.tensor_tensor(dv2, bv[:, :, CH - 1:CH].to_broadcast([P, NCH, CH]), bv, ALU.subtract).then_inc(b_ok, 1)
                dve.tensor_tensor(lf[:, SEQ:NT], bb[:, NT - 1:NT].to_broadcast([P, META]), bb[:, SEQ:NT],
                                  ALU.subtract).then_inc(b_ok, 1)
                dve.wait_ge(q_ok, 2 * h + 2)
                dve.wait_ge(e_ok, 5 * h + 5)
                c.mark(dve.tensor_tensor(qs[:, :], qs[:, :], q[:, :], ALU.mult))
                c.mark(dve.tensor_tensor(ks[:, :], ks[:, :], k[:, 0:SEQ], ALU.mult))
                c.mark(dve.tensor_tensor(qd[:, :], qd[:, :], q[:, :], ALU.mult))
                dve.tensor_tensor(kd[:, :], kd[:, :], k[:, :], ALU.mult).then_inc(kd_ok, 1)
                dve.wait_ge(s0_ok, h + 1)

                def scores(t):
                    dve.wait_ge(a_mm, TT * h + t + 1)
                    settle(dve, g)
                    dve.copy_predicated(at[:, t % 2, :], causal[:, :].bitcast(U32), bank(AB + t % 2, 0, P)).then_inc(a_ok, 1)

                scores(0)
                for t in range(TT):
                    dve.wait_ge(kv_mm, TT * h + t + 1)
                    for ci in range(4):
                        n = 4 * t + ci
                        if n == 4 * TT - 1:
                            break
                        if n:
                            dve.wait_ge(s_ok, (4 * TT - 1) * h + n)
                        if ci == 3 and t >= 1:
                            dve.wait_ge(o_mm, TT * h + t)
                        dve.scalar_tensor_tensor(out=S[:, (n + 1) % 8, :], in0=S[:, n % 8, :], scalar=dec[:, n:n + 1],
                                                 in1=bank(KVB + t % 2, ci * P, P), op0=ALU.mult,
                                                 op1=ALU.add).then_inc(s_ok, 1)
                    if t + 1 < TT:
                        scores(t + 1)
                for n in range(2):
                    dve.wait_ge(rt_ok, 2 * h + n + 1)
                c.link(dve.reciprocal(qs[:, :], qs[:, :]))
                dve.wait_ge(o_ok, TT * h + TT)
                c.link(dve.tensor_tensor(ot[:, :], ot[:, :], qs[:, :], ALU.mult))
                dve.wait_ge(g_ok, 2 * h + 2)
                dve.tensor_tensor(ot[:, :], ot[:, :], gt[:, :], ALU.mult).then_inc(on_ok, 1)
                dve.wait_ge(hi_ok, h + 1)
                c.mark(dve.tensor_tensor(g.ohTl[:, bass.ds(h, 1), :], ot[:, :].rearrange("p (a t) -> p a t", a=1),
                                         g.ohTh[:, bass.ds(h, 1), :].bitcast(F32), ALU.subtract))
                c.leave(HG)

        @block.tensor
        def _(pe):
            def project(h, r, base, cols):
                pe.wait_ge(wl_done, 4 * h + r + 1)
                for n, (col, m) in enumerate(cols):
                    for j in range(DK):
                        last = mm3(pe, bank(base + n, 0, m), wh[r % 2][:, j, :], wl[r % 2][:, j, :],
                                   g.uTh[:, j, col:col + m], g.uTl[:, j, col:col + m], j == 0, j == DK - 1)
                    last.then_inc(mm_done, 1)

            def head(h, first):
                if not first:
                    pe.wait_ge(a_ok, TT * h)
                    pe.wait_ge(o_ok, TT * h)
                project(h, 0, FB, pieces)
                if not first:
                    pe.wait_ge(s_ok, (4 * TT - 1) * h)
                project(h, 1, VB, pieces)
                pe.wait_ge(sig_f, 3 * h + 3)
                project(h, 2, QB, pieces[:2])
                pe.wait_ge(vt_ok, 3 * h + 3)
                project(h, 3, GB, pieces[:2])
                if not first:
                    pe.wait_ge(rt_ok, 2 * h)
                for n in range(2):
                    for t in range(4):
                        tt = 4 * n + t
                        last = pe.transpose(bank(6 + n, t * P, P), vt[:, tt * P:(tt + 1) * P], g.ident[:, :])
                    last.then_inc(vtr, 1)
                pe.transpose(g.ps[0:META, 2 * 512:2 * 512 + P], vt[:, SEQ:NT], g.ident[:, :]).then_inc(vtr, 1)
                pe.wait_ge(kd_ok, h + 1)
                pe.wait_ge(v_ok, 3 * h + 3)
                pe.transpose(g.ps[0:META, 2 * 512:2 * 512 + P], kd[:, SEQ:NT], g.ident[:, :]).then_inc(ktr, 1)
                pe.wait_ge(kdn_ok, 9 * h + 1)
                pe.matmul(bank(5, 0, P), kdm[:, :], v[0:META, TT, :], start=True, stop=True).then_inc(s0_mm, 1)
                pe.wait_ge(g_ok, 2 * h + 2)
                pe.wait_ge(q_ok, 2 * h + 2)

                def ahead(t):
                    if t >= 2:
                        pe.wait_ge(kdn_ok, 9 * h + t)
                        pe.wait_ge(a_ok, TT * h + t - 1)
                        pe.wait_ge(s_ok, (4 * TT - 1) * h + 4 * (t - 1))
                    pe.transpose(bank(TB + t % 2, 0, P), kd[:, t * P:(t + 1) * P], g.ident[:, :]).then_inc(ktr, 1)
                    pe.matmul(bank(AB + t % 2, 0, P), ks[:, t * P:(t + 1) * P], qs[:, t * P:(t + 1) * P],
                              start=True, stop=True).then_inc(a_mm, 1)
                    pe.wait_ge(kdn_ok, 9 * h + t + 2)
                    pe.wait_ge(vb_ok, 4 * (TT * h + t + 1))
                    pe.matmul(bank(KVB + t % 2), kdn[:, t % 2, :], vb[t % 2][:, :], start=True, stop=True).then_inc(kv_mm, 1)

                ahead(0)
                pe.wait_ge(s0_ok, h + 1)
                for t in range(TT):
                    if t + 1 < TT:
                        ahead(t + 1)
                    pe.wait_ge(a_ok, TT * h + t + 1)
                    if t >= 2:
                        pe.wait_ge(o_ok, TT * h + t - 1)
                    pe.matmul(bank(OB[t % 2], 0, P), v[:, t, :], at[:, t % 2, :], start=True, stop=False)
                    for ci in range(4):
                        n = 4 * t + ci
                        if n:
                            pe.wait_ge(s_ok, (4 * TT - 1) * h + n)
                        last = pe.matmul(bank(OB[t % 2], ci * CH, CH), S[:, n % 8, :], qd[:, n * CH:(n + 1) * CH],
                                         start=False, stop=ci == 3)
                    last.then_inc(o_mm, 1)
                pe.wait_ge(sq_ok, h + 1)
                for n in range(2):
                    pe.matmul(bank(TB + n), g.ones[:, :], d1[:, n * 512:(n + 1) * 512],
                              start=True, stop=True).then_inc(ms_mm, 1)

            head(0, True)
            with pe.Fori(1, HG) as h:
                head(h, False)


def phase_latents(nc, g):
    with ExitStack() as ph:
        sb = lambda n, s, d=F32: ph.enter_context(nc.sbuf_tensor(n, s, d))
        sem = semaphores(nc, ph)
        w = [sb(f"l_w{b}", [P, DK, P]) for b in range(2)]
        wh = [sb(f"l_wh{b}", [P, DK, P], F32R) for b in range(2)]
        wl = [sb(f"l_wl{b}", [P, DK, P], F32R) for b in range(2)]
        raw = sb("l_raw", [P, 5, NT])
        sq, rt = sb("l_sq", [P, NT]), sb("l_rt", [P, NT])
        gain = sb("l_gain", [P, 5])
        cst_in, zero = sem("l_cst_in"), sem("l_zero")
        w_in = [sem(f"l_w_in{b}") for b in range(2)]
        wh_done, wl_done, mm_done, raw_ok, kpe_ok = (sem("l_wh_done"), sem("l_wl_done"), sem("l_mm_done"),
                                                     sem("l_raw_ok"), sem("l_kpe_ok"))
        sq_ok, ms_mm, rt_ok, n_ok, hi_ok, lo_ok, dv = (sem("l_sq_ok"), sem("l_ms_mm"), sem("l_rt_ok"), sem("l_n_ok"),
                                                       sem("l_hi_ok"), sem("l_lo_ok"), sem("l_dv"))
        block = ph.enter_context(nc.Block())
        w_src = g.w_in[0].rearrange("(p j) n -> p j n", j=DK)
        bank = lambda i, a=0, n=512: g.ps[:, i * 512 + a:i * 512 + a + n]
        real, full = [(0, 512), (512, 512)], [(0, 512), (512, 512), (SEQ, META)]
        BLOCKS = [(C_CQ + i * P, P, real) for i in range(3)] + [(C_CKV + i * P, P, full) for i in range(2)] \
            + [(C_KPE - NOPE, QH, full)]
        NORMS = [(range(0, 3), SEQ, QL, g.cqh, g.cql, real), (range(3, 5), NT, KVL, g.ckh, g.ckl, full)]
        mm_before = [sum(len(b[2]) for b in BLOCKS[:n]) for n in range(7)]
        fbank = lambda n: 3 * (n % 2)

        @block.sync
        def _(sp):
            with nc.allow_non_contiguous_dma(reason="small vectors turned once"):
                sp.dma_start(gain[:, 0:3], g.q_norm[0].rearrange("(j p) -> p j", p=P)).then_inc(cst_in, 16)
                sp.dma_start(gain[:, 3:5], g.kv_norm[0].rearrange("(j p) -> p j", p=P)).then_inc(cst_in, 16)
            sp.dma_start(g.cos[NOPE:QH, :], g.rope_cos).then_inc(cst_in, 16)
            sp.dma_start(g.sin[NOPE:QH, :], g.rope_sin).then_inc(cst_in, 16)
            for n, (col, m, _) in enumerate(BLOCKS):
                if n >= 2:
                    sp.wait_ge(wl_done, n - 1)
                sp.dma_start(w[n % 2][:, :, 0:m], w_src[:, :, col:col + m]).then_inc(w_in[n % 2], 16)
            sp.wait_ge(cst_in, 64)

        @block.scalar
        def _(act):
            def split(n):
                if n >= 2:
                    act.wait_ge(mm_done, mm_before[n - 1])
                m = BLOCKS[n][1]
                act.wait_ge(w_in[n % 2], 16 * (n // 2) + 16)
                act.activation(wh[n % 2][:, :, 0:m], w[n % 2][:, :, 0:m], ACT.Copy).then_inc(wh_done, 1)

            split(0)
            split(1)
            for n in range(5):
                for p, (c, m) in enumerate(BLOCKS[n][2]):
                    act.wait_ge(mm_done, mm_before[n] + p + 1)
                    act.activation(raw[:, n, c:c + m], bank(fbank(n) + p, 0, m), ACT.Copy).then_inc(raw_ok, 1)
                if n + 2 < 6:
                    split(n + 2)
            done = 0
            for z, (js, width, size, _, _, cols) in enumerate(NORMS):
                for p, (c, m) in enumerate(cols):
                    act.wait_ge(ms_mm, done + p + 1)
                    act.activation(rt[:, c:c + m], bank([6, 7, 2][p], 0, m), ACT.Sqrt, scale=1.0 / size,
                                   bias=g.eps[:, :]).then_inc(rt_ok, 1)
                done += len(cols)
                for j in js:
                    act.wait_ge(n_ok, j + 1)
                    hi = NORMS[z][3]
                    act.activation(hi[:, j - js[0], 0:width], raw[:, j, 0:width], ACT.Copy).then_inc(hi_ok, 1)

        @block.vector
        def _(dve):
            v = Steps(dve, dv)

            def low(n):
                dve.wait_ge(wh_done, n + 1)
                m = BLOCKS[n][1]
                dve.tensor_tensor(wl[n % 2][:, :, 0:m], w[n % 2][:, :, 0:m], wh[n % 2][:, :, 0:m].bitcast(F32),
                                  ALU.subtract).then_inc(wl_done, 1)

            def squares(js, width, z):
                for j in js:
                    dve.wait_ge(raw_ok, mm_before[j + 1])
                    x = raw[:, j, 0:width]
                    if j == js[0]:
                        v.link(dve.tensor_tensor(sq[:, 0:width], x, x, ALU.mult))
                    else:
                        v.link(dve.tensor_tensor(rt[:, 0:width], x, x, ALU.mult))
                        ins = dve.tensor_tensor(sq[:, 0:width], sq[:, 0:width], rt[:, 0:width], ALU.add)
                        if j == js[-1]:
                            ins.then_inc(sq_ok, 1)
                        else:
                            v.link(ins)
                    if j + 2 < 6:
                        low(j + 2)

            def normed(z):
                js, width, _, hi, lo, cols = NORMS[z]
                dve.wait_ge(rt_ok, 2 if z == 0 else 5)
                v.link(dve.reciprocal(rt[:, 0:width], rt[:, 0:width]))
                for j in js:
                    dve.scalar_tensor_tensor(out=raw[:, j, 0:width], in0=raw[:, j, 0:width], scalar=gain[:, j:j + 1],
                                             in1=rt[:, 0:width], op0=ALU.mult, op1=ALU.mult).then_inc(n_ok, 1)
                for j in js:
                    dve.wait_ge(hi_ok, j + 1)
                    dve.tensor_tensor(lo[:, j - js[0], 0:width], raw[:, j, 0:width],
                                      hi[:, j - js[0], 0:width].bitcast(F32), ALU.subtract).then_inc(lo_ok, 1)

            low(0)
            low(1)
            dve.wait_ge(cst_in, 64)
            squares(range(0, 3), SEQ, 0)
            normed(0)
            squares(range(3, 5), NT, 1)
            normed(1)
            rows = slice(NOPE, QH)
            for p, (c, m) in enumerate(full):
                dve.wait_ge(mm_done, mm_before[5] + p + 1)
                b = g.ps[rows, (3 + p) * 512:(3 + p) * 512 + m]
                v.link(dve.stream_shuffle(out=sq[rows, c:c + m], in_=b, mask=SWAP))
                dve.tensor_tensor(g.kpe[rows, c:c + m], b, g.cos[rows, c:c + m], ALU.mult).then_inc(kpe_ok, 1)
            dve.wait_ge(kpe_ok, 3)
            v.link(dve.tensor_tensor(sq[rows, :], sq[rows, :], g.sin[rows, :], ALU.mult))
            v.link(dve.tensor_tensor(g.kpe[rows, :], g.kpe[rows, :], sq[rows, :], ALU.add))

        @block.tensor
        def _(pe):
            def project(n):
                pe.wait_ge(wl_done, n + 1)
                if n >= 2:
                    pe.wait_ge(raw_ok, mm_before[n - 1])
                m = BLOCKS[n][1]
                for p, (col, k) in enumerate(BLOCKS[n][2]):
                    for j in range(DK):
                        last = mm3(pe, g.ps[0:m, (fbank(n) + p) * 512:(fbank(n) + p) * 512 + k], wh[n % 2][:, j, 0:m],
                                   wl[n % 2][:, j, 0:m], g.uTh[:, j, col:col + k], g.uTl[:, j, col:col + k],
                                   j == 0, j == DK - 1)
                    last.then_inc(mm_done, 1)

            def sums(z, cols):
                pe.wait_ge(sq_ok, z + 1)
                for p, (c, m) in enumerate(cols):
                    pe.matmul(bank([6, 7, 2][p], 0, m), g.ones[:, :], sq[:, c:c + m], start=True, stop=True).then_inc(ms_mm, 1)

            for n in range(4):
                project(n)
            sums(0, real)
            project(4)
            pe.wait_ge(raw_ok, mm_before[4])
            project(5)
            pe.wait_ge(rt_ok, 2)
            pe.wait_ge(raw_ok, mm_before[5])
            sums(1, full)


def phase_heads(nc, g):
    with ExitStack() as ph:
        sb = lambda n, s, d=F32: ph.enter_context(nc.sbuf_tensor(n, s, d))
        sem = semaphores(nc, ph)
        wq = [sb(f"p_wq{b}", [P, 3, QH]) for b in range(2)]
        wkv = [sb(f"p_wkv{b}", [P, 2, P]) for b in range(2)]
        wqh = [sb(f"p_wqh{b}", [P, 3, QH], F32R) for b in range(2)]
        wql = [sb(f"p_wql{b}", [P, 3, QH], F32R) for b in range(2)]
        wkh = [sb(f"p_wkh{b}", [P, 2, P], F32R) for b in range(2)]
        wkl = [sb(f"p_wkl{b}", [P, 2, P], F32R) for b in range(2)]
        KVT = [sb(f"p_KVT{b}", [P, NT]) for b in range(2)]
        rot = sb("p_rot", [QH, SEQ])
        w_in = [sem(f"p_w_in{b}") for b in range(2)]
        k_out = [sem(f"p_k_out{b}") for b in range(2)]
        kpe_out = sem("p_kpe_out")
        wh_ok, wl_ok, q_mm, kv_mm = sem("p_wh_ok"), sem("p_wl_ok"), sem("p_q_mm"), sem("p_kv_mm")
        qn_ok, qp_ok, kvt_ok, v_tr, v_ok, dv = (sem("p_qn_ok"), sem("p_qp_ok"), sem("p_kvt_ok"), sem("p_v_tr"),
                                                sem("p_v_ok"), sem("p_dv"))
        block = ph.enter_context(nc.Block())
        bank = lambda i, a=0, n=512: g.ps[:, i * 512 + a:i * 512 + a + n]
        pieces = [(0, 512), (512, 512), (SEQ, META)]
        Q_BANK, KV_BANK, V_BANK = 0, 2, 5
        q_src = g.w_uq[0].rearrange("(j p) n -> p j n", p=P)
        kv_src = g.w_ukv[0].rearrange("(j p) n -> p j n", p=P)

        def each_head(eng, body):
            body(0, 0, 0)
            body(1, 0, 1)
            with eng.Fori(1, HEADS // 2 - 1) as n:
                for b in range(2):
                    body(2 * n + b, n, b)
            body(HEADS - 2, HEADS // 2 - 1, 0)
            body(HEADS - 1, HEADS // 2 - 1, 1)

        has = lambda h, d: not isinstance(h, int) or 0 <= h + d < HEADS

        @block.sync
        def _(sp):
            def load(h, b):
                sp.dma_start(wq[b][:, :, :], q_src[:, :, bass.ds(h * QH, QH)]).then_inc(w_in[b], 16)
                sp.dma_start(wkv[b][:, :, :], kv_src[:, :, bass.ds(h * P, P)]).then_inc(w_in[b], 16)

            load(0, 0)
            load(1, 1)
            with sp.Fori(0, HEADS) as h:
                sp.dma_start(g.KT[NOPE:QH, bass.ds(h, 1), :], g.kpe[NOPE:QH, :].rearrange("p (a t) -> p a t", a=1)
                             ).then_inc(kpe_out, 16)

            def body(h, n, b):
                if has(h, 2):
                    sp.wait_ge(wl_ok, 2 * h + 2)
                    load(h + 2, b)
                sp.wait_ge(kvt_ok, 3 * h + 3)
                sp.dma_start(g.KT[0:NOPE, bass.ds(h, 1), :], KVT[b][0:NOPE, :].rearrange("p (a t) -> p a t", a=1)
                             ).then_inc(k_out[b], 16)

            each_head(sp, body)
            sp.wait_ge(kpe_out, 16 * HEADS)
            for b in range(2):
                sp.wait_ge(k_out[b], 16 * (HEADS // 2))

        @block.scalar
        def _(act):
            def split(h, n, b):
                if has(h, -2):
                    act.wait_ge(kv_mm, 3 * h - 3)
                act.wait_ge(w_in[b], 32 * n + 32)
                act.activation(wqh[b][:, :, :], wq[b][:, :, :], ACT.Copy).then_inc(wh_ok, 1)
                act.activation(wkh[b][:, :, :], wkv[b][:, :, :], ACT.Copy).then_inc(wh_ok, 1)

            def values(h, n, b):
                cols = slice(0, VD) if b == 0 else slice(VD, VD + P)
                src = slice(NOPE, P) if b == 0 else slice(0, P)
                for x in range(2):
                    act.wait_ge(v_tr, 3 * h + x + 1)
                    settle(act, g)
                    act.activation(g.V[:, bass.ds(n, 1), 4 * x:4 * x + 4, cols].rearrange("p a t c -> p (a t) c"),
                                   bank(V_BANK + x).rearrange("p (t c) -> p t c", t=4)[:, :, src], ACT.Copy).then_inc(v_ok, 1)
                act.wait_ge(v_tr, 3 * h + 3)
                settle(act, g)
                act.activation(g.V[0:META, bass.ds(n, 1), TT, cols].rearrange("p a c -> p (a c)"),
                               g.ps[0:META, (V_BANK + 2) * 512 + src.start:(V_BANK + 2) * 512 + P],
                               ACT.Copy).then_inc(v_ok, 1)

            def body(h, n, b):
                if has(h, 1):
                    split(h + 1, n + b, 1 - b)
                for x in range(2):
                    act.wait_ge(q_mm, 2 * h + x + 1)
                    settle(act, g)
                    act.activation(g.QT[0:NOPE, bass.ds(h, 1), x * 512:(x + 1) * 512].rearrange("p a t -> p (a t)"),
                                   g.ps[0:NOPE, (Q_BANK + x) * 512:(Q_BANK + x + 1) * 512], ACT.Copy,
                                   scale=SCALE).then_inc(qn_ok, 1)
                if has(h, -1):
                    values(h - 1, n - 1 + b, 1 - b)
                if has(h, -2):
                    act.wait_ge(k_out[b], 16 * n)
                for x, (c, m) in enumerate(pieces):
                    act.wait_ge(kv_mm, 3 * h + x + 1)
                    act.activation(KVT[b][:, c:c + m], bank(KV_BANK + x, 0, m), ACT.Copy).then_inc(kvt_ok, 1)

            split(0, 0, 0)
            each_head(act, body)
            values(HEADS - 1, HEADS // 2 - 1, 1)

        @block.vector
        def _(dve):
            c = Steps(dve, dv)
            rows = slice(NOPE, QH)

            def low(h, b):
                for x, (raw, hi, lo) in enumerate([(wq, wqh, wql), (wkv, wkh, wkl)]):
                    dve.wait_ge(wh_ok, 2 * h + x + 1)
                    dve.tensor_tensor(lo[b][:, :, :], raw[b][:, :, :], hi[b][:, :, :].bitcast(F32),
                                      ALU.subtract).then_inc(wl_ok, 1)

            def body(h, n, b):
                if has(h, 1):
                    low(h + 1, 1 - b)
                for x in range(2):
                    dve.wait_ge(qn_ok, 2 * h + x + 1)
                    src = g.ps[rows, (Q_BANK + x) * 512:(Q_BANK + x + 1) * 512]
                    cols = slice(x * 512, (x + 1) * 512)
                    dst = g.QT[rows, bass.ds(h, 1), cols].rearrange("p a t -> p (a t)")
                    settle(dve, g)
                    c.mark(dve.stream_shuffle(out=rot[rows, cols], in_=src, mask=SWAP))
                    ins = dve.scalar_tensor_tensor(out=dst, in0=src, scalar=SCALE, in1=g.cos[rows, cols],
                                                   op0=ALU.mult, op1=ALU.mult)
                    if x == 0:
                        c.mark(ins)
                    else:
                        c.link(ins)
                dve.sem_inc(qp_ok, 1)
                c.link(dve.scalar_tensor_tensor(out=rot[rows, :], in0=rot[rows, :], scalar=SCALE, in1=g.sin[rows, 0:SEQ],
                                                op0=ALU.mult, op1=ALU.mult))
                dst = g.QT[rows, bass.ds(h, 1), :].rearrange("p a t -> p (a t)")
                c.link(dve.tensor_tensor(dst, dst, rot[rows, :], ALU.add))

            low(0, 0)
            per = 6
            body(0, 0, 0)
            body(1, 0, 1)
            with dve.Fori(1, HEADS // 2 - 1) as n:
                c.enter(n - 1, 2 * per)
                for b in range(2):
                    body(2 * n + b, n, b)
                c.leave(HEADS // 2 - 2)
            body(HEADS - 2, HEADS // 2 - 1, 0)
            body(HEADS - 1, HEADS // 2 - 1, 1)

        @block.tensor
        def _(pe):
            def values(h, b):
                pe.wait_ge(kvt_ok, 3 * h + 3)
                wait(pe, v_ok, 3 * h)
                for x in range(2):
                    for t in range(4):
                        last = pe.transpose(bank(V_BANK + x, t * P, P), KVT[b][:, (4 * x + t) * P:(4 * x + t + 1) * P], g.ident[:, :])
                    last.then_inc(v_tr, 1)
                pe.transpose(g.ps[0:META, (V_BANK + 2) * 512:(V_BANK + 2) * 512 + P], KVT[b][:, SEQ:NT], g.ident[:, :]).then_inc(v_tr, 1)

            def body(h, n, b):
                pe.wait_ge(wl_ok, 2 * h + 2)
                wait(pe, qn_ok, 2 * h)
                wait(pe, qp_ok, h)
                for x in range(2):
                    for j in range(3):
                        last = mm3(pe, g.ps[0:QH, (Q_BANK + x) * 512:(Q_BANK + x + 1) * 512], wqh[b][:, j, :], wql[b][:, j, :],
                                   g.cqh[:, j, x * 512:(x + 1) * 512], g.cql[:, j, x * 512:(x + 1) * 512], j == 0, j == 2)
                    last.then_inc(q_mm, 1)
                if has(h, -1):
                    values(h - 1, 1 - b)
                for x, (col, m) in enumerate(pieces):
                    for j in range(2):
                        last = mm3(pe, bank(KV_BANK + x, 0, m), wkh[b][:, j, :], wkl[b][:, j, :],
                                   g.ckh[:, j, col:col + m], g.ckl[:, j, col:col + m], j == 0, j == 1)
                    last.then_inc(kv_mm, 1)

            each_head(pe, body)
            values(HEADS - 1, 1)


def phase_attention(nc, g):
    with ExitStack() as ph:
        sb = lambda n, s, d=F32: ph.enter_context(nc.sbuf_tensor(n, s, d))
        sem = semaphores(nc, ph)
        Q = [sb(f"t_Q{b}", [QH, SEQ]) for b in range(2)]
        V = [sb("t_V0", [P, TT + 1, VD]), sb("t_V1", [P, TT + 1, P])]
        pr = [sb(f"t_p{b}", [P, NT]) for b in range(2)]
        PT = [sb(f"t_PT{b}", [P, TT + 1, P]) for b in range(2)]
        mask = sb("t_mask", [P, P])
        diag = [sb(f"t_diag{b}", [P, P]) for b in range(2)]
        negmax, total, inv = sb("t_negmax", [P, 2]), sb("t_total", [P, 2]), sb("t_inv", [P, 2])
        cst = sem("t_cst")
        q_in = [sem(f"t_q_in{b}") for b in range(2)]
        v_in = [sem(f"t_v_in{b}") for b in range(2)]
        s_mm, mx_ok, exp_ok, dg_ok, p_tr, pa_ok, pd_ok, o_mm, oh_ok, ol_ok, dv = (
            sem("t_s_mm"), sem("t_mx_ok"), sem("t_exp_ok"), sem("t_dg_ok"), sem("t_p_tr"), sem("t_pa_ok"), sem("t_pd_ok"),
            sem("t_o_mm"), sem("t_oh_ok"), sem("t_ol_ok"), sem("t_dv"))
        block = ph.enter_context(nc.Block())
        bank = lambda i, a=0, n=512: g.ps[:, i * 512 + a:i * 512 + a + n]
        tiles = lambda i: list(range(i + 1)) + [TT]
        groups = lambda i: [tiles(i)[a:a + 4] for a in range(0, i + 2, 4)]
        before = [sum(len(groups(m)) for m in range(i)) for i in range(TT + 1)]
        NG = before[TT]
        assert NG % 2 == 0
        HALF = NG // 2
        sbank = lambda i: 3 * (i % 2)
        obank = lambda i: 5 if i < TT // 2 else 2
        orows = lambda b: slice(VD * b, VD * b + VD)

        def heads(eng, body):
            with eng.Fori(0, HEADS // 2 - 1) as n:
                for b in range(2):
                    body(2 * n + b, n, b, True)
            body(HEADS - 2, HEADS // 2 - 1, 0, True)
            body(HEADS - 1, HEADS // 2 - 1, 1, False)

        def taken(i, grp, b):
            real = [t for t in grp if t != TT]
            out = []
            if real:
                out.append((PT[i % 2][:, real[0]:real[0] + len(real), :],
                            g.ps[:, b * 512:b * 512 + len(real) * P].rearrange("p (t c) -> p t c", c=P)))
            if TT in grp:
                at = b * 512 + len(real) * P
                out.append((PT[i % 2][0:META, TT, :], g.ps[0:META, at:at + P]))
            return out

        @block.sync
        def _(sp):
            def load_q(h, b):
                sp.dma_start(Q[b][:, :], g.QT[:, bass.ds(h, 1), :].rearrange("p a t -> p (a t)")).then_inc(q_in[b], 16)

            def load_v(n, b):
                cols = slice(0, VD) if b == 0 else slice(VD, VD + P)
                sp.dma_start(V[b][:, 0:TT, :], g.V[:, bass.ds(n, 1), 0:TT, cols].rearrange("p a t c -> p (a t) c")
                             ).then_inc(v_in[b], 16)
                sp.dma_start(V[b][0:META, TT, :], g.V[0:META, bass.ds(n, 1), TT, cols].rearrange("p a c -> p (a c)")
                             ).then_inc(v_in[b], 16)

            for b in range(2):
                load_q(b, b)
                load_v(0, b)
            with sp.Fori(1, HEADS // 2) as n:
                for b in range(2):
                    sp.wait_ge(s_mm, TT * (2 * n + b - 1))
                    load_q(2 * n + b, b)
                    sp.wait_ge(o_mm, 2 * (2 * n + b - 1))
                    load_v(n, b)

        @block.gpsimd
        def _(pool):
            pool.memset(mask[:, :], 0.0).then_inc(cst, 1)
            pool.wait_ge(cst, 1)
            pool.affine_select(out=mask[:, :], in_=mask[:, :], compare_op=ALU.is_ge, fill=-1e30, base=0,
                               pattern=[[-1, P]], channel_multiplier=1).then_inc(cst, 1)

        @block.scalar
        def _(act):
            def expo(h, i):
                act.wait_ge(mx_ok, TT * h + i + 1)
                s, n = i % 2, META + P * (i + 1)
                act.activation(pr[s][:, 0:n], g.ps[:, sbank(i) * 512:sbank(i) * 512 + n], ACT.Exp,
                               bias=negmax[:, s:s + 1], accum_out=total[:, s:s + 1]).then_inc(exp_ok, 1)

            def copies(h, i, gi):
                n = before[i] + gi
                if n % 2 == 0:
                    act.wait_ge(p_tr, NG * h + n + 1)
                    for dst, src in taken(i, groups(i)[gi], 6):
                        ins = act.activation(dst, src, ACT.Copy)
                    ins.then_inc(pa_ok, 1)

            def body(h, n, b, nxt):
                for i in range(TT):
                    copies(h, i, 0)
                    if i + 1 < TT:
                        expo(h, i + 1)
                    elif nxt:
                        expo(h + 1, 0)
                    for gi in range(1, len(groups(i))):
                        copies(h, i, gi)
                    if i % 4 == 3:
                        act.wait_ge(o_mm, 2 * h + i // 4 + 1)
                        settle(act, g)
                        act.activation(g.omTh[orows(b), bass.ds(n, 1), (i - 3) * P:(i + 1) * P].rearrange("p a t -> p (a t)"),
                                       g.ps[orows(b), obank(i) * 512:obank(i) * 512 + 512], ACT.Copy).then_inc(oh_ok, 1)

            expo(0, 0)
            heads(act, body)

        @block.vector
        def _(dve):
            c = Steps(dve, dv)

            def stats(h, i):
                s, n = i % 2, META + P * (i + 1)
                dve.wait_ge(s_mm, TT * h + i + 1)
                d = g.ps[:, sbank(i) * 512 + P * i:sbank(i) * 512 + P * (i + 1)]
                c.link(dve.tensor_tensor(d, d, mask[:, :], ALU.add))
                dve.tensor_reduce(out=negmax[:, s:s + 1], in_=g.ps[:, sbank(i) * 512:sbank(i) * 512 + n], axis=AX.X,
                                  op=ALU.max, negate=True).then_inc(mx_ok, 1)

            def scaling(h, i):
                s = i % 2
                dve.wait_ge(exp_ok, TT * h + i + 1)
                c.link(dve.reciprocal(inv[:, s:s + 1], total[:, s:s + 1]))
                dve.tensor_scalar(diag[s][:, :], g.ident[:, :], inv[:, s:s + 1], None, ALU.mult).then_inc(dg_ok, 1)

            def body(h, n, b, nxt):
                for i in range(TT):
                    ahead = (h, i + 1) if i + 1 < TT else (h + 1, 0)
                    more = i + 1 < TT or nxt
                    if more:
                        stats(*ahead)
                    for gi, grp in enumerate(groups(i)):
                        m = before[i] + gi
                        if m % 2 == 1:
                            dve.wait_ge(p_tr, NG * h + m + 1)
                            for dst, src in taken(i, grp, 7):
                                ins = dve.tensor_copy(dst, src)
                            ins.then_inc(pd_ok, 1)
                    if more:
                        scaling(*ahead)
                    if i % 4 == 3:
                        dve.wait_ge(oh_ok, 2 * h + i // 4 + 1)
                        hi = g.omTh[orows(b), bass.ds(n, 1), (i - 3) * P:(i + 1) * P].rearrange("p a t -> p (a t)")
                        lo = g.omTl[orows(b), bass.ds(n, 1), (i - 3) * P:(i + 1) * P].rearrange("p a t -> p (a t)")
                        dve.tensor_tensor(lo, g.ps[orows(b), obank(i) * 512:obank(i) * 512 + 512], hi.bitcast(F32),
                                          ALU.subtract).then_inc(ol_ok, 1)

            dve.wait_ge(cst, 2)
            stats(0, 0)
            scaling(0, 0)
            with dve.Fori(0, HEADS // 2 - 1) as n:
                c.enter(n, 2 * 2 * TT)
                for b in range(2):
                    body(2 * n + b, n, b, True)
                c.leave(HEADS // 2 - 1)
            body(HEADS - 2, HEADS // 2 - 1, 0, True)
            body(HEADS - 1, HEADS // 2 - 1, 1, False)

        @block.tensor
        def _(pe):
            def scores(h, n, b, i):
                if i == 0:
                    pe.wait_ge(q_in[b], 16 * n + 16)
                if i == TT - 1:
                    pe.wait_ge(ol_ok, 2 * h + 1)
                base = sbank(i) * 512
                q = Q[b][:, i * P:(i + 1) * P]
                m = P * (i + 1)
                key = lambda c, k: g.KT[:, bass.ds(h, 1), c:c + k].rearrange("p a t -> p (a t)")
                for c in range(0, m, 512):
                    k = min(512, m - c)
                    pe.matmul(g.ps[:, base + c:base + c + k], q, key(c, k), start=True, stop=True)
                pe.matmul(g.ps[:, base + m:base + m + META], q, key(SEQ, META), start=True, stop=True).then_inc(s_mm, 1)

            def taken_by(h, m):
                half = m // 2 + 1
                wait(pe, pa_ok if m % 2 == 0 else pd_ok, HALF * h + half)

            def body(h, n, b, nxt):
                for i in range(TT):
                    s, gs = i % 2, groups(i)
                    pe.wait_ge(dg_ok, TT * h + i + 1)
                    if i == 0:
                        pe.wait_ge(v_in[b], 32 * n + 32)
                        pe.wait_ge(exp_ok, TT * h + 1)

                    def weighted(gi):
                        taken_by(h, before[i] + gi)
                        for t in gs[gi]:
                            k = META if t == TT else P
                            ins = pe.matmul(g.ps[0:VD + VD * b, obank(i) * 512 + (i % 4) * P:obank(i) * 512 + (i % 4 + 1) * P],
                                            V[b][0:k, t, :], PT[s][0:k, t, :], start=t == 0, stop=t == TT)
                        return ins

                    for gi, grp in enumerate(gs):
                        m = before[i] + gi
                        taken_by(h, m - 2)
                        for x, t in enumerate(grp):
                            if t == TT:
                                last = pe.matmul(g.ps[0:META, (6 + m % 2) * 512 + x * P:(6 + m % 2) * 512 + (x + 1) * P],
                                                 pr[s][:, P * (i + 1):P * (i + 1) + META], diag[s][:, :], start=True, stop=True)
                            else:
                                last = pe.matmul(bank(6 + m % 2, x * P, P), pr[s][:, t * P:(t + 1) * P], diag[s][:, :],
                                                 start=True, stop=True)
                        last.then_inc(p_tr, 1)
                        if gi >= 1:
                            if gi == 1 and i == 4:
                                wait(pe, ol_ok, 2 * h)
                            weighted(gi - 1)
                    if i + 2 < TT:
                        scores(h, n, b, i + 2)
                    elif nxt:
                        scores(h + 1, n + b, 1 - b, i + 2 - TT)
                    ins = weighted(len(gs) - 1)
                    if i % 4 == 3:
                        ins.then_inc(o_mm, 1)

            pe.wait_ge(cst, 2)
            scores(0, 0, 0, 0)
            scores(0, 0, 0, 1)
            body(0, 0, 0, True)
            body(1, 0, 1, True)
            with pe.Fori(1, HEADS // 2 - 1) as n:
                for b in range(2):
                    body(2 * n + b, n, b, True)
            body(HEADS - 2, HEADS // 2 - 1, 0, True)
            body(HEADS - 1, HEADS // 2 - 1, 1, False)


def expert_loaders(g):
    up = [a[0].rearrange("e (p j) f -> p e j f", j=DK) for a in (g.w1, g.w3)]
    down = g.w2[0].rearrange("e (p j) n -> p e j n", j=2)

    def load_up(eng, e, b):
        for r in range(2):
            eng.dma_start(g.r13[b][:, r, :, :], up[r][:, bass.ds(e, 1), :, :].rearrange("p a j f -> p (a j) f")
                          ).then_inc(g.w_up_in[b], 16)

    def load_down(eng, e, b):
        eng.dma_start(g.r2[b][:, :, :], down[:, bass.ds(e, 1), :, :].rearrange("p a j n -> p (a j) n")
                      ).then_inc(g.w_down_in[b], 16)

    return load_up, load_down


def phase_merge(nc, g):
    with ExitStack() as ph:
        sb = lambda n, s, d=F32: ph.enter_context(nc.sbuf_tensor(n, s, d))
        sem = semaphores(nc, ph)
        w = [sb(f"e_w{b}", [P, 2, 4, P]) for b in range(2)]
        wh = [sb(f"e_wh{b}", [P, 2, 4, P], F32R) for b in range(2)]
        wl = [sb(f"e_wl{b}", [P, 2, 4, P], F32R) for b in range(2)]
        gate = [sb(f"e_gate{b}", [P, 2, SEQ]) for b in range(2)]
        m = [sb(f"e_m{b}", [P, SEQ]) for b in range(2)]
        w_in = [sem(f"e_w_in{b}") for b in range(2)]
        gate_in = [sem(f"e_gate_in{b}") for b in range(2)]
        stored = [sem(f"e_stored{b}") for b in range(2)]
        wh_ok, wl_ok, mm_ok, m_ok, dv = sem("e_wh_ok"), sem("e_wl_ok"), sem("e_mm_ok"), sem("e_m_ok"), sem("e_dv")
        block = ph.enter_context(nc.Block())
        bank = lambda i: g.ps[:, i * 512:(i + 1) * 512]
        br = [a[0].rearrange("(j p) n -> p j n", p=P) for a in (g.w_br_mla, g.w_br_hgrn)]

        @block.sync
        def _(sp):
            def load(n, b):
                for r in range(2):
                    sp.dma_start(w[b][:, r, :, :], br[r][:, :, bass.ds(n * P, P)]).then_inc(w_in[b], 16)
                    sp.dma_start(gate[b][:, r, :], g.gates[bass.ds(n * P + r * D, P), :]).then_inc(gate_in[b], 16)

            def store(n, b):
                sp.wait_ge(m_ok, n + 1)
                sp.dma_start(g.merged[bass.ds(n * P, P), :], m[b][:, :]).then_inc(stored[b], 16)

            load(0, 0)
            load(1, 1)
            with sp.Fori(0, DK // 2 - 1) as i:
                for b in range(2):
                    store(2 * i + b, b)
                    load(2 * i + b + 2, b)
            for b in range(2):
                store(DK - 2 + b, b)
                sp.wait_ge(stored[b], 16 * (DK // 2))

        @block.scalar
        def _(act):
            for b in range(2):
                act.wait_ge(w_in[b], 32)
                act.activation(wh[b][:, :, :, :], w[b][:, :, :, :], ACT.Copy).then_inc(wh_ok, 1)
            with act.Fori(1, DK // 2) as i:
                for b in range(2):
                    act.wait_ge(mm_ok, 4 * (2 * i + b - 1))
                    act.wait_ge(w_in[b], 32 * i + 32)
                    act.activation(wh[b][:, :, :, :], w[b][:, :, :, :], ACT.Copy).then_inc(wh_ok, 1)

        @block.vector
        def _(dve):
            c = Steps(dve, dv)

            def low(n, b):
                dve.wait_ge(wh_ok, n + 1)
                dve.tensor_tensor(wl[b][:, :, :, :], w[b][:, :, :, :], wh[b][:, :, :, :].bitcast(F32),
                                  ALU.subtract).then_inc(wl_ok, 1)

            def merge(n, b, turn, first):
                dve.wait_ge(gate_in[b], 32 * turn + 32)
                if not first:
                    dve.wait_ge(stored[b], 16 * turn)
                for r in range(2):
                    for q in range(2):
                        dve.wait_ge(mm_ok, 4 * n + 2 * r + q + 1)
                        cols = slice(q * 512, (q + 1) * 512)
                        c.mark(dve.tensor_tensor((m[b] if r == 0 else gate[b][:, 1, :])[:, cols], gate[b][:, r, cols],
                                                 bank(4 * b + 2 * r + q), ALU.mult))
                dve.wait_ge(dv, c.now())
                dve.tensor_tensor(m[b][:, :], m[b][:, :], gate[b][:, 1, :], ALU.add).then_inc(m_ok, 1)

            low(0, 0)
            low(1, 1)
            for b in range(2):
                merge(b, b, 0, True)
            with dve.Fori(1, DK // 2) as i:
                c.outer, c.per, c.base, c.k = 0, 8, i * 8, 0
                for b in range(2):
                    low(2 * i + b, b)
                for b in range(2):
                    merge(2 * i + b, b, i, False)

        @block.tensor
        def _(pe):
            def products(n, b):
                pe.wait_ge(wl_ok, n + 1)
                for r, (oh, ol) in enumerate([(g.omTh, g.omTl), (g.ohTh, g.ohTl)]):
                    for q in range(2):
                        cols = slice(q * 512, (q + 1) * 512)
                        for j in range(4):
                            last = mm3(pe, bank(4 * b + 2 * r + q), wh[b][:, r, j, :], wl[b][:, r, j, :],
                                       oh[:, j, cols], ol[:, j, cols], j == 0, j == 3)
                        last.then_inc(mm_ok, 1)

            for b in range(2):
                products(b, b)
            with pe.Fori(1, DK // 2) as i:
                for b in range(2):
                    pe.wait_ge(m_ok, 2 * i + b - 1)
                    products(2 * i + b, b)


def phase_output(nc, g):
    with ExitStack() as ph:
        sb = lambda n, s, d=F32: ph.enter_context(nc.sbuf_tensor(n, s, d))
        sem = semaphores(nc, ph)
        w = [sb(f"f_w{b}", [P, 2, D]) for b in range(2)]
        woh, wol = sb("f_woh", [P, DK, D], F32R), sb("f_wol", [P, DK, D], F32R)
        m = [sb(f"f_m{b}", [P, DK, P]) for b in range(2)]
        mh = [sb(f"f_mh{b}", [P, DK, P], F32R) for b in range(2)]
        ml = [sb(f"f_ml{b}", [P, DK, P], F32R) for b in range(2)]
        x = [sb(f"f_x{b}", [P, D]) for b in range(2)]
        u = [sb(f"f_u{b}", [P, D]) for b in range(2)]
        junk, gain, uT = sb("f_junk", [P, D]), sb("f_gain", [P, D]), sb("f_uT", [P, DK, P])
        R = GROUPS + EXPERTS
        wr, br = sb("f_wr", [P, DK, R]), sb("f_br", [P, R])
        st = sb("f_stat", [P, 4])
        lg, top, idx, ex8, oh8, sel, es = (sb("f_lg", [P, R]), sb("f_top", [P, 2, 8]), sb("f_idx", [P, 2, 8], U32),
                                           sb("f_ex8", [P, 8]), sb("f_oh8", [P, 8]), sb("f_sel", [P, 8, 8]), sb("f_es", [P, 8]))
        sc = sb("f_sc", [P, 16])
        M = [sb(f"f_M{b}", [P, 3, EXPERTS]) for b in range(2)]
        Mcum, R2, tmp = sb("f_Mcum", [P, EXPERTS]), sb("f_R2", [P, EXPERTS]), sb("f_tmp", [P, EXPERTS])
        slot = [sb(f"f_slot{b}", [P, 2], I32) for b in range(2)]
        slotf = sb("f_slotf", [P, 2])
        rec = [sb(f"f_rec{b}", [P, 2, ROWS]) for b in range(2)]
        io8, io64, off64, tok, upper = (sb("f_io8", [P, 8]), sb("f_io64", [P, EXPERTS]), sb("f_off64", [P, EXPERTS]),
                                        sb("f_tok", [P, 1]), sb("f_upper", [P, P]))
        fill = sb("f_fill", [P, EXPERTS * SLOTS * ROWS // P])
        rec_z = sem("f_rec_z")
        cst_in, cst, filled, wh_ok, wl_ok = sem("f_cst_in"), sem("f_cst"), sem("f_filled"), sem("f_wh_ok"), sem("f_wl_ok")
        w_in = [sem(f"f_w_in{b}") for b in range(2)]
        m_in = [sem(f"f_m_in{b}") for b in range(2)]
        x_in = [sem(f"f_x_in{b}") for b in range(2)]
        h_out = [sem(f"f_h_out{b}") for b in range(2)]
        u_out = [sem(f"f_u_out{b}") for b in range(2)]
        rec_out = sem("f_rec_out")
        mh_ok, ml_ok, w_mm, h_ok, ss_ok, rt_ok, u_ok = (sem("f_mh_ok"), sem("f_ml_ok"), sem("f_w_mm"), sem("f_h_ok"),
                                                        sem("f_ss_ok"), sem("f_rt_ok"), sem("f_u_ok"))
        u_tr, uT_ok, lg_mm, lg_ok, eg_ok, d_ok, ed_ok, M_ok, rk_mm, cum_ok, dv = (
            sem("f_u_tr"), sem("f_uT_ok"), sem("f_lg_mm"), sem("f_lg_ok"), sem("f_eg_ok"), sem("f_d_ok"), sem("f_ed_ok"),
            sem("f_M_ok"), sem("f_rk_mm"), sem("f_cum_ok"), sem("f_dv"))
        block = ph.enter_context(nc.Block())
        bank = lambda i, a=0, n=512: g.ps[:, i * 512 + a:i * 512 + a + n]
        w_src = g.w_out[0].rearrange("(j p) n -> p j n", p=P)
        m_src = g.merged.rearrange("(j p) t -> p j t", p=P)

        def tiles(body, eng):
            body(0, 0, True, False)
            with eng.Fori(0, TT // 2 - 1) as i:
                for b in (1, 0):
                    body(2 * i + 2 - b, b, False, False, i)
            body(TT - 1, 1, False, True)

        def turn(t, b, i):
            if isinstance(t, int):
                return t // 2
            return i if b else i + 1

        @block.sync
        def _(sp):
            sp.dma_start(gain[:, :], g.ffn_norm[0:1, :].to_broadcast([P, D])).then_inc(cst_in, 16)
            sp.dma_start(wr[:, :, 0:GROUPS], g.w_group[0].rearrange("(j p) n -> p j n", p=P)).then_inc(cst_in, 16)
            sp.dma_start(wr[:, :, GROUPS:R], g.w_route[0].rearrange("(j p) n -> p j n", p=P)).then_inc(cst_in, 16)
            sp.dma_start(br[:, 0:GROUPS], g.b_group[0:1, :].to_broadcast([P, GROUPS])).then_inc(cst_in, 16)
            sp.dma_start(br[:, GROUPS:R], g.b_route[0:1, :].to_broadcast([P, EXPERTS])).then_inc(cst_in, 16)
            for n in range(2):
                sp.dma_start(w[n][:, :, :], w_src[:, 2 * n:2 * n + 2, :]).then_inc(w_in[n], 16)
            for b in range(2):
                sp.dma_start(m[b][:, :, :], m_src[:, :, b * P:(b + 1) * P]).then_inc(m_in[b], 16)
                sp.dma_start(x[b][:, :], g.x[0, b * P:(b + 1) * P, :]).then_inc(x_in[b], 16)
            for n in range(2, 4):
                sp.wait_ge(wl_ok, n - 1)
                sp.dma_start(w[n % 2][:, :, :], w_src[:, 2 * n:2 * n + 2, :]).then_inc(w_in[n % 2], 16)
            sp.wait_ge(cst, 8)
            sp.dma_start(g.table.rearrange("(p s) r -> p (s r)", p=P), fill[:, :]).then_inc(filled, 16)
            for b in range(2):
                g.load_up(sp, b, b)
                g.load_down(sp, b, b)

            def body(t, b, first, last, i=None):
                n = turn(t, b, i)
                sp.wait_ge(h_ok, t + 1)
                sp.dma_start(g.h[bass.ds(t * P, P), :], x[b][:, :]).then_inc(h_out[b], 16)
                sp.wait_ge(u_ok, t + 1)
                sp.dma_start(g.u2[bass.ds(t * P, P), :], u[b][:, :]).then_inc(u_out[b], 16)

            def loads(t, b, i):
                sp.wait_ge(ml_ok, t - 1)
                sp.dma_start(m[b][:, :, :], m_src[:, :, bass.ds(t * P, P)]).then_inc(m_in[b], 16)
                sp.wait_ge(h_out[b], 16 * (i + 1))
                sp.dma_start(x[b][:, :], g.x[0, bass.ds(t * P, P), :]).then_inc(x_in[b], 16)

            with sp.Fori(0, TT // 2 - 1) as i:
                for b in range(2):
                    body(2 * i + b, b, False, False, i if b else i)
                    loads(2 * i + b + 2, b, i)
            for b in range(2):
                body(TT - 2 + b, b, False, True)
                sp.wait_ge(h_out[b], 16 * (TT // 2))
                sp.wait_ge(u_out[b], 16 * (TT // 2 + b))

        @block.gpsimd
        def _(pool):
            pool.sem_inc(u_out[1], 16)
            pool.iota(io8[:, :], pattern=[[1, 8]], base=0, channel_multiplier=0,
                      allow_small_or_imprecise_dtypes=True).then_inc(cst, 1)
            pool.iota(io64[:, :], pattern=[[1, EXPERTS]], base=0, channel_multiplier=0,
                      allow_small_or_imprecise_dtypes=True).then_inc(cst, 1)
            pool.iota(off64[:, :], pattern=[[SLOTS, EXPERTS]], base=0, channel_multiplier=0,
                      allow_small_or_imprecise_dtypes=True).then_inc(cst, 1)
            pool.iota(tok[:, :], pattern=[[0, 1]], base=0, channel_multiplier=1,
                      allow_small_or_imprecise_dtypes=True).then_inc(cst, 1)
            pool.memset(Mcum[:, :], 0.0).then_inc(cst, 1)
            pool.affine_select(out=upper[:, :], in_=g.ones[:, :], compare_op=ALU.is_gt, fill=0.0, base=0,
                               pattern=[[1, P]], channel_multiplier=-1).then_inc(cst, 1)
            for b in range(2):
                pool.memset(rec[b][:, :, :], 0.0).then_inc(rec_z, 1)
            pool.memset(fill[:, 0:SLOTS], SKIP).then_inc(cst, 1)
            pool.memset(fill[:, SLOTS:], SKIP).then_inc(cst, 1)

            pool.wait_ge(filled, 16)
            with pool.Fori(0, TT // 2) as i:
                for b in range(2):
                    pool.wait_ge(cum_ok, 2 * i + b + 1)
                    settle(pool, g)
                    for c in range(2):
                        pool.indirect_dma_start(out=g.table, out_offset=bass.IndirectOffsetOnAxis(ap=slot[b][:, c:c + 1], axis=0),
                                                in_=rec[b][:, c, :], in_offset=None).then_inc(rec_out, 16)
            pool.wait_ge(rec_out, 32 * TT)

        @block.scalar
        def _(act):
            def split(t, b, n):
                act.wait_ge(m_in[b], 16 * n + 16)
                act.activation(mh[b][:, :, :], m[b][:, :, :], ACT.Copy).then_inc(mh_ok, 1)

            def body(t, b, first, last, i=None):
                if not last:
                    nxt = turn(t + 1, 1 - b, i) if isinstance(t, int) else (i + 1)
                    if not first:
                        act.wait_ge(w_mm, t)
                    split(t + 1, 1 - b, nxt)
                act.wait_ge(h_ok, t + 1)
                act.activation(junk[:, :], x[b][:, :], ACT.Square, accum_out=st[:, b:b + 1]).then_inc(ss_ok, 1)
                act.wait_ge(ss_ok, t + 1)
                act.activation(st[:, 2 + b:3 + b], st[:, b:b + 1], ACT.Sqrt, scale=1.0 / D, bias=g.eps[:, :]).then_inc(rt_ok, 1)
                for q in range(2):
                    act.wait_ge(u_tr, 2 * t + q + 1)
                    act.activation(uT[:, 4 * q:4 * q + 4, :], bank(4 + q).rearrange("p (j t) -> p j t", j=4),
                                   ACT.Copy).then_inc(uT_ok, 1)
                act.wait_ge(lg_ok, t + 1)
                act.activation(ex8[:, :], lg[:, 0:8], ACT.Exp, bias=sc[:, 0:1], accum_out=sc[:, 1:2]).then_inc(eg_ok, 1)
                act.wait_ge(d_ok, t + 1)
                act.activation(sc[:, 7:8], sc[:, 6:7], ACT.Exp).then_inc(ed_ok, 1)

            for n in range(4):
                act.wait_ge(w_in[n % 2], 16 * (n // 2) + 16)
                act.activation(woh[:, 2 * n:2 * n + 2, :], w[n % 2][:, :, :], ACT.Copy).then_inc(wh_ok, 1)
            split(0, 0, 0)
            tiles(body, act)

        @block.vector
        def _(dve):
            c = Steps(dve, dv)

            def low(t, b):
                dve.wait_ge(mh_ok, t + 1)
                dve.tensor_tensor(ml[b][:, :, :], m[b][:, :, :], mh[b][:, :, :].bitcast(F32), ALU.subtract).then_inc(ml_ok, 1)

            def choose(t, b):
                dve.wait_ge(lg_mm, t + 1)
                c.link(dve.tensor_tensor(lg[:, :], bank(6, 0, R), br[:, :], ALU.add))
                settle(dve, g)
                c.link(dve.max(out=top[:, 0, :], in_=lg[:, 0:8]))
                dve.tensor_scalar(sc[:, 0:1], top[:, 0, 0:1], -1.0, None, ALU.mult).then_inc(lg_ok, 1)
                settle(dve, g)
                c.link(dve.max_index(out=idx[:, 0, :], in_max=top[:, 0, :], in_values=lg[:, 0:8]))
                c.link(dve.tensor_copy(sc[:, 2:3], idx[:, 0, 0:1]))
                c.link(dve.tensor_scalar(oh8[:, :], io8[:, :], sc[:, 2:3], None, ALU.is_equal))
                c.link(dve.tensor_tensor(sel[:, :, :], lg[:, 8:R].rearrange("p (g e) -> p g e", g=8),
                                         oh8[:, :].rearrange("p (g a) -> p g a", a=1).to_broadcast([P, 8, 8]), ALU.mult))
                c.link(dve.tensor_reduce(out=es[:, :], in_=sel[:, :, :].rearrange("p g e -> p e g"), axis=AX.X, op=ALU.add))
                settle(dve, g)
                c.link(dve.max(out=top[:, 1, :], in_=es[:, :]))
                dve.tensor_tensor(sc[:, 6:7], top[:, 1, 1:2], top[:, 1, 0:1], ALU.subtract).then_inc(d_ok, 1)
                settle(dve, g)
                c.link(dve.max_index(out=idx[:, 1, :], in_max=top[:, 1, :], in_values=es[:, :]))
                c.link(dve.tensor_copy(sc[:, 4:6], idx[:, 1, 0:2]))
                c.link(dve.tensor_scalar(sc[:, 3:4], sc[:, 2:3], 8.0, None, ALU.mult))
                c.link(dve.tensor_scalar(sc[:, 4:6], sc[:, 4:6], sc[:, 3:4], None, ALU.add))
                for k in range(2):
                    c.link(dve.tensor_scalar(M[b][:, k, :], io64[:, :], sc[:, 4 + k:5 + k], None, ALU.is_equal))
                dve.tensor_tensor(M[b][:, 2, :], M[b][:, 0, :], M[b][:, 1, :], ALU.add).then_inc(M_ok, 1)
                dve.wait_ge(eg_ok, t + 1)
                c.link(dve.reciprocal(sc[:, 8:9], sc[:, 1:2]))
                dve.wait_ge(ed_ok, t + 1)
                c.link(dve.tensor_scalar(sc[:, 9:10], sc[:, 7:8], 1.0, None, ALU.add))
                c.link(dve.reciprocal(sc[:, 9:10], sc[:, 9:10]))
                c.link(dve.tensor_tensor(sc[:, 10:11], sc[:, 8:9], sc[:, 9:10], ALU.mult))
                c.link(dve.tensor_tensor(sc[:, 11:12], sc[:, 10:11], sc[:, 7:8], ALU.mult))

            def place(t, b, n, first):
                dve.wait_ge(rk_mm, t + 1)
                c.link(dve.tensor_tensor(R2[:, :], bank(7, 0, EXPERTS), off64[:, :], ALU.add))
                for k in range(2):
                    c.link(dve.scalar_tensor_tensor(out=tmp[:, :], in0=M[b][:, k, :], scalar=1.0, in1=R2[:, :], op0=ALU.mult,
                                                    op1=ALU.mult, accum_out=slotf[:, k:k + 1]))
                if not first:
                    dve.wait_ge(rec_out, 32 * t)
                c.link(dve.tensor_copy(slot[b][:, :], slotf[:, :]))
                for k in range(2):
                    c.link(dve.tensor_scalar(rec[b][:, k, 0:1], tok[:, :], 2.0, float(k), ALU.mult, ALU.add))
                    c.link(dve.tensor_copy(rec[b][:, k, 1:2], sc[:, 10 + k:11 + k]))
                    c.link(dve.tensor_copy(rec[b][:, k, 2:3], tok[:, :]))
                c.link(dve.tensor_scalar(tok[:, :], tok[:, :], float(P), None, ALU.add))
                dve.tensor_tensor(Mcum[:, :], Mcum[:, :], M[b][:, 2, :], ALU.add).then_inc(cum_ok, 1)

            def body(t, b, first, last, i=None):
                if not last:
                    low(t + 1, 1 - b)
                n = turn(t, b, i)
                dve.wait_ge(x_in[b], 16 * n + 16)
                for q in range(2):
                    dve.wait_ge(w_mm, t + 1)
                    ins = dve.tensor_tensor(x[b][:, q * 512:(q + 1) * 512], x[b][:, q * 512:(q + 1) * 512],
                                            bank(2 * b + q), ALU.add)
                ins.then_inc(h_ok, 1)
                dve.wait_ge(rt_ok, t + 1)
                c.link(dve.reciprocal(st[:, 2 + b:3 + b], st[:, 2 + b:3 + b]))
                if not first:
                    dve.wait_ge(u_out[b], 16 * (n + b))
                dve.scalar_tensor_tensor(out=u[b][:, :], in0=x[b][:, :], scalar=st[:, 2 + b:3 + b], in1=gain[:, :],
                                         op0=ALU.mult, op1=ALU.mult).then_inc(u_ok, 1)
                choose(t, b)
                place(t, b, n, first)

            for n in range(4):
                dve.wait_ge(wh_ok, n + 1)
                dve.tensor_tensor(wol[:, 2 * n:2 * n + 2, :], w[n % 2][:, :, :], woh[:, 2 * n:2 * n + 2, :].bitcast(F32),
                                  ALU.subtract).then_inc(wl_ok, 1)
            low(0, 0)
            dve.wait_ge(cst_in, 80)
            dve.wait_ge(cst, 8)
            dve.wait_ge(rec_z, 2)
            per = 31
            body(0, 0, True, False)
            with dve.Fori(0, TT // 2 - 1) as i:
                c.enter(i, 2 * per)
                for b in (1, 0):
                    body(2 * i + 2 - b, b, False, False, i)
                c.leave(TT // 2 - 1)
            body(TT - 1, 1, False, True)
            dve.wait_ge(rk_mm, TT + 1)
            c.link(dve.tensor_reduce(out=sc[:, 12:13], in_=bank(7, 0, EXPERTS), axis=AX.X, op=ALU.max))
            c.link(dve.tensor_copy(g.most[:, :], sc[:, 12:13]))

        @block.tensor
        def _(pe):
            pe.wait_ge(wl_ok, 4)

            def times_out(t, b, first):
                pe.wait_ge(ml_ok, t + 1)
                for q in range(2):
                    for j in range(DK):
                        last = mm3(pe, bank(2 * b + q), mh[b][:, j, :], ml[b][:, j, :], woh[:, j, q * 512:(q + 1) * 512],
                                   wol[:, j, q * 512:(q + 1) * 512], j == 0, j == DK - 1)
                last.then_inc(w_mm, 1)

            def body(t, b, first, last, i=None):
                if not last:
                    if not first:
                        pe.wait_ge(h_ok, t)
                    times_out(t + 1, 1 - b, first)
                pe.wait_ge(u_ok, t + 1)
                for q in range(2):
                    for j in range(4):
                        last_i = pe.transpose(bank(4 + q, j * P, P), u[b][:, (4 * q + j) * P:(4 * q + j + 1) * P], g.ident[:, :])
                    last_i.then_inc(u_tr, 1)
                pe.wait_ge(uT_ok, 2 * t + 2)
                for j in range(DK):
                    ins = pe.matmul(bank(6, 0, R), uT[:, j, :], wr[:, j, :], start=j == 0, stop=j == DK - 1)
                ins.then_inc(lg_mm, 1)
                pe.wait_ge(M_ok, t + 1)
                if not first:
                    pe.wait_ge(cum_ok, t)
                pe.matmul(bank(7, 0, EXPERTS), upper[:, :], M[b][:, 2, :], start=True, stop=False)
                pe.matmul(bank(7, 0, EXPERTS), g.ones[:, :], Mcum[:, :], start=False, stop=True).then_inc(rk_mm, 1)

            pe.wait_ge(cst_in, 80)
            pe.wait_ge(cst, 8)
            times_out(0, 0, True)
            tiles(body, pe)
            pe.wait_ge(cum_ok, TT)
            pe.matmul(bank(7, 0, EXPERTS), g.ones[:, :], Mcum[:, :], start=True, stop=True).then_inc(rk_mm, 1)


def inside(e, d=0):
    return not isinstance(e, int) or 0 <= e + d < EXPERTS


def each_expert(eng, body):
    for e in range(-2, 4):
        body(e, e // 2, e % 2)
    with eng.Fori(2, EXPERTS // 2 - 2) as n:
        for b in range(2):
            body(2 * n + b, n, b)
    for e in range(EXPERTS - 4, EXPERTS + 2):
        body(e, e // 2, e % 2)


def wait(eng, sem, value):
    if not isinstance(value, int) or value > 0:
        eng.wait_ge(sem, value)


def phase_experts(nc, g):
    with ExitStack() as ph:
        sb = lambda n, s, d=F32: ph.enter_context(nc.sbuf_tensor(n, s, d))
        sem = semaphores(nc, ph)
        up_h = [sb(f"m_up_h{b}", [P, 2, DK, DE], F32R) for b in range(2)]
        up_l = [sb(f"m_up_l{b}", [P, 2, DK, DE], F32R) for b in range(2)]
        dn_h = [sb(f"m_dn_h{b}", [P, 2, D], F32R) for b in range(2)]
        dn_l = [sb(f"m_dn_l{b}", [P, 2, D], F32R) for b in range(2)]
        x = [sb(f"m_x{b}", [CAP, D]) for b in range(2)]
        xT_h = [sb(f"m_xT_h{b}", [P, DK, WIDE], F32R) for b in range(2)]
        xT_l = [sb(f"m_xT_l{b}", [P, DK, WIDE], F32R) for b in range(2)]
        sig, prod, hid = sb("m_sig", [CAP, DE]), sb("m_prod", [CAP, DE]), sb("m_hid", [CAP, DE])
        hT_h, hT_l = sb("m_hT_h", [P, 2, WIDE], F32R), sb("m_hT_l", [P, 2, WIDE], F32R)
        zero = sb("m_zero", [P, DK, WIDE - CAP])
        y = [sb(f"m_y{b}", [CAP, D]) for b in range(2)]
        tab = sb("m_tab", [EXPERTS, CAP * ROWS])
        rows = sb("m_rows", [CAP, 2, EXPERTS], I32)
        gate = sb("m_gate", [CAP, EXPERTS])
        src_row = [sb(f"m_src_row{b}", [CAP, 1], I32) for b in range(2)]
        dst_row = [sb(f"m_dst_row{b}", [CAP, 1], I32) for b in range(2)]
        tab_in, tab_tr, rows_ok, x_zero, pad_ok = (sem("m_tab_in"), sem("m_tab_tr"), sem("m_rows_ok"), sem("m_x_zero"),
                                                   sem("m_pad_ok"))
        x_in = [sem(f"m_x_in{b}") for b in range(2)]
        y_out = [sem(f"m_y_out{b}") for b in range(2)]
        row_ok = sem("m_row_ok")
        up_h_ok, up_l_ok, dn_h_ok, dn_l_ok = sem("m_up_h_ok"), sem("m_up_l_ok"), sem("m_dn_h_ok"), sem("m_dn_l_ok")
        x_tr, xh_ok, xl_ok, up_mm, sig_ok, prod_ok, hid_ok = (sem("m_x_tr"), sem("m_xh_ok"), sem("m_xl_ok"), sem("m_up_mm"),
                                                              sem("m_sig_ok"), sem("m_prod_ok"), sem("m_hid_ok"))
        h_tr, hh_ok, hl_ok, dn_mm, y_ok = sem("m_h_tr"), sem("m_hh_ok"), sem("m_hl_ok"), sem("m_dn_mm"), sem("m_y_ok")
        block = ph.enter_context(nc.Block())
        bank = lambda i, a=0, n=512, rows=P: g.ps[0:rows, i * 512 + a:i * 512 + a + n]
        turned = lambda i, n: bank(i, 0, n * CAP).rearrange("p (j t) -> p j t", j=n)
        X_BANK, UP_BANK, Y_BANK, H_BANK = 0, 2, 4, 6

        @block.sync
        def _(sp):
            sp.dma_start(tab[:, :], g.table.rearrange("(e s) r -> e s r", e=EXPERTS)[:, 0:CAP, :]
                         .rearrange("e s r -> e (s r)")).then_inc(tab_in, 16)

            def body(e, n, b):
                if inside(e, 3) and (not isinstance(e, int) or e > -2):
                    sp.wait_ge(up_l_ok, 2 * e + 4)
                    g.load_up(sp, e + 3, 1 - b)
                if inside(e, 2) and (not isinstance(e, int) or e > -1):
                    sp.wait_ge(dn_l_ok, e + 1)
                    g.load_down(sp, e + 2, b)

            each_expert(sp, body)

        @block.gpsimd
        def _(pool):
            k = [0]
            pool.memset(zero[:, :, :], 0.0).then_inc(x_zero, 1)
            for b in range(2):
                pool.memset(x[b][:, :], 0.0).then_inc(x_zero, 1)
            pool.wait_ge(x_zero, 3)
            pool.wait_ge(rows_ok, 3)

            def body(e, n, b):
                before = k[0] if isinstance(e, int) else 2 * e
                if inside(e, 2):
                    wait(pool, x_tr, 2 * e + 2)
                    settle(pool, g)
                    pool.tensor_copy(src_row[b][:, :], rows[:, 1, bass.ds(e + 2, 1)]).then_inc(row_ok, 1)
                    pool.wait_ge(row_ok, before + 1)
                    settle(pool, g)
                    pool.indirect_dma_start(out=x[b][:, :], out_offset=None, in_=g.u2,
                                            in_offset=bass.IndirectOffsetOnAxis(ap=src_row[b][:, 0:1], axis=0),
                                            bounds_check=SEQ - 1, oob_is_err=False).then_inc(x_in[b], 16)
                    before = before + 1
                if inside(e, -2):
                    pool.wait_ge(y_ok, 2 * e - 2)
                    settle(pool, g)
                    pool.tensor_copy(dst_row[b][:, :], rows[:, 0, bass.ds(e - 2, 1)]).then_inc(row_ok, 1)
                    pool.wait_ge(row_ok, before + 1)
                    settle(pool, g)
                    pool.indirect_dma_start(out=g.y, out_offset=bass.IndirectOffsetOnAxis(ap=dst_row[b][:, 0:1], axis=0),
                                            in_=y[b][:, :], in_offset=None,
                                            bounds_check=2 * SEQ - 1, oob_is_err=False).then_inc(y_out[b], 16)
                    before = before + 1
                k[0] = before if isinstance(e, int) else 2 * (EXPERTS - 4)

            each_expert(pool, body)
            for b in range(2):
                pool.wait_ge(y_out[b], 16 * (EXPERTS // 2))

        @block.scalar
        def _(act):
            act.wait_ge(x_zero, 3)
            for t in (*xT_h, *xT_l, hT_h, hT_l):
                act.activation(t[:, :, CAP:WIDE], zero[:, 0:t.shape[1], :], ACT.Copy).then_inc(pad_ok, 1)
            act.wait_ge(rows_ok, 3)

            def split_up(e, n, b, r):
                if r == 0:
                    act.wait_ge(g.w_up_in[1 - b], 32 * (n + b + 1))
                act.activation(up_h[1 - b][:, r, :, :], g.r13[1 - b][:, r, :, :], ACT.Copy).then_inc(up_h_ok, 1)

            def body(e, n, b):
                if inside(e, -1):
                    act.wait_ge(up_mm, e)
                    act.activation(sig[:, :], bank(UP_BANK + 1 - b, 0, DE, CAP), ACT.Sigmoid).then_inc(sig_ok, 1)
                if inside(e, 1):
                    split_up(e, n, b, 0)
                if inside(e, -2):
                    if inside(e, -4):
                        act.wait_ge(y_out[b], 16 * (n - 1))
                    for q in range(2):
                        act.wait_ge(dn_mm, 2 * e + q - 3)
                        settle(act, g)
                        act.activation(y[b][:, q * 512:(q + 1) * 512], bank(Y_BANK + q, rows=CAP), ACT.Copy,
                                       scale=gate[:, bass.ds(e - 2, 1)]).then_inc(y_ok, 1)
                if inside(e):
                    act.wait_ge(g.w_down_in[b], 16 * (n + 1))
                    act.activation(dn_h[b][:, :, :], g.r2[b][:, :, :], ACT.Copy).then_inc(dn_h_ok, 1)
                if inside(e, -1):
                    act.wait_ge(h_tr, e)
                    act.activation(hT_h[:, :, 0:CAP], turned(H_BANK, 2), ACT.Copy).then_inc(hh_ok, 1)
                if inside(e, 1):
                    for q in range(2):
                        act.wait_ge(x_tr, 2 * e + q + 3)
                        act.activation(xT_h[1 - b][:, 4 * q:4 * q + 4, 0:CAP], turned(X_BANK + q, 4),
                                       ACT.Copy).then_inc(xh_ok, 1)
                    split_up(e, n, b, 1)

            each_expert(act, body)

        @block.vector
        def _(dve):
            dve.wait_ge(tab_tr, 1)
            for c in range(2):
                dve.tensor_copy(rows[:, c, :], bank(H_BANK + 1, 2 * c * EXPERTS, EXPERTS, CAP)).then_inc(rows_ok, 1)
            dve.tensor_copy(gate[:, :], bank(H_BANK + 1, EXPERTS, EXPERTS, CAP)).then_inc(rows_ok, 1)

            def split_up(e, b, r):
                dve.wait_ge(up_h_ok, 2 * e + r + 3)
                dve.tensor_tensor(up_l[1 - b][:, r, :, :], g.r13[1 - b][:, r, :, :], up_h[1 - b][:, r, :, :].bitcast(F32),
                                  ALU.subtract).then_inc(up_l_ok, 1)

            def body(e, n, b):
                if inside(e, -1):
                    dve.wait_ge(sig_ok, e)
                    dve.tensor_tensor(prod[:, :], sig[:, :], bank(UP_BANK + 1 - b, 0, DE, CAP), ALU.mult).then_inc(prod_ok, 1)
                    dve.wait_ge(prod_ok, e)
                    dve.tensor_tensor(hid[:, :], prod[:, :], bank(UP_BANK + 1 - b, DE, DE, CAP), ALU.mult).then_inc(hid_ok, 1)
                if inside(e, 1):
                    split_up(e, b, 0)
                if inside(e, -1):
                    dve.wait_ge(hh_ok, e)
                    dve.tensor_tensor(hT_l[:, :, 0:CAP], turned(H_BANK, 2), hT_h[:, :, 0:CAP].bitcast(F32),
                                      ALU.subtract).then_inc(hl_ok, 1)
                if inside(e, 1):
                    for q in range(2):
                        dve.wait_ge(xh_ok, 2 * e + q + 3)
                        dve.tensor_tensor(xT_l[1 - b][:, 4 * q:4 * q + 4, 0:CAP], turned(X_BANK + q, 4),
                                          xT_h[1 - b][:, 4 * q:4 * q + 4, 0:CAP].bitcast(F32), ALU.subtract).then_inc(xl_ok, 1)
                if inside(e):
                    dve.wait_ge(dn_h_ok, e + 1)
                    dve.tensor_tensor(dn_l[b][:, :, :], g.r2[b][:, :, :], dn_h[b][:, :, :].bitcast(F32),
                                      ALU.subtract).then_inc(dn_l_ok, 1)
                if inside(e, 1):
                    split_up(e, b, 1)

            each_expert(dve, body)

        @block.tensor
        def _(pe):
            pe.wait_ge(tab_in, 16)
            for c in range(3):
                ins = pe.transpose(bank(H_BANK + 1, c * EXPERTS, EXPERTS, CAP), tab[:, c::ROWS], g.ident[0:EXPERTS, 0:EXPERTS])
            ins.then_inc(tab_tr, 1)
            pe.wait_ge(rows_ok, 3)
            pe.wait_ge(pad_ok, 6)

            def up(b, js):
                for j in js:
                    ins = mm3(pe, bank(UP_BANK + b, rows=WIDE).rearrange("p (r f) -> p r f", r=2), xT_h[b][:, j, :], xT_l[b][:, j, :],
                              up_h[b][:, :, j, :], up_l[b][:, :, j, :], j == 0, j == DK - 1)
                return ins

            def body(e, n, b):
                if inside(e):
                    pe.wait_ge(up_l_ok, 2 * e + 2)
                    pe.wait_ge(xl_ok, 2 * e + 2)
                    up(b, range(DK // 2))
                if inside(e, -1):
                    pe.wait_ge(hid_ok, e)
                    settle(pe, g)
                    for j in range(2):
                        ins = pe.transpose(bank(H_BANK, j * CAP, CAP), hid[:, j::2], g.ident[0:CAP, 0:CAP])
                    ins.then_inc(h_tr, 1)
                if inside(e, 1):
                    pe.wait_ge(x_in[1 - b], 16 * (n + b + 1))
                    wait(pe, xl_ok, 2 * e + 2)
                    settle(pe, g)
                    for q in range(2):
                        for j in range(4):
                            ins = pe.transpose(bank(X_BANK + q, j * CAP, CAP), x[1 - b][:, 4 * q + j::DK], g.ident[0:CAP, 0:CAP])
                        ins.then_inc(x_tr, 1)
                if inside(e):
                    up(b, range(DK // 2, DK)).then_inc(up_mm, 1)
                if inside(e, -1):
                    pe.wait_ge(hl_ok, e)
                    pe.wait_ge(dn_l_ok, e)
                    if inside(e, -2):
                        pe.wait_ge(y_ok, 2 * e - 2)
                    for q in range(2):
                        for j in range(2):
                            ins = mm3(pe, bank(Y_BANK + q, rows=WIDE), hT_h[:, j, :], hT_l[:, j, :],
                                      dn_h[1 - b][:, j, q * 512:(q + 1) * 512], dn_l[1 - b][:, j, q * 512:(q + 1) * 512],
                                      j == 0, j == 1)
                        ins.then_inc(dn_mm, 1)

            each_expert(pe, body)


def phase_overflow(nc, g):
    BLOCKS = (SLOTS // CAP - 1) * EXPERTS
    with ExitStack() as ph:
        sb = lambda n, s, d=F32: ph.enter_context(nc.sbuf_tensor(n, s, d))
        sem = semaphores(nc, ph)
        x, xT = sb("v_x", [CAP, D]), sb("v_xT", [P, DK, CAP])
        sig, prod, hid, hT = sb("v_sig", [CAP, DE]), sb("v_prod", [CAP, DE]), sb("v_hid", [CAP, DE]), sb("v_hT", [P, 2, CAP])
        y = sb("v_y", [CAP, D])
        rec, rows = sb("v_rec", [CAP, ROWS]), sb("v_rows", [CAP, ROWS], I32)
        up_in, down_in, rec_in, x_zero = sem("v_up_in"), sem("v_down_in"), sem("v_rec_in"), sem("v_x_zero")
        rows_ok, x_in, x_tr, xT_ok, up_mm = sem("v_rows_ok"), sem("v_x_in"), sem("v_x_tr"), sem("v_xT_ok"), sem("v_up_mm")
        sig_ok, prod_ok, hid_ok, h_tr, hT_ok = sem("v_sig_ok"), sem("v_prod_ok"), sem("v_hid_ok"), sem("v_h_tr"), sem("v_hT_ok")
        dn_mm, y_ok, y_out, turn = sem("v_dn_mm"), sem("v_y_ok"), sem("v_y_out"), sem("v_turn")
        block = ph.enter_context(nc.Block())
        bank = lambda i, a=0, n=512, rows=P: g.ps[0:rows, i * 512 + a:i * 512 + a + n]
        turned = lambda i, n: bank(i, 0, n * CAP).rearrange("p (j t) -> p j t", j=n)
        X_BANK, UP_BANK, Y_BANK, H_BANK = 0, 2, 4, 6

        def blocks(eng, body):
            most = eng.value_load(g.most[0:1, 0:1], min_val=0, max_val=SLOTS)
            with eng.If(most > CAP):
                with eng.Fori(1, SLOTS // CAP) as c:
                    with eng.Fori(0, EXPERTS) as e:
                        body((c - 1) * EXPERTS + e, e, c)
                eng.sem_inc(g.settled, 1)
            with eng.Else():
                eng.sem_inc(g.settled, 1)

        @block.sync
        def _(sp):
            table = g.table.rearrange("(e b s) r -> e b s r", e=EXPERTS, s=CAP)
            up = [a[0].rearrange("e (p j) f -> p e j f", j=DK) for a in (g.w1, g.w3)]
            down = g.w2[0].rearrange("e (p j) n -> p e j n", j=2)

            def body(k, e, c):
                sp.wait_ge(turn, k + 1)
                sp.dma_start(rec[:, :], table[bass.ds(e, 1), bass.ds(c, 1), :, :].rearrange("a b s r -> (a b s) r")
                             ).then_inc(rec_in, 16)
                for r in range(2):
                    sp.dma_start(g.r13[0][:, r, :, :], up[r][:, bass.ds(e, 1), :, :].rearrange("p a j f -> p (a j) f")
                                 ).then_inc(up_in, 16)
                sp.dma_start(g.r2[0][:, :, :], down[:, bass.ds(e, 1), :, :].rearrange("p a j n -> p (a j) n")
                             ).then_inc(down_in, 16)

            blocks(sp, body)

        @block.gpsimd
        def _(pool):
            pool.memset(x[:, :], 0.0).then_inc(x_zero, 1)
            pool.sem_inc(turn, 1)
            pool.wait_ge(x_zero, 1)

            def body(k, e, c):
                pool.wait_ge(rows_ok, k + 1)
                settle(pool, g)
                pool.indirect_dma_start(out=x[:, :], out_offset=None, in_=g.u2,
                                        in_offset=bass.IndirectOffsetOnAxis(ap=rows[:, 2:3], axis=0),
                                        bounds_check=SEQ - 1, oob_is_err=False).then_inc(x_in, 16)
                pool.wait_ge(y_ok, 2 * k + 2)
                settle(pool, g)
                pool.indirect_dma_start(out=g.y, out_offset=bass.IndirectOffsetOnAxis(ap=rows[:, 0:1], axis=0),
                                        in_=y[:, :], in_offset=None,
                                        bounds_check=2 * SEQ - 1, oob_is_err=False).then_inc(y_out, 16)
                pool.wait_ge(y_out, 16 * k + 16)
                pool.sem_inc(turn, 1)

            blocks(pool, body)

        @block.scalar
        def _(act):
            def body(k, e, c):
                for q in range(2):
                    act.wait_ge(x_tr, 2 * k + q + 1)
                    act.activation(xT[:, 4 * q:4 * q + 4, :], turned(X_BANK + q, 4), ACT.Copy).then_inc(xT_ok, 1)
                act.wait_ge(up_mm, k + 1)
                act.activation(sig[:, :], bank(UP_BANK, 0, DE, CAP), ACT.Sigmoid).then_inc(sig_ok, 1)
                act.wait_ge(h_tr, k + 1)
                act.activation(hT[:, :, :], turned(H_BANK, 2), ACT.Copy).then_inc(hT_ok, 1)
                for q in range(2):
                    act.wait_ge(dn_mm, 2 * k + q + 1)
                    act.activation(y[:, q * 512:(q + 1) * 512], bank(Y_BANK + q, rows=CAP), ACT.Copy,
                                   scale=rec[:, 1:2]).then_inc(y_ok, 1)

            blocks(act, body)

        @block.vector
        def _(dve):
            def body(k, e, c):
                dve.wait_ge(rec_in, 16 * k + 16)
                dve.tensor_copy(rows[:, :], rec[:, :]).then_inc(rows_ok, 1)
                dve.wait_ge(sig_ok, k + 1)
                dve.tensor_tensor(prod[:, :], sig[:, :], bank(UP_BANK, 0, DE, CAP), ALU.mult).then_inc(prod_ok, 1)
                dve.wait_ge(prod_ok, k + 1)
                dve.tensor_tensor(hid[:, :], prod[:, :], bank(UP_BANK, DE, DE, CAP), ALU.mult).then_inc(hid_ok, 1)

            blocks(dve, body)

        @block.tensor
        def _(pe):
            def body(k, e, c):
                pe.wait_ge(x_in, 16 * k + 16)
                settle(pe, g)
                for q in range(2):
                    for j in range(4):
                        ins = pe.transpose(bank(X_BANK + q, j * CAP, CAP), x[:, 4 * q + j::DK], g.ident[0:CAP, 0:CAP])
                    ins.then_inc(x_tr, 1)
                pe.wait_ge(up_in, 32 * k + 32)
                pe.wait_ge(xT_ok, 2 * k + 2)
                for j in range(DK):
                    ins = pe.matmul(bank(UP_BANK, rows=CAP).rearrange("p (r f) -> p r f", r=2), xT[:, j, :],
                                    g.r13[0][:, :, j, :], start=j == 0, stop=j == DK - 1)
                ins.then_inc(up_mm, 1)
                pe.wait_ge(hid_ok, k + 1)
                settle(pe, g)
                for j in range(2):
                    ins = pe.transpose(bank(H_BANK, j * CAP, CAP), hid[:, j::2], g.ident[0:CAP, 0:CAP])
                ins.then_inc(h_tr, 1)
                pe.wait_ge(down_in, 16 * k + 16)
                pe.wait_ge(hT_ok, k + 1)
                for q in range(2):
                    for j in range(2):
                        ins = pe.matmul(bank(Y_BANK + q, rows=CAP), hT[:, j, :], g.r2[0][:, j, q * 512:(q + 1) * 512],
                                        start=j == 0, stop=j == 1)
                    ins.then_inc(dn_mm, 1)

            blocks(pe, body)


def phase_final(nc, g):
    with ExitStack() as ph:
        sb = lambda n, s, d=F32: ph.enter_context(nc.sbuf_tensor(n, s, d))
        sem = semaphores(nc, ph)
        NB = 4
        h = [sb(f"z_h{b}", [P, D]) for b in range(NB)]
        y = [sb(f"z_y{b}", [P, 2, D]) for b in range(NB)]
        o = [sb(f"z_o{b}", [P, D]) for b in range(NB)]
        gain, junk = sb("z_gain", [P, D]), sb("z_junk", [P, D])
        st = [sb(f"z_stat{b}", [P, 2]) for b in range(NB)]
        gain_in = sem("z_gain_in")
        t_in = [sem(f"z_t_in{b}") for b in range(NB)]
        stored = [sem(f"z_stored{b}") for b in range(NB)]
        s0_ok, s1_ok, ss_ok, rt_ok, rc_ok, o_ok = (sem("z_s0_ok"), sem("z_s1_ok"), sem("z_ss_ok"), sem("z_rt_ok"),
                                                   sem("z_rc_ok"), sem("z_o_ok"))
        block = ph.enter_context(nc.Block())
        y_src = g.y.rearrange("(t c) d -> t c d", c=2)

        def rounds(eng, body):
            with eng.Fori(0, TT // NB) as i:
                for b in range(NB):
                    body(NB * i + b, b, i)

        @block.sync
        def _(sp):
            def load(t, b):
                sp.dma_start(h[b][:, :], g.h[bass.ds(t * P, P), :]).then_inc(t_in[b], 16)
                sp.dma_start(y[b][:, :, :], y_src[bass.ds(t * P, P), :, :]).then_inc(t_in[b], 16)

            load(0, 0)
            sp.dma_start(gain[:, :], g.final_norm[None, :].to_broadcast([P, D])).then_inc(gain_in, 16)
            for b in range(1, NB):
                load(b, b)
            with sp.Fori(0, TT // NB - 1) as i:
                for b in range(NB):
                    sp.wait_ge(o_ok, NB * i + b + 1)
                    load(NB * i + NB + b, b)

        @block.gpsimd
        def _(pool):
            def body(t, b, i):
                pool.wait_ge(o_ok, t + 1)
                settle(pool, g)
                pool.dma_start(g.out[0, bass.ds(t * P, P), :], o[b][:, :]).then_inc(stored[b], 16)

            rounds(pool, body)
            for b in range(NB):
                pool.wait_ge(stored[b], 16 * (TT // NB))

        @block.scalar
        def _(act):
            def body(t, b, i):
                act.wait_ge(s1_ok, t + 1)
                act.activation(junk[:, :], h[b][:, :], ACT.Square, accum_out=st[b][:, 0:1]).then_inc(ss_ok, 1)
                act.wait_ge(ss_ok, t + 1)
                act.activation(st[b][:, 1:2], st[b][:, 0:1], ACT.Sqrt, scale=1.0 / D, bias=g.eps[:, :]).then_inc(rt_ok, 1)

            rounds(act, body)

        @block.vector
        def _(dve):
            dve.wait_ge(gain_in, 16)

            def body(t, b, i):
                dve.wait_ge(t_in[b], 32 * i + 32)
                for c, done in ((0, s0_ok), (1, s1_ok)):
                    dve.tensor_tensor(h[b][:, :], h[b][:, :], y[b][:, c, :], ALU.add).then_inc(done, 1)
                    dve.wait_ge(done, t + 1)
                dve.wait_ge(rt_ok, t + 1)
                dve.reciprocal(st[b][:, 1:2], st[b][:, 1:2]).then_inc(rc_ok, 1)
                dve.wait_ge(rc_ok, t + 1)
                wait(dve, stored[b], 16 * i)
                dve.scalar_tensor_tensor(out=o[b][:, :], in0=h[b][:, :], scalar=st[b][:, 1:2], in1=gain[:, :],
                                         op0=ALU.mult, op1=ALU.mult).then_inc(o_ok, 1)

            for b in range(NB):
                body(b, b, 0)
            with dve.Fori(1, TT // NB) as i:
                for b in range(NB):
                    body(NB * i + b, b, i)


def program(nc, a, out):
    g = Ctx(a, out)
    g.gates = nc.dram_tensor("gates", [2 * D, SEQ], F32, kind="Internal").ap()
    g.merged = nc.dram_tensor("merged", [D, SEQ], F32, kind="Internal").ap()
    g.h = nc.dram_tensor("h_mid", [SEQ, D], F32, kind="Internal").ap()
    g.u2 = nc.dram_tensor("u_moe", [SEQ, D], F32, kind="Internal").ap()
    g.y = nc.dram_tensor("y_moe", [2 * SEQ, D], F32, kind="Internal").ap()
    g.table = nc.dram_tensor("slots", [EXPERTS * SLOTS, ROWS], F32, kind="Internal").ap()
    with ExitStack() as keep:
        g.most = keep.enter_context(nc.sbuf_tensor("most", [P, 1], I32))
        g.ident = keep.enter_context(nc.sbuf_tensor("ident", [P, P], F32))
        g.ones = keep.enter_context(nc.sbuf_tensor("ones", [P, P], F32))
        g.eps = keep.enter_context(nc.sbuf_tensor("eps", [P, 1], F32))
        g.settled = keep.enter_context(nc.semaphore("settled"))
        g.ps = keep.enter_context(nc.psum_tensor("ps", [P, 8 * 512], F32))
        left = lambda st, n, sh, d=F32: st.enter_context(nc.sbuf_tensor(n, sh, d))
        oh = ExitStack()
        g.ohTh, g.ohTl = left(oh, "ohTh", [P, HG, SEQ], F32R), left(oh, "ohTl", [P, HG, SEQ], F32R)
        with ExitStack() as ust:
            g.uTh = ust.enter_context(nc.sbuf_tensor("uTh", [P, DK, NT], F32R, side="right"))
            g.uTl = ust.enter_context(nc.sbuf_tensor("uTl", [P, DK, NT], F32R, side="right"))
            phase_norm_in(nc, g)
            phase_gates(nc, g)
            phase_hgrn(nc, g)
            lat = ExitStack()
            g.cqh, g.cql = left(lat, "cqh", [P, 3, SEQ], F32R), left(lat, "cql", [P, 3, SEQ], F32R)
            g.ckh, g.ckl = left(lat, "ckh", [P, 2, NT], F32R), left(lat, "ckl", [P, 2, NT], F32R)
            g.kpe = left(lat, "kpe", [QH, NT])
            g.cos, g.sin = left(lat, "cos", [QH, NT]), left(lat, "sin", [QH, NT])
            phase_latents(nc, g)
        with ExitStack() as qkv:
            right = lambda n, sh: qkv.enter_context(nc.sbuf_tensor(n, sh, F32, side="right"))
            g.QT, g.KT = right("QT", [QH, HEADS, SEQ]), right("KT", [QH, HEADS, NT])
            g.V = right("V", [P, HEADS // 2, TT + 1, VD + P])
            phase_heads(nc, g)
            lat.close()
            om = ExitStack()
            g.omTh, g.omTl = left(om, "omTh", [P, 4, SEQ], F32R), left(om, "omTl", [P, 4, SEQ], F32R)
            phase_attention(nc, g)
        phase_merge(nc, g)
        om.close()
        oh.close()
        wraw = ExitStack()
        g.r13 = [wraw.enter_context(nc.sbuf_tensor(f"r13_{b}", [P, 2, DK, DE], F32, side="right")) for b in range(2)]
        g.r2 = [wraw.enter_context(nc.sbuf_tensor(f"r2_{b}", [P, 2, D], F32, side="right")) for b in range(2)]
        g.w_up_in = [keep.enter_context(nc.semaphore(f"w_up_in{b}")) for b in range(2)]
        g.w_down_in = [keep.enter_context(nc.semaphore(f"w_down_in{b}")) for b in range(2)]
        g.load_up, g.load_down = expert_loaders(g)
        phase_output(nc, g)
        phase_experts(nc, g)
        phase_overflow(nc, g)
        wraw.close()
        phase_final(nc, g)

_INPUTS = ["x", "meta_tokens", "attn_norm", "w_in", "q_norm", "w_uq", "kv_norm", "w_ukv", "lb_table", "hg_norm",
           "w_br_mla", "w_br_hgrn", "b_gate", "w_out", "ffn_norm", "w_group", "b_group", "w_route", "b_route",
           "w1", "w3", "w2", "final_norm"]


def rotary():
    inv = (np.float32(10000.0) ** (-np.arange(0, ROPE, 2, dtype=np.float32) / np.float32(ROPE))).astype(np.float32)
    pos = np.concatenate([np.arange(META, META + SEQ), np.arange(META)]).astype(np.float32)
    ang = (inv[:, None] * pos[None, :]).astype(np.float32)
    cos, sin = np.cos(ang), np.sin(ang)
    return (np.concatenate([cos, cos], 0).astype(np.float32), np.concatenate([-sin, sin], 0).astype(np.float32))


def kernel(**inputs):
    import concourse.bacc as bacc
    from concourse.bass_utils import run_bass_kernel_spmd

    nc = bacc.Bacc("TRN2", target_bir_lowering=False, num_devices=1)
    arrays, aps = {}, {}
    cos, sin = rotary()
    for name in _INPUTS + ["rope_cos", "rope_sin"]:
        a = cos if name == "rope_cos" else sin if name == "rope_sin" else np.ascontiguousarray(inputs[name])
        arrays["in_" + name] = a
        aps[name] = nc.dram_tensor("in_" + name, a.shape, mybir.dt.from_np(a.dtype), kind="ExternalInput").ap()
    out = nc.dram_tensor("out_0", (1, SEQ, D), F32, kind="ExternalOutput").ap()
    program(nc, aps, out)
    r = run_bass_kernel_spmd(nc, [arrays], core_ids=[0])
    return r.results[0]["out_0"]
```

```python
from contextlib import ExitStack

import numpy as np
import concourse.bass as bass
from concourse import mybir

F32 = mybir.dt.float32
F32R = mybir.dt.float32r
I32 = mybir.dt.int32
U32 = mybir.dt.uint32
ACT = mybir.ActivationFunctionType
ALU = mybir.AluOpType
AX = mybir.AxisListType

P = 128
D = 1024
DK = D // P
SEQ = 1024
TT = SEQ // P
META = 16
NT = SEQ + META
EPS = 1e-6
QL, KVL, ROPE = 384, 256, 32
NOPE, VD, HEADS = 64, 64, 8
QH = NOPE + ROPE
HG = 4
CH = 32
SCALE = QH ** -0.5
C_CQ, C_CKV = 0, QL
C_KPE = QL + KVL
C_HQ = C_KPE + ROPE
C_HF = C_HQ + 512
C_HI = C_HF + 512
C_HG = C_HI + 512
C_GM = C_HG + 512
GROUPS, EXPERTS, DE = 8, 64, 256
ROWS = 4
SLOTS = 1024
CAP = 64
WIDE = 96
SKIP = 4096.0
PIECES = [(0, 512), (512, 512), (SEQ, META)]
HG_BANKS = (0, 3)
LATENT_BANKS = (0, 3)
SWAP = [(i + ROPE // 2) % ROPE for i in range(ROPE)]


class Steps:

    def __init__(self, eng, sem):
        self.eng, self.sem, self.base, self.k = eng, sem, 0, 0

    def mark(self, ins):
        ins.then_inc(self.sem, 1)
        self.k += 1

    def link(self, ins):
        self.mark(ins)
        self.eng.wait_ge(self.sem, self.base + self.k)

    def now(self):
        return self.base + self.k

    def enter(self, i, per):
        self.outer, self.per = self.base + self.k, per
        self.base, self.k = self.outer + i * per, 0

    def leave(self, n):
        assert self.k == self.per, (self.k, self.per)
        self.base, self.k = self.outer + n * self.per, 0


class Ctx:

    def __init__(self, a, out):
        self.x, self.meta_tokens, self.attn_norm, self.w_in = a["x"], a["meta_tokens"], a["attn_norm"], a["w_in"]
        self.q_norm, self.w_uq, self.kv_norm, self.w_ukv = a["q_norm"], a["w_uq"], a["kv_norm"], a["w_ukv"]
        self.lb_table, self.hg_norm, self.b_gate = a["lb_table"], a["hg_norm"], a["b_gate"]
        self.w_br_mla, self.w_br_hgrn, self.w_out = a["w_br_mla"], a["w_br_hgrn"], a["w_out"]
        self.ffn_norm, self.w_group, self.b_group = a["ffn_norm"], a["w_group"], a["b_group"]
        self.w_route, self.b_route, self.final_norm = a["w_route"], a["b_route"], a["final_norm"]
        self.w1, self.w3, self.w2 = a["w1"], a["w3"], a["w2"]
        self.rope_cos, self.rope_sin = a["rope_cos"], a["rope_sin"]
        self.out = out


def semaphores(nc, phase):
    made = []

    def clear():
        nc.clear_and_free_semaphores(made)
        nc.all_engine_barrier()

    phase.callback(clear)

    def sem(name):
        made.append(nc.alloc_semaphore(name=name))
        return made[-1]

    return sem


def wait(eng, sem, value):
    if not isinstance(value, int) or value > 0:
        eng.wait_ge(sem, value)


def settle(eng, g):
    eng.sem_inc(g.settled, 1)


def mm3(pe, out, lh, ll, rh, rl, start, stop):
    pe.matmul(out, lh, rh, start=start, stop=False)
    pe.matmul(out, lh, rl, start=False, stop=False)
    return pe.matmul(out, ll, rh, start=False, stop=stop)


def phase_norm_in(nc, g):
    with ExitStack() as ph:
        sb = lambda n, s, d=F32: ph.enter_context(nc.sbuf_tensor(n, s, d))
        sem = semaphores(nc, ph)
        x = sb("a_x", [P, 2, D])
        sq = sb("a_sq", [P, D])
        u = sb("a_u", [P, 2, D])
        gain = sb("a_gain", [P, D])
        ss = sb("a_ss", [P, 4])
        x_in = [sem("a_x_in0"), sem("a_x_in1")]
        const_in, meta_in = sem("a_const_in"), sem("a_meta_in")
        ss_done, rt_done, u_done, tr_done = sem("a_ss_done"), sem("a_rt_done"), sem("a_u_done"), sem("a_tr_done")
        hi_done, lo_done, dv, consts = sem("a_hi"), sem("a_lo"), sem("a_dv"), sem("a_consts")
        block = ph.enter_context(nc.Block())

        @block.sync
        def _(sp):
            sp.dma_start(x[0:META, 1, :], g.meta_tokens).then_inc(meta_in, 16)
            sp.dma_start(gain[:, :], g.attn_norm[0:1, :].to_broadcast([P, D])).then_inc(const_in, 16)
            sp.dma_start(x[:, 0, :], g.x[0, 0:P, :]).then_inc(x_in[0], 16)
            sp.wait_ge(u_done, 1)
            sp.dma_start(x[:, 1, :], g.x[0, P:2 * P, :]).then_inc(x_in[1], 16)
            with sp.Fori(0, TT // 2 - 1) as i:
                for b in range(2):
                    sp.wait_ge(u_done, 2 * i + b + 2)
                    t = 2 * i + b + 2
                    sp.dma_start(x[:, b, :], g.x[0, bass.ds(t * P, P), :]).then_inc(x_in[b], 16)

        @block.gpsimd
        def _(pool):
            pool.memset(g.ident[:, :], 0.0).then_inc(consts, 1)
            pool.memset(g.ones[:, :], 1.0).then_inc(consts, 1)
            pool.memset(g.eps[:, :], EPS).then_inc(consts, 1)
            pool.wait_ge(consts, 3)
            pool.affine_select(out=g.ident[:, :], in_=g.ident[:, :], compare_op=ALU.not_equal, fill=1.0,
                               base=0, pattern=[[-1, P]], channel_multiplier=1).then_inc(consts, 1)

        @block.scalar
        def _(act):
            act.wait_ge(consts, 4)

            def sums(n, xs, rows, b):
                act.activation(sq[0:rows, :], xs, ACT.Square, accum_out=ss[0:rows, b:b + 1]).then_inc(ss_done, 1)
                act.wait_ge(ss_done, n + 1)
                act.activation(ss[0:rows, 2 + b:3 + b], ss[0:rows, b:b + 1], ACT.Sqrt, scale=1.0 / D,
                               bias=g.eps[0:rows, :]).then_inc(rt_done, 1)

            def evac(n, rows, b, col):
                for q in range(2):
                    act.wait_ge(tr_done, 2 * n + q + 1)
                    settle(act, g)
                    src = g.ps[:, (2 * b + q) * 512:(2 * b + q + 1) * 512].rearrange("p (j t) -> p j t", j=4)
                    act.activation(g.uTh[:, 4 * q:4 * q + 4, bass.ds(col, rows)], src[:, :, 0:rows],
                                   ACT.Copy).then_inc(hi_done, 1)

            def body(t, n, b, more=True):
                if more:
                    act.wait_ge(x_in[1 - b], 16 * (n + b) + 16)
                    act.wait_ge(u_done, t + 1)
                    sums(t + 2, x[:, 1 - b, :], P, 1 - b)
                evac(t + 1, P, b, t * P)

            act.wait_ge(meta_in, 16)
            sums(0, x[0:META, 1, :], META, 1)
            act.wait_ge(x_in[0], 16)
            sums(1, x[:, 0, :], P, 0)
            evac(0, META, 1, SEQ)
            with act.Fori(0, TT // 2 - 1) as n:
                for b in range(2):
                    body(2 * n + b, n, b)
            body(TT - 2, TT // 2 - 1, 0)
            body(TT - 1, TT // 2 - 1, 1, False)

        @block.vector
        def _(dve):
            v = Steps(dve, dv)

            def scaled(n, rows, b):
                dve.wait_ge(rt_done, n + 1)
                v.link(dve.reciprocal(ss[0:rows, 2 + b:3 + b], ss[0:rows, 2 + b:3 + b]))
                dve.scalar_tensor_tensor(out=u[0:rows, b, :], in0=x[0:rows, b, :], scalar=ss[0:rows, 2 + b:3 + b],
                                         in1=gain[0:rows, :], op0=ALU.mult, op1=ALU.mult).then_inc(u_done, 1)

            def low(n, rows, b, col):
                for q in range(2):
                    dve.wait_ge(hi_done, 2 * n + q + 1)
                    src = g.ps[:, (2 * b + q) * 512:(2 * b + q + 1) * 512].rearrange("p (j t) -> p j t", j=4)
                    dve.tensor_tensor(g.uTl[:, 4 * q:4 * q + 4, bass.ds(col, rows)], src[:, :, 0:rows],
                                      g.uTh[:, 4 * q:4 * q + 4, bass.ds(col, rows)].bitcast(F32),
                                      ALU.subtract).then_inc(lo_done, 1)

            def body(t, b, more=True):
                if more:
                    scaled(t + 2, P, 1 - b)
                low(t + 1, P, b, t * P)

            dve.wait_ge(const_in, 16)
            dve.wait_ge(meta_in, 16)
            scaled(0, META, 1)
            dve.wait_ge(x_in[0], 16)
            scaled(1, P, 0)
            low(0, META, 1, SEQ)
            with dve.Fori(0, TT // 2 - 1) as n:
                v.enter(n, 2)
                for b in range(2):
                    dve.wait_ge(x_in[1 - b], 16 * (n + b) + 16)
                    body(2 * n + b, b)
                v.leave(TT // 2 - 1)
            dve.wait_ge(x_in[1], 16 * (TT // 2))
            body(TT - 2, 0)
            body(TT - 1, 1, False)

        @block.tensor
        def _(pe):
            pe.wait_ge(consts, 4)

            def flip(n, rows, b):
                pe.wait_ge(u_done, n + 1)
                for q in range(2):
                    for j in range(4):
                        last = pe.transpose(g.ps[:, (2 * b + q) * 512 + j * P:(2 * b + q) * 512 + j * P + rows],
                                            u[0:rows, b, 4 * q + j::DK], g.ident[0:rows, 0:rows])
                    last.then_inc(tr_done, 1)

            flip(0, META, 1)
            with pe.Fori(0, TT // 2) as i:
                for b in range(2):
                    pe.wait_ge(lo_done, 4 * i + 2 * b + 1)
                    flip(2 * i + b + 1, P, b)


def phase_gates(nc, g):
    NB = 2 * DK
    with ExitStack() as ph:
        sb = lambda n, s, d=F32: ph.enter_context(nc.sbuf_tensor(n, s, d))
        sem = semaphores(nc, ph)
        w = [sb(f"g_w{b}", [P, DK, P]) for b in range(2)]
        wh = [sb(f"g_wh{b}", [P, DK, P], F32R) for b in range(2)]
        wl = [sb(f"g_wl{b}", [P, DK, P], F32R) for b in range(2)]
        sg = [sb(f"g_sg{b}", [P, SEQ]) for b in range(2)]
        bias = sb("g_bias", [P, NB])
        w_in = [sem(f"g_w_in{b}") for b in range(2)]
        out_sem = [sem(f"g_out{b}") for b in range(2)]
        bias_in, wh_done, wl_done, mm_done, sg_done = (sem("g_bias_in"), sem("g_wh_done"), sem("g_wl_done"),
                                                       sem("g_mm_done"), sem("g_sg_done"))
        block = ph.enter_context(nc.Block())
        w_src = g.w_in[0].rearrange("(p j) n -> p j n", j=DK)

        @block.sync
        def _(sp):
            with nc.allow_non_contiguous_dma(reason="a small bias turned once"):
                sp.dma_start(bias[:, :], g.b_gate[0].rearrange("a (j p) -> p (a j)", p=P)).then_inc(bias_in, 16)
            for b in range(2):
                sp.dma_start(w[b][:, :, :], w_src[:, :, C_GM + b * P:C_GM + (b + 1) * P]).then_inc(w_in[b], 16)
            with sp.Fori(0, NB // 2 - 1) as i:
                for b in range(2):
                    sp.wait_ge(wl_done, 2 * i + b + 1)
                    sp.dma_start(w[b][:, :, :], w_src[:, :, bass.ds(C_GM + (2 * i + b + 2) * P, P)]).then_inc(w_in[b], 16)
            for b, col in enumerate((C_HF, C_HI)):
                sp.wait_ge(wl_done, NB - 1 + b)
                sp.dma_start(w[b][:, :, :], w_src[:, :, col:col + P]).then_inc(w_in[b], 16)

        @block.gpsimd
        def _(pool):
            with pool.Fori(0, NB // 2) as i:
                for b in range(2):
                    pool.wait_ge(sg_done, 4 * i + 2 * b + 2)
                    settle(pool, g)
                    pool.dma_start(g.gates[bass.ds((2 * i + b) * P, P), :], sg[b][:, :]).then_inc(out_sem[b], 16)
            for b in range(2):
                pool.wait_ge(out_sem[b], 16 * (NB // 2))

        @block.scalar
        def _(act):
            act.wait_ge(bias_in, 16)

            def split(b, turn):
                act.wait_ge(w_in[b], 16 * turn + 16)
                act.activation(wh[b][:, :, :], w[b][:, :, :], ACT.Copy).then_inc(wh_done, 1)

            def gate(b, n):
                for q in range(2):
                    act.wait_ge(mm_done, 2 * n + q + 1)
                    settle(act, g)
                    act.activation(sg[b][:, q * 512:(q + 1) * 512], g.ps[:, (6 * b + q) * 512:(6 * b + q + 1) * 512],
                                   ACT.Sigmoid, bias=bias[:, bass.ds(n, 1)]).then_inc(sg_done, 1)

            split(0, 0)
            split(1, 0)
            gate(0, 0)
            act.wait_ge(mm_done, 2)
            split(0, 1)
            gate(1, 1)
            with act.Fori(0, NB // 2 - 2) as i:
                for b in range(2):
                    act.wait_ge(mm_done, 4 * i + 2 * b + 4)
                    split(1 - b, i + 1 + b)
                    act.wait_ge(out_sem[b], 16 * i + 16)
                    gate(b, 2 * i + b + 2)
            act.wait_ge(mm_done, 2 * (NB - 2))
            split(1, NB // 2 - 1)
            for b in range(2):
                act.wait_ge(out_sem[b], 16 * (NB // 2 - 1))
                gate(b, NB - 2 + b)
                split(b, NB // 2)

        @block.vector
        def _(dve):
            with dve.Fori(0, NB // 2 + 1) as i:
                for b in range(2):
                    dve.wait_ge(wh_done, 2 * i + b + 1)
                    dve.tensor_tensor(wl[b][:, :, :], w[b][:, :, :], wh[b][:, :, :].bitcast(F32),
                                      ALU.subtract).then_inc(wl_done, 1)

        @block.tensor
        def _(pe):
            def project(n, b):
                pe.wait_ge(wl_done, n + 1)
                for q in range(2):
                    for j in range(DK):
                        last = mm3(pe, g.ps[:, (6 * b + q) * 512:(6 * b + q + 1) * 512], wh[b][:, j, :], wl[b][:, j, :],
                                   g.uTh[:, j, q * 512:(q + 1) * 512], g.uTl[:, j, q * 512:(q + 1) * 512],
                                   j == 0, j == DK - 1)
                    last.then_inc(mm_done, 1)

            project(0, 0)
            project(1, 1)
            with pe.Fori(1, NB // 2) as i:
                for b in range(2):
                    pe.wait_ge(sg_done, 4 * i + 2 * b - 2)
                    project(2 * i + b, b)
            pe.wait_ge(sg_done, 2 * NB - 2)
            for b in range(2):
                pe.wait_ge(wl_done, NB + b + 1)
                for n, (col, size) in enumerate(PIECES):
                    for j in range(DK):
                        at = (HG_BANKS[b] + n) * 512
                        last = mm3(pe, g.ps[:, at:at + size], wh[b][:, j, :], wl[b][:, j, :],
                                   g.uTh[:, j, col:col + size], g.uTl[:, j, col:col + size], j == 0, j == DK - 1)
                    last.then_inc(mm_done, 1)


def phase_hgrn(nc, g):
    NCH = SEQ // CH
    with ExitStack() as ph:
        sb = lambda n, s, d=F32: ph.enter_context(nc.sbuf_tensor(n, s, d))
        sem = semaphores(nc, ph)
        w = [sb(f"h_w{b}", [P, DK, P]) for b in range(2)]
        wh = [sb(f"h_wh{b}", [P, DK, P], F32R) for b in range(2)]
        wl = [sb(f"h_wl{b}", [P, DK, P], F32R) for b in range(2)]
        lb_raw, lb, oml, hgain = sb("h_lb_raw", [P, 2, HG]), sb("h_lb", [P, HG]), sb("h_oml", [P, HG]), sb("h_hgain", [P, HG])
        lbd = sb("h_lbd", [P, HG])
        reset = sb("h_reset", [P, NT])
        causal = sb("h_causal", [P, P])
        f, k, lf, bb, d1 = sb("h_f", [P, NT]), sb("h_k", [P, NT]), sb("h_lf", [P, NT]), sb("h_b", [P, NT]), sb("h_d1", [P, SEQ])
        qs, ks, qd, kd = sb("h_qs", [P, SEQ]), sb("h_ks", [P, SEQ]), sb("h_qd", [P, SEQ]), sb("h_kd", [P, NT])
        q, vt, gt, ot = sb("h_q", [P, SEQ]), sb("h_vt", [P, NT]), sb("h_gt", [P, SEQ]), sb("h_ot", [P, SEQ])
        dec = sb("h_dec", [P, NCH])
        v = sb("h_v", [P, TT + 1, P])
        kdn = sb("h_kdn", [P, 2, P])
        kdm = sb("h_kdm", [META, P])
        at = sb("h_at", [P, 2, P])
        vb = [sb(f"h_vb{b}", [P, 4 * P]) for b in range(2)]
        S = sb("h_S", [P, 8, P])
        vb_zero, vb_ok, vb_ok2 = sem("h_vb_zero"), sem("h_vb_ok"), sem("h_vb_ok2")
        cst_in, cst, lb_ok = sem("h_cst_in"), sem("h_cst"), sem("h_lb_ok")
        w_in = [sem(f"h_w_in{b}") for b in range(2)]
        wh_done, wl_done, mm_done = sem("h_wh_done"), sem("h_wl_done"), sem("h_mm_done")
        sig_f, f_ok, lf_ok, b_ok, sig_q, e_ok, kd_ok = (sem("h_sig_f"), sem("h_f_ok"), sem("h_lf_ok"), sem("h_b_ok"),
                                                        sem("h_sig_q"), sem("h_e_ok"), sem("h_kd_ok"))
        q_ok, sig_g, g_ok, vt_ok, vtr, v_ok = (sem("h_q_ok"), sem("h_sig_g"), sem("h_g_ok"), sem("h_vt_ok"),
                                               sem("h_vtr"), sem("h_v_ok"))
        ktr, kdn_ok, s0_mm, s0_ok, a_mm, a_ok, kv_mm, s_ok, o_mm, o_ok = (
            sem("h_ktr"), sem("h_kdn_ok"), sem("h_s0_mm"), sem("h_s0_ok"), sem("h_a_mm"), sem("h_a_ok"),
            sem("h_kv_mm"), sem("h_s_ok"), sem("h_o_mm"), sem("h_o_ok"))
        sq_ok, ms_mm, rt_ok, on_ok, hi_ok, dv = (sem("h_sq_ok"), sem("h_ms_mm"), sem("h_rt_ok"), sem("h_on_ok"),
                                                 sem("h_hi_ok"), sem("h_dv"))
        block = ph.enter_context(nc.Block())
        w_src = g.w_in[0].rearrange("(p j) n -> p j n", j=DK)
        bank = lambda i, a=0, n=512: g.ps[:, i * 512 + a:i * 512 + a + n]
        pieces = PIECES
        COLS = [C_HF, C_HI, C_HQ, C_HG]
        FB, VB = HG_BANKS
        QB, GB = 0, 3
        AB, KVB, TB, OB = 0, 3, 6, [2, 5]
        chunked = lambda t: t[:, 0:SEQ].rearrange("p (c t) -> p c t", t=CH)

        @block.sync
        def _(sp):
            with nc.allow_non_contiguous_dma(reason="small vectors turned once"):
                sp.dma_start(lb_raw[:, :, :], g.lb_table.rearrange("a (h p) -> p a h", p=P)).then_inc(cst_in, 16)
                sp.dma_start(hgain[:, :], g.hg_norm[0].rearrange("(h p) -> p h", p=P)).then_inc(cst_in, 16)
            for r in range(2):
                sp.sem_inc(w_in[r], 16)

            def load(h, r, col):
                sp.wait_ge(wl_done, 4 * h + r + 1)
                sp.dma_start(w[r % 2][:, :, :], w_src[:, :, bass.ds(col, P)]).then_inc(w_in[r % 2], 16)

            with sp.Fori(0, HG - 1) as h:
                for r in range(4):
                    load(h, r, COLS[(r + 2) % 4] + h * P + (P if r >= 2 else 0))
            for r, col in enumerate((COLS[2] + (HG - 1) * P, COLS[3] + (HG - 1) * P, C_CQ, C_CQ + P)):
                load(HG - 1, r, col)

        @block.gpsimd
        def _(pool):
            pool.memset(reset[:, :], 1.0).then_inc(cst, 1)
            pool.memset(at[:, :, :], 0.0).then_inc(cst, 1)
            pool.wait_ge(cst, 2)
            pool.memset(reset[:, 0:SEQ:CH], 0.0).then_inc(cst, 1)
            pool.memset(reset[:, SEQ:SEQ + 1], 0.0).then_inc(cst, 1)
            cv = causal[:, :].rearrange("p (c t) -> p c t", t=CH)
            ov = g.ones[:, :].rearrange("p (c t) -> p c t", t=CH)
            pool.affine_select(out=cv, in_=ov, compare_op=ALU.is_ge, fill=0.0, base=0,
                               pattern=[[CH, P // CH], [1, CH]], channel_multiplier=-1).then_inc(cst, 1)
            pool.wait_ge(cst, 5)
            pool.affine_select(out=cv, in_=cv, compare_op=ALU.is_ge, fill=0.0, base=0,
                               pattern=[[-CH, P // CH], [0, CH]], channel_multiplier=1).then_inc(cst, 1)
            for b in range(2):
                pool.memset(vb[b][:, :], 0.0).then_inc(vb_zero, 1)
            pool.wait_ge(vb_zero, 2)

            def spread(h, t):
                for ci in range(2):
                    rows = slice(ci * CH, (ci + 1) * CH)
                    pool.tensor_copy(vb[t % 2][rows, ci * P:(ci + 1) * P], v[rows, t, :]).then_inc(vb_ok, 1)

            with pool.Fori(0, HG) as h:
                for t in range(TT):
                    pool.wait_ge(v_ok, 3 * h + 2)
                    if t >= 2:
                        pool.wait_ge(kv_mm, TT * h + t - 1)
                    settle(pool, g)
                    spread(h, t)

        @block.scalar
        def _(act):
            def split(b, n_in, n_mm):
                act.wait_ge(mm_done, n_mm)
                act.wait_ge(w_in[b], n_in)
                act.activation(wh[b][:, :, :], w[b][:, :, :], ACT.Copy).then_inc(wh_done, 1)

            act.sem_inc(wh_done, 2)
            act.wait_ge(cst_in, 32)
            act.wait_ge(dv, 1)
            act.activation(lb[:, :], lbd[:, :], ACT.Sigmoid).then_inc(lb_ok, 1)
            with act.Fori(0, HG) as h:
                w0 = 32 * h + 32
                split(0, w0, 10 * h + 3)
                for n, (c, m) in enumerate(pieces):
                    act.wait_ge(mm_done, 10 * h + n + 1)
                    act.activation(f[:, c:c + m], bank(FB + n, 0, m), ACT.Sigmoid).then_inc(sig_f, 1)
                act.wait_ge(f_ok, h + 1)
                act.activation(lf[:, :], f[:, :], ACT.Ln).then_inc(lf_ok, 1)
                for n, (c, m) in enumerate(pieces):
                    act.wait_ge(mm_done, 10 * h + n + 4)
                    act.activation(vt[:, c:c + m], bank(VB + n, 0, m), ACT.Copy).then_inc(vt_ok, 1)
                split(1, w0, 10 * h + 6)
                act.wait_ge(b_ok, 3 * h + 3)
                act.activation(qs[:, :], d1[:, :], ACT.Exp).then_inc(e_ok, 1)
                act.activation(ks[:, :], d1[:, :], ACT.Exp, scale=-1.0).then_inc(e_ok, 1)
                act.activation(qd[:, :], bb[:, 0:SEQ], ACT.Exp).then_inc(e_ok, 1)
                act.activation(kd[:, :], lf[:, :], ACT.Exp).then_inc(e_ok, 1)
                act.activation(dec[:, :], bb[:, CH - 1:SEQ:CH], ACT.Exp).then_inc(e_ok, 1)
                for n in range(2):
                    act.wait_ge(mm_done, 10 * h + n + 7)
                    act.activation(q[:, n * 512:(n + 1) * 512], bank(QB + n), ACT.Sigmoid).then_inc(sig_q, 1)
                split(0, w0 + 16, 10 * h + 8)
                for n in range(2):
                    act.wait_ge(vtr, 3 * h + n + 1)
                    act.activation(v[:, 4 * n:4 * n + 4, :], bank(6 + n).rearrange("p (t c) -> p t c", t=4),
                                   ACT.Copy).then_inc(v_ok, 1)
                act.wait_ge(vtr, 3 * h + 3)
                act.activation(v[0:META, TT, :], g.ps[0:META, 2 * 512:2 * 512 + P], ACT.Copy).then_inc(v_ok, 1)
                for n in range(2):
                    act.wait_ge(mm_done, 10 * h + n + 9)
                    act.activation(gt[:, n * 512:(n + 1) * 512], bank(GB + n), ACT.Sigmoid).then_inc(sig_g, 1)
                split(1, w0 + 16, 10 * h + 10)
                act.wait_ge(ktr, 9 * h + 1)
                act.activation(kdm[:, :], g.ps[0:META, 2 * 512:2 * 512 + P], ACT.Copy).then_inc(kdn_ok, 1)
                act.wait_ge(s0_mm, h + 1)
                act.activation(S[:, 0, :], bank(5, 0, P), ACT.Copy).then_inc(s0_ok, 1)

                def kd_rows(t):
                    act.wait_ge(ktr, 9 * h + t + 2)
                    act.activation(kdn[:, t % 2, :], bank(TB + t % 2, 0, P), ACT.Copy).then_inc(kdn_ok, 1)

                def spread(t):
                    for ci in (2, 3):
                        rows = slice(ci * CH, (ci + 1) * CH)
                        act.activation(vb[t % 2][rows, ci * P:(ci + 1) * P], v[rows, t, :], ACT.Copy).then_inc(vb_ok2, 1)

                act.wait_ge(v_ok, 3 * h + 2)
                act.wait_ge(vb_zero, 2)
                spread(0)
                spread(1)
                kd_rows(0)
                kd_rows(1)
                for t in range(TT):
                    if t + 2 < TT:
                        kd_rows(t + 2)
                        act.wait_ge(kv_mm, TT * h + t + 1)
                        spread(t + 2)
                    act.wait_ge(o_mm, TT * h + t + 1)
                    act.activation(ot[:, t * P:(t + 1) * P], bank(OB[t % 2], 0, P), ACT.Copy).then_inc(o_ok, 1)
                act.wait_ge(o_ok, TT * h + TT)
                act.activation(d1[:, :], ot[:, :], ACT.Square).then_inc(sq_ok, 1)
                for n in range(2):
                    act.wait_ge(ms_mm, 2 * h + n + 1)
                    act.activation(qs[:, n * 512:(n + 1) * 512], bank(TB + n), ACT.Sqrt, scale=1.0 / P,
                                   bias=g.eps[:, :]).then_inc(rt_ok, 1)
                act.wait_ge(on_ok, h + 1)
                settle(act, g)
                act.activation(g.ohTh[:, bass.ds(h, 1), :], ot[:, :].rearrange("p (a t) -> p a t", a=1),
                               ACT.Copy).then_inc(hi_ok, 1)

        @block.vector
        def _(dve):
            c = Steps(dve, dv)

            def low(b, n):
                dve.wait_ge(wh_done, n)
                dve.tensor_tensor(wl[b][:, :, :], w[b][:, :, :], wh[b][:, :, :].bitcast(F32),
                                  ALU.subtract).then_inc(wl_done, 1)

            dve.sem_inc(wl_done, 2)
            dve.wait_ge(cst_in, 32)
            c.link(dve.tensor_tensor(lbd[:, :], lb_raw[:, 0, :], lb_raw[:, 1, :], ALU.subtract))
            dve.wait_ge(cst, 6)
            dve.wait_ge(lb_ok, 1)
            c.link(dve.tensor_scalar(oml[:, :], lb[:, :], -1.0, 1.0, ALU.mult, ALU.add))
            with dve.Fori(0, HG) as h:
                c.enter(h, 8)
                low(0, 4 * h + 3)
                dve.wait_ge(sig_f, 3 * h + 3)
                c.link(dve.tensor_scalar(f[:, :], f[:, :], oml[:, bass.ds(h, 1)], lb[:, bass.ds(h, 1)], ALU.mult, ALU.add))
                dve.tensor_scalar(k[:, :], f[:, :], -1.0, 1.0, ALU.mult, ALU.add).then_inc(f_ok, 1)
                dve.wait_ge(lf_ok, h + 1)
                dve.tensor_tensor_scan(bb[:, :], reset[:, :], lf[:, :], 0.0, ALU.mult, ALU.add).then_inc(b_ok, 1)
                dve.wait_ge(b_ok, 3 * h + 1)
                bv, dv1, dv2 = chunked(bb), chunked(d1), chunked(lf)
                c.mark(dve.tensor_tensor(dv1, bv, bv[:, :, CH // 2 - 1:CH // 2].to_broadcast([P, NCH, CH]), ALU.subtract))
                dve.tensor_tensor(dv2, bv[:, :, CH - 1:CH].to_broadcast([P, NCH, CH]), bv, ALU.subtract).then_inc(b_ok, 1)
                dve.tensor_tensor(lf[:, SEQ:NT], bb[:, NT - 1:NT].to_broadcast([P, META]), bb[:, SEQ:NT],
                                  ALU.subtract).then_inc(b_ok, 1)
                low(1, 4 * h + 4)
                for n in range(2):
                    dve.wait_ge(sig_q, 2 * h + n + 1)
                    dve.tensor_tensor(q[:, n * 512:(n + 1) * 512], q[:, n * 512:(n + 1) * 512], bank(QB + n),
                                      ALU.mult).then_inc(q_ok, 1)
                low(0, 4 * h + 5)
                dve.wait_ge(q_ok, 2 * h + 2)
                dve.wait_ge(e_ok, 5 * h + 5)
                c.mark(dve.tensor_tensor(qs[:, :], qs[:, :], q[:, :], ALU.mult))
                c.mark(dve.tensor_tensor(ks[:, :], ks[:, :], k[:, 0:SEQ], ALU.mult))
                c.mark(dve.tensor_tensor(qd[:, :], qd[:, :], q[:, :], ALU.mult))
                dve.tensor_tensor(kd[:, :], kd[:, :], k[:, :], ALU.mult).then_inc(kd_ok, 1)
                for n in range(2):
                    dve.wait_ge(sig_g, 2 * h + n + 1)
                    dve.scalar_tensor_tensor(out=gt[:, n * 512:(n + 1) * 512], in0=gt[:, n * 512:(n + 1) * 512],
                                             scalar=hgain[:, bass.ds(h, 1)], in1=bank(GB + n),
                                             op0=ALU.mult, op1=ALU.mult).then_inc(g_ok, 1)
                low(1, 4 * h + 6)
                dve.wait_ge(s0_ok, h + 1)

                def scores(t):
                    dve.wait_ge(a_mm, TT * h + t + 1)
                    settle(dve, g)
                    dve.copy_predicated(at[:, t % 2, :], causal[:, :].bitcast(U32), bank(AB + t % 2, 0, P)).then_inc(a_ok, 1)

                scores(0)
                for t in range(TT):
                    dve.wait_ge(kv_mm, TT * h + t + 1)
                    for ci in range(4):
                        n = 4 * t + ci
                        if n == 4 * TT - 1:
                            break
                        if n:
                            dve.wait_ge(s_ok, (4 * TT - 1) * h + n)
                        if ci == 3 and t >= 1:
                            dve.wait_ge(o_mm, TT * h + t)
                        dve.scalar_tensor_tensor(out=S[:, (n + 1) % 8, :], in0=S[:, n % 8, :], scalar=dec[:, n:n + 1],
                                                 in1=bank(KVB + t % 2, ci * P, P), op0=ALU.mult,
                                                 op1=ALU.add).then_inc(s_ok, 1)
                    if t + 1 < TT:
                        scores(t + 1)
                for n in range(2):
                    dve.wait_ge(rt_ok, 2 * h + n + 1)
                c.link(dve.reciprocal(qs[:, :], qs[:, :]))
                dve.wait_ge(o_ok, TT * h + TT)
                c.link(dve.tensor_tensor(ot[:, :], ot[:, :], qs[:, :], ALU.mult))
                dve.wait_ge(g_ok, 2 * h + 2)
                dve.tensor_tensor(ot[:, :], ot[:, :], gt[:, :], ALU.mult).then_inc(on_ok, 1)
                dve.wait_ge(hi_ok, h + 1)
                c.mark(dve.tensor_tensor(g.ohTl[:, bass.ds(h, 1), :], ot[:, :].rearrange("p (a t) -> p a t", a=1),
                                         g.ohTh[:, bass.ds(h, 1), :].bitcast(F32), ALU.subtract))
                c.leave(HG)

        @block.tensor
        def _(pe):
            def project(h, r, base, cols):
                pe.wait_ge(wl_done, 4 * h + r + 1)
                for n, (col, m) in enumerate(cols):
                    for j in range(DK):
                        last = mm3(pe, bank(base + n, 0, m), wh[r % 2][:, j, :], wl[r % 2][:, j, :],
                                   g.uTh[:, j, col:col + m], g.uTl[:, j, col:col + m], j == 0, j == DK - 1)
                    last.then_inc(mm_done, 1)

            def head(h, first):
                if not first:
                    pe.wait_ge(a_ok, TT * h)
                    pe.wait_ge(o_ok, TT * h)
                    project(h, 0, FB, pieces)
                if not first:
                    pe.wait_ge(s_ok, (4 * TT - 1) * h)
                    project(h, 1, VB, pieces)
                pe.wait_ge(sig_f, 3 * h + 3)
                project(h, 2, QB, pieces[:2])
                pe.wait_ge(vt_ok, 3 * h + 3)
                if not first:
                    pe.wait_ge(rt_ok, 2 * h)
                for n in range(2):
                    for t in range(4):
                        tt = 4 * n + t
                        last = pe.transpose(bank(6 + n, t * P, P), vt[:, tt * P:(tt + 1) * P], g.ident[:, :])
                    last.then_inc(vtr, 1)
                pe.transpose(g.ps[0:META, 2 * 512:2 * 512 + P], vt[:, SEQ:NT], g.ident[:, :]).then_inc(vtr, 1)
                project(h, 3, GB, pieces[:2])
                pe.wait_ge(kd_ok, h + 1)
                pe.wait_ge(v_ok, 3 * h + 3)
                pe.transpose(g.ps[0:META, 2 * 512:2 * 512 + P], kd[:, SEQ:NT], g.ident[:, :]).then_inc(ktr, 1)
                pe.wait_ge(kdn_ok, 9 * h + 1)
                pe.matmul(bank(5, 0, P), kdm[:, :], v[0:META, TT, :], start=True, stop=True).then_inc(s0_mm, 1)
                pe.wait_ge(g_ok, 2 * h + 2)
                pe.wait_ge(q_ok, 2 * h + 2)

                def turn(t):
                    if t >= 2:
                        pe.wait_ge(kdn_ok, 9 * h + t)
                    pe.transpose(bank(TB + t % 2, 0, P), kd[:, t * P:(t + 1) * P], g.ident[:, :]).then_inc(ktr, 1)

                def ahead(t):
                    if t >= 2:
                        pe.wait_ge(a_ok, TT * h + t - 1)
                        pe.wait_ge(s_ok, (4 * TT - 1) * h + 4 * (t - 1))
                    pe.matmul(bank(AB + t % 2, 0, P), ks[:, t * P:(t + 1) * P], qs[:, t * P:(t + 1) * P],
                              start=True, stop=True).then_inc(a_mm, 1)
                    pe.wait_ge(kdn_ok, 9 * h + t + 2)
                    pe.wait_ge(vb_ok, 2 * (TT * h + t + 1))
                    pe.wait_ge(vb_ok2, 2 * (TT * h + t + 1))
                    pe.matmul(bank(KVB + t % 2), kdn[:, t % 2, :], vb[t % 2][:, :], start=True, stop=True).then_inc(kv_mm, 1)

                turn(0)
                turn(1)
                ahead(0)
                pe.wait_ge(s0_ok, h + 1)
                for t in range(TT):
                    if t + 2 < TT:
                        turn(t + 2)
                    if t + 1 < TT:
                        ahead(t + 1)
                    pe.wait_ge(a_ok, TT * h + t + 1)
                    if t >= 2:
                        pe.wait_ge(o_ok, TT * h + t - 1)
                    pe.matmul(bank(OB[t % 2], 0, P), v[:, t, :], at[:, t % 2, :], start=True, stop=False)
                    for ci in range(4):
                        n = 4 * t + ci
                        if n:
                            pe.wait_ge(s_ok, (4 * TT - 1) * h + n)
                        last = pe.matmul(bank(OB[t % 2], ci * CH, CH), S[:, n % 8, :], qd[:, n * CH:(n + 1) * CH],
                                         start=False, stop=ci == 3)
                    last.then_inc(o_mm, 1)
                pe.wait_ge(sq_ok, h + 1)
                for n in range(2):
                    pe.matmul(bank(TB + n), g.ones[:, :], d1[:, n * 512:(n + 1) * 512],
                              start=True, stop=True).then_inc(ms_mm, 1)

            pe.sem_inc(mm_done, 2 * len(pieces))
            head(0, True)
            with pe.Fori(1, HG) as h:
                head(h, False)
            pe.wait_ge(a_ok, TT * HG)
            project(HG, 0, LATENT_BANKS[0], pieces[:2])
            pe.wait_ge(s_ok, (4 * TT - 1) * HG)
            project(HG, 1, LATENT_BANKS[1], pieces[:2])


def phase_latents(nc, g):
    with ExitStack() as ph:
        sb = lambda n, s, d=F32: ph.enter_context(nc.sbuf_tensor(n, s, d))
        sem = semaphores(nc, ph)
        w = [sb(f"l_w{b}", [P, DK, P]) for b in range(2)]
        wh = [sb(f"l_wh{b}", [P, DK, P], F32R) for b in range(2)]
        wl = [sb(f"l_wl{b}", [P, DK, P], F32R) for b in range(2)]
        raw = sb("l_raw", [P, 5, NT])
        sq, rt, swapped = sb("l_sq", [P, NT]), sb("l_rt", [P, NT]), sb("l_swapped", [QH, NT])
        gain = sb("l_gain", [P, 5])
        cst_in = sem("l_cst_in")
        w_in = [sem(f"l_w_in{b}") for b in range(2)]
        wh_done, wl_done, mm_done, raw_ok, kpe_ok = (sem("l_wh_done"), sem("l_wl_done"), sem("l_mm_done"),
                                                     sem("l_raw_ok"), sem("l_kpe_ok"))
        sq_ok, ms_mm, rt_ok, n_ok, hi_ok, lo_ok, dv = (sem("l_sq_ok"), sem("l_ms_mm"), sem("l_rt_ok"), sem("l_n_ok"),
                                                       sem("l_hi_ok"), sem("l_lo_ok"), sem("l_dv"))
        block = ph.enter_context(nc.Block())
        w_src = g.w_in[0].rearrange("(p j) n -> p j n", j=DK)
        bank = lambda i, a=0, n=512: g.ps[:, i * 512 + a:i * 512 + a + n]
        real, full = [(0, 512), (512, 512)], [(0, 512), (512, 512), (SEQ, META)]
        BLOCKS = [(C_CQ + i * P, P, real) for i in range(3)] + [(C_CKV + i * P, P, full) for i in range(2)] \
            + [(C_KPE - NOPE, QH, full)]
        NORMS = [(range(0, 3), SEQ, QL, g.cqh, g.cql, real), (range(3, 5), NT, KVL, g.ckh, g.ckl, full)]
        mm_before = [sum(len(b[2]) for b in BLOCKS[:n]) for n in range(7)]
        fbank = lambda n: LATENT_BANKS[n % 2]

        @block.sync
        def _(sp):
            def load_constants():
                with nc.allow_non_contiguous_dma(reason="small vectors turned once"):
                    sp.dma_start(gain[:, 0:3], g.q_norm[0].rearrange("(j p) -> p j", p=P)).then_inc(cst_in, 16)
                    sp.dma_start(gain[:, 3:5], g.kv_norm[0].rearrange("(j p) -> p j", p=P)).then_inc(cst_in, 16)
                sp.dma_start(g.cos[NOPE:QH, :], g.rope_cos).then_inc(cst_in, 16)
                sp.dma_start(g.sin[NOPE:QH, :], g.rope_sin).then_inc(cst_in, 16)

            for n, (col, m, _) in enumerate(BLOCKS):
                if n < 2:
                    continue
                if n >= 4:
                    sp.wait_ge(wl_done, n - 1)
                sp.dma_start(w[n % 2][:, :, 0:m], w_src[:, :, col:col + m]).then_inc(w_in[n % 2], 16)
                if n == 3:
                    load_constants()
            sp.wait_ge(cst_in, 64)

        @block.scalar
        def _(act):
            def split(n):
                if n >= 4:
                    act.wait_ge(mm_done, mm_before[n - 1])
                m = BLOCKS[n][1]
                act.wait_ge(w_in[n % 2], 16 * (n // 2))
                act.activation(wh[n % 2][:, :, 0:m], w[n % 2][:, :, 0:m], ACT.Copy).then_inc(wh_done, 1)

            act.sem_inc(wh_done, 2)
            def evac(n):
                for p, (c, m) in enumerate(BLOCKS[n][2]):
                    act.wait_ge(mm_done, mm_before[n] + p + 1)
                    act.activation(raw[:, n, c:c + m], bank(fbank(n) + p, 0, m), ACT.Copy).then_inc(raw_ok, 1)
                if n + 2 < 6:
                    split(n + 2)

            def norm(z, done):
                js, width, size, hi, _, cols = NORMS[z]
                for p, (c, m) in enumerate(cols):
                    act.wait_ge(ms_mm, done + p + 1)
                    act.activation(rt[:, c:c + m], bank([6, 7, 2][p], 0, m), ACT.Sqrt, scale=1.0 / size,
                                   bias=g.eps[:, :]).then_inc(rt_ok, 1)
                for j in js:
                    act.wait_ge(n_ok, j + 1)
                    act.activation(hi[:, j - js[0], 0:width], raw[:, j, 0:width], ACT.Copy).then_inc(hi_ok, 1)

            for n in range(4):
                evac(n)
            norm(0, 0)
            evac(4)
            norm(1, len(real))

        @block.vector
        def _(dve):
            v = Steps(dve, dv)

            def low(n):
                dve.wait_ge(wh_done, n + 1)
                m = BLOCKS[n][1]
                dve.tensor_tensor(wl[n % 2][:, :, 0:m], w[n % 2][:, :, 0:m], wh[n % 2][:, :, 0:m].bitcast(F32),
                                  ALU.subtract).then_inc(wl_done, 1)

            def squares(js, width, z):
                for j in js:
                    dve.wait_ge(raw_ok, mm_before[j + 1])
                    x = raw[:, j, 0:width]
                    if j == js[0]:
                        v.link(dve.tensor_tensor(sq[:, 0:width], x, x, ALU.mult))
                    else:
                        v.link(dve.tensor_tensor(rt[:, 0:width], x, x, ALU.mult))
                        ins = dve.tensor_tensor(sq[:, 0:width], sq[:, 0:width], rt[:, 0:width], ALU.add)
                        if j == js[-1]:
                            ins.then_inc(sq_ok, 1)
                        else:
                            v.link(ins)
                    if j == 2:
                        low(4)

            def normed(z):
                js, width, _, hi, lo, cols = NORMS[z]
                dve.wait_ge(rt_ok, 2 if z == 0 else 5)
                v.link(dve.reciprocal(rt[:, 0:width], rt[:, 0:width]))
                for j in js:
                    dve.scalar_tensor_tensor(out=raw[:, j, 0:width], in0=raw[:, j, 0:width], scalar=gain[:, j:j + 1],
                                             in1=rt[:, 0:width], op0=ALU.mult, op1=ALU.mult).then_inc(n_ok, 1)
                for j in js:
                    dve.wait_ge(hi_ok, j + 1)
                    dve.tensor_tensor(lo[:, j - js[0], 0:width], raw[:, j, 0:width],
                                      hi[:, j - js[0], 0:width].bitcast(F32), ALU.subtract).then_inc(lo_ok, 1)

            dve.sem_inc(wl_done, 2)
            low(2)
            low(3)
            dve.wait_ge(cst_in, 64)
            squares(range(0, 3), SEQ, 0)
            low(5)
            normed(0)
            squares(range(3, 5), NT, 1)
            rows = slice(NOPE, QH)
            for p, (c, m) in enumerate(full):
                dve.wait_ge(mm_done, mm_before[5] + p + 1)
                b = g.ps[rows, (3 + p) * 512:(3 + p) * 512 + m]
                v.link(dve.stream_shuffle(out=swapped[rows, c:c + m], in_=b, mask=SWAP))
                dve.tensor_tensor(g.kpe[rows, c:c + m], b, g.cos[rows, c:c + m], ALU.mult).then_inc(kpe_ok, 1)
            normed(1)
            dve.wait_ge(kpe_ok, 3)
            v.link(dve.tensor_tensor(swapped[rows, :], swapped[rows, :], g.sin[rows, :], ALU.mult))
            v.link(dve.tensor_tensor(g.kpe[rows, :], g.kpe[rows, :], swapped[rows, :], ALU.add))

        @block.tensor
        def _(pe):
            def project(n):
                pe.wait_ge(wl_done, n + 1)
                if n >= 2:
                    pe.wait_ge(raw_ok, mm_before[n - 1])
                m = BLOCKS[n][1]
                for p, (col, k) in enumerate(BLOCKS[n][2]):
                    for j in range(DK):
                        last = mm3(pe, g.ps[0:m, (fbank(n) + p) * 512:(fbank(n) + p) * 512 + k], wh[n % 2][:, j, 0:m],
                                   wl[n % 2][:, j, 0:m], g.uTh[:, j, col:col + k], g.uTl[:, j, col:col + k],
                                   j == 0, j == DK - 1)
                    last.then_inc(mm_done, 1)

            def sums(z, cols):
                pe.wait_ge(sq_ok, z + 1)
                for p, (c, m) in enumerate(cols):
                    pe.matmul(bank([6, 7, 2][p], 0, m), g.ones[:, :], sq[:, c:c + m], start=True, stop=True).then_inc(ms_mm, 1)

            pe.sem_inc(mm_done, mm_before[2])
            for n in range(2, 4):
                project(n)
            sums(0, real)
            project(4)
            pe.wait_ge(raw_ok, mm_before[4])
            project(5)
            pe.wait_ge(rt_ok, 2)
            pe.wait_ge(raw_ok, mm_before[5])
            sums(1, full)


def phase_heads(nc, g):
    with ExitStack() as ph:
        sb = lambda n, s, d=F32: ph.enter_context(nc.sbuf_tensor(n, s, d))
        sem = semaphores(nc, ph)
        wq = [sb(f"p_wq{b}", [P, 3, QH]) for b in range(2)]
        wkv = [sb(f"p_wkv{b}", [P, 2, P]) for b in range(2)]
        wqh = [sb(f"p_wqh{b}", [P, 3, QH], F32R) for b in range(2)]
        wql = [sb(f"p_wql{b}", [P, 3, QH], F32R) for b in range(2)]
        wkh = [sb(f"p_wkh{b}", [P, 2, P], F32R) for b in range(2)]
        wkl = [sb(f"p_wkl{b}", [P, 2, P], F32R) for b in range(2)]
        KVT = [sb(f"p_KVT{b}", [P, NT]) for b in range(2)]
        rot = sb("p_rot", [QH, SEQ])
        w_in = [sem(f"p_w_in{b}") for b in range(2)]
        k_out = [sem(f"p_k_out{b}") for b in range(2)]
        kpe_out = sem("p_kpe_out")
        wh_ok, wl_ok, q_mm, kv_mm = sem("p_wh_ok"), sem("p_wl_ok"), sem("p_q_mm"), sem("p_kv_mm")
        qn_ok, qp_ok, kvt_ok, v_tr, v_ok, dv = (sem("p_qn_ok"), sem("p_qp_ok"), sem("p_kvt_ok"), sem("p_v_tr"),
                                                sem("p_v_ok"), sem("p_dv"))
        block = ph.enter_context(nc.Block())
        bank = lambda i, a=0, n=512: g.ps[:, i * 512 + a:i * 512 + a + n]
        pieces = PIECES
        Q_BANK, KV_BANK, V_BANK = 0, 2, 5
        q_src = g.w_uq[0].rearrange("(j p) n -> p j n", p=P)
        kv_src = g.w_ukv[0].rearrange("(j p) n -> p j n", p=P)

        def each_head(eng, body):
            body(0, 0, 0)
            body(1, 0, 1)
            with eng.Fori(1, HEADS // 2 - 1) as n:
                for b in range(2):
                    body(2 * n + b, n, b)
            body(HEADS - 2, HEADS // 2 - 1, 0)
            body(HEADS - 1, HEADS // 2 - 1, 1)

        has = lambda h, d: not isinstance(h, int) or 0 <= h + d < HEADS

        @block.sync
        def _(sp):
            def load(h, b):
                sp.dma_start(wq[b][:, :, :], q_src[:, :, bass.ds(h * QH, QH)]).then_inc(w_in[b], 16)
                sp.dma_start(wkv[b][:, :, :], kv_src[:, :, bass.ds(h * P, P)]).then_inc(w_in[b], 16)

            load(0, 0)
            load(1, 1)
            with sp.Fori(0, HEADS) as h:
                sp.dma_start(g.KT[NOPE:QH, bass.ds(h, 1), :], g.kpe[NOPE:QH, :].rearrange("p (a t) -> p a t", a=1)
                             ).then_inc(kpe_out, 16)

            def body(h, n, b):
                if has(h, 2):
                    sp.wait_ge(wl_ok, 2 * h + 2)
                    load(h + 2, b)
                sp.wait_ge(kvt_ok, 3 * h + 3)
                sp.dma_start(g.KT[0:NOPE, bass.ds(h, 1), :], KVT[b][0:NOPE, :].rearrange("p (a t) -> p a t", a=1)
                             ).then_inc(k_out[b], 16)

            each_head(sp, body)
            sp.wait_ge(kpe_out, 16 * HEADS)
            for b in range(2):
                sp.wait_ge(k_out[b], 16 * (HEADS // 2))

        @block.scalar
        def _(act):
            def split(h, n, b):
                if has(h, -2):
                    act.wait_ge(kv_mm, 3 * h - 3)
                act.wait_ge(w_in[b], 32 * n + 32)
                act.activation(wqh[b][:, :, :], wq[b][:, :, :], ACT.Copy).then_inc(wh_ok, 1)
                act.activation(wkh[b][:, :, :], wkv[b][:, :, :], ACT.Copy).then_inc(wh_ok, 1)

            def values(h, n, b):
                cols = slice(0, VD) if b == 0 else slice(VD, VD + P)
                src = slice(NOPE, P) if b == 0 else slice(0, P)
                for x in range(2):
                    act.wait_ge(v_tr, 3 * h + x + 1)
                    settle(act, g)
                    act.activation(g.V[:, bass.ds(n, 1), 4 * x:4 * x + 4, cols].rearrange("p a t c -> p (a t) c"),
                                   bank(V_BANK + x).rearrange("p (t c) -> p t c", t=4)[:, :, src], ACT.Copy).then_inc(v_ok, 1)
                act.wait_ge(v_tr, 3 * h + 3)
                settle(act, g)
                act.activation(g.V[0:META, bass.ds(n, 1), TT, cols].rearrange("p a c -> p (a c)"),
                               g.ps[0:META, (V_BANK + 2) * 512 + src.start:(V_BANK + 2) * 512 + P],
                               ACT.Copy).then_inc(v_ok, 1)

            def body(h, n, b):
                if has(h, 1):
                    split(h + 1, n + b, 1 - b)
                for x in range(2):
                    act.wait_ge(q_mm, 2 * h + x + 1)
                    settle(act, g)
                    act.activation(g.QT[0:NOPE, bass.ds(h, 1), x * 512:(x + 1) * 512].rearrange("p a t -> p (a t)"),
                                   g.ps[0:NOPE, (Q_BANK + x) * 512:(Q_BANK + x + 1) * 512], ACT.Copy,
                                   scale=SCALE).then_inc(qn_ok, 1)
                if has(h, -1):
                    values(h - 1, n - 1 + b, 1 - b)
                if has(h, -2):
                    act.wait_ge(k_out[b], 16 * n)
                for x, (c, m) in enumerate(pieces):
                    act.wait_ge(kv_mm, 3 * h + x + 1)
                    act.activation(KVT[b][:, c:c + m], bank(KV_BANK + x, 0, m), ACT.Copy).then_inc(kvt_ok, 1)

            split(0, 0, 0)
            each_head(act, body)
            values(HEADS - 1, HEADS // 2 - 1, 1)

        @block.vector
        def _(dve):
            c = Steps(dve, dv)
            rows = slice(NOPE, QH)

            def low(h, b):
                for x, (raw, hi, lo) in enumerate([(wq, wqh, wql), (wkv, wkh, wkl)]):
                    dve.wait_ge(wh_ok, 2 * h + x + 1)
                    dve.tensor_tensor(lo[b][:, :, :], raw[b][:, :, :], hi[b][:, :, :].bitcast(F32),
                                      ALU.subtract).then_inc(wl_ok, 1)

            def body(h, n, b):
                if has(h, 1):
                    low(h + 1, 1 - b)
                for x in range(2):
                    dve.wait_ge(qn_ok, 2 * h + x + 1)
                    src = g.ps[rows, (Q_BANK + x) * 512:(Q_BANK + x + 1) * 512]
                    cols = slice(x * 512, (x + 1) * 512)
                    dst = g.QT[rows, bass.ds(h, 1), cols].rearrange("p a t -> p (a t)")
                    settle(dve, g)
                    c.mark(dve.stream_shuffle(out=rot[rows, cols], in_=src, mask=SWAP))
                    ins = dve.scalar_tensor_tensor(out=dst, in0=src, scalar=SCALE, in1=g.cos[rows, cols],
                                                   op0=ALU.mult, op1=ALU.mult)
                    if x == 0:
                        c.mark(ins)
                    else:
                        c.link(ins)
                dve.sem_inc(qp_ok, 1)
                c.link(dve.scalar_tensor_tensor(out=rot[rows, :], in0=rot[rows, :], scalar=SCALE, in1=g.sin[rows, 0:SEQ],
                                                op0=ALU.mult, op1=ALU.mult))
                dst = g.QT[rows, bass.ds(h, 1), :].rearrange("p a t -> p (a t)")
                c.link(dve.tensor_tensor(dst, dst, rot[rows, :], ALU.add))

            low(0, 0)
            per = 6
            body(0, 0, 0)
            body(1, 0, 1)
            with dve.Fori(1, HEADS // 2 - 1) as n:
                c.enter(n - 1, 2 * per)
                for b in range(2):
                    body(2 * n + b, n, b)
                c.leave(HEADS // 2 - 2)
            body(HEADS - 2, HEADS // 2 - 1, 0)
            body(HEADS - 1, HEADS // 2 - 1, 1)

        @block.tensor
        def _(pe):
            def values(h, b):
                pe.wait_ge(kvt_ok, 3 * h + 3)
                wait(pe, v_ok, 3 * h)
                for x in range(2):
                    for t in range(4):
                        last = pe.transpose(bank(V_BANK + x, t * P, P), KVT[b][:, (4 * x + t) * P:(4 * x + t + 1) * P], g.ident[:, :])
                    last.then_inc(v_tr, 1)
                pe.transpose(g.ps[0:META, (V_BANK + 2) * 512:(V_BANK + 2) * 512 + P], KVT[b][:, SEQ:NT], g.ident[:, :]).then_inc(v_tr, 1)

            def body(h, n, b):
                pe.wait_ge(wl_ok, 2 * h + 2)
                wait(pe, qn_ok, 2 * h)
                wait(pe, qp_ok, h)
                for x in range(2):
                    for j in range(3):
                        last = mm3(pe, g.ps[0:QH, (Q_BANK + x) * 512:(Q_BANK + x + 1) * 512], wqh[b][:, j, :], wql[b][:, j, :],
                                   g.cqh[:, j, x * 512:(x + 1) * 512], g.cql[:, j, x * 512:(x + 1) * 512], j == 0, j == 2)
                    last.then_inc(q_mm, 1)
                if has(h, -1):
                    values(h - 1, 1 - b)
                for x, (col, m) in enumerate(pieces):
                    for j in range(2):
                        last = mm3(pe, bank(KV_BANK + x, 0, m), wkh[b][:, j, :], wkl[b][:, j, :],
                                   g.ckh[:, j, col:col + m], g.ckl[:, j, col:col + m], j == 0, j == 1)
                    last.then_inc(kv_mm, 1)

            each_head(pe, body)
            values(HEADS - 1, 1)


def phase_attention(nc, g):
    with ExitStack() as ph:
        sb = lambda n, s, d=F32: ph.enter_context(nc.sbuf_tensor(n, s, d))
        sem = semaphores(nc, ph)
        Q = [sb(f"t_Q{b}", [QH, SEQ]) for b in range(2)]
        V = [sb("t_V0", [P, TT + 1, VD]), sb("t_V1", [P, TT + 1, P])]
        pr = [sb(f"t_p{b}", [P, NT]) for b in range(2)]
        PT = [sb(f"t_PT{b}", [P, TT + 1, P]) for b in range(2)]
        mask = sb("t_mask", [P, P])
        diag = [sb(f"t_diag{b}", [P, P]) for b in range(2)]
        negmax, total, inv = sb("t_negmax", [P, 2]), sb("t_total", [P, 2]), sb("t_inv", [P, 2])
        cst = sem("t_cst")
        q_in = [sem(f"t_q_in{b}") for b in range(2)]
        v_in = [sem(f"t_v_in{b}") for b in range(2)]
        s_mm, mx_ok, exp_ok, dg_ok, p_tr, pa_ok, pd_ok, o_mm, oh_ok, ol_ok, dv = (
            sem("t_s_mm"), sem("t_mx_ok"), sem("t_exp_ok"), sem("t_dg_ok"), sem("t_p_tr"), sem("t_pa_ok"), sem("t_pd_ok"),
            sem("t_o_mm"), sem("t_oh_ok"), sem("t_ol_ok"), sem("t_dv"))
        block = ph.enter_context(nc.Block())
        bank = lambda i, a=0, n=512: g.ps[:, i * 512 + a:i * 512 + a + n]
        tiles = lambda i: list(range(i + 1)) + [TT]
        groups = lambda i: [tiles(i)[a:a + 4] for a in range(0, i + 2, 4)]
        before = [sum(len(groups(m)) for m in range(i)) for i in range(TT + 1)]
        NG = before[TT]
        assert NG % 2 == 0
        HALF = NG // 2
        sbank = lambda i: 3 * (i % 2)
        obank = lambda i: 5 if i < TT // 2 else 2
        orows = lambda b: slice(VD * b, VD * b + VD)

        def heads(eng, body):
            with eng.Fori(0, HEADS // 2 - 1) as n:
                for b in range(2):
                    body(2 * n + b, n, b, True)
            body(HEADS - 2, HEADS // 2 - 1, 0, True)
            body(HEADS - 1, HEADS // 2 - 1, 1, False)

        def taken(i, grp, b):
            real = [t for t in grp if t != TT]
            out = []
            if real:
                out.append((PT[i % 2][:, real[0]:real[0] + len(real), :],
                            g.ps[:, b * 512:b * 512 + len(real) * P].rearrange("p (t c) -> p t c", c=P)))
            if TT in grp:
                at = b * 512 + len(real) * P
                out.append((PT[i % 2][0:META, TT, :], g.ps[0:META, at:at + P]))
            return out

        @block.sync
        def _(sp):
            def load_q(h, b):
                sp.dma_start(Q[b][:, :], g.QT[:, bass.ds(h, 1), :].rearrange("p a t -> p (a t)")).then_inc(q_in[b], 16)

            def load_v(n, b):
                cols = slice(0, VD) if b == 0 else slice(VD, VD + P)
                sp.dma_start(V[b][:, 0:TT, :], g.V[:, bass.ds(n, 1), 0:TT, cols].rearrange("p a t c -> p (a t) c")
                             ).then_inc(v_in[b], 16)
                sp.dma_start(V[b][0:META, TT, :], g.V[0:META, bass.ds(n, 1), TT, cols].rearrange("p a c -> p (a c)")
                             ).then_inc(v_in[b], 16)

            for b in range(2):
                load_q(b, b)
                load_v(0, b)
            with sp.Fori(1, HEADS // 2) as n:
                for b in range(2):
                    sp.wait_ge(s_mm, TT * (2 * n + b - 1))
                    load_q(2 * n + b, b)
                    sp.wait_ge(o_mm, 2 * (2 * n + b - 1))
                    load_v(n, b)

        @block.gpsimd
        def _(pool):
            pool.memset(mask[:, :], 0.0).then_inc(cst, 1)
            pool.wait_ge(cst, 1)
            pool.affine_select(out=mask[:, :], in_=mask[:, :], compare_op=ALU.is_ge, fill=-1e30, base=0,
                               pattern=[[-1, P]], channel_multiplier=1).then_inc(cst, 1)

        @block.scalar
        def _(act):
            def expo(h, i):
                act.wait_ge(mx_ok, TT * h + i + 1)
                s, n = i % 2, META + P * (i + 1)
                act.activation(pr[s][:, 0:n], g.ps[:, sbank(i) * 512:sbank(i) * 512 + n], ACT.Exp,
                               bias=negmax[:, s:s + 1], accum_out=total[:, s:s + 1]).then_inc(exp_ok, 1)

            def copies(h, i, gi):
                n = before[i] + gi
                if n % 2 == 0:
                    act.wait_ge(p_tr, NG * h + n + 1)
                    for dst, src in taken(i, groups(i)[gi], 6):
                        ins = act.activation(dst, src, ACT.Copy)
                    ins.then_inc(pa_ok, 1)

            def body(h, n, b, nxt):
                for i in range(TT):
                    copies(h, i, 0)
                    if i:
                        act.wait_ge(p_tr, NG * h + before[i])
                    if i + 1 < TT:
                        expo(h, i + 1)
                    elif nxt:
                        expo(h + 1, 0)
                    for gi in range(1, len(groups(i))):
                        copies(h, i, gi)
                    if i % 4 == 3:
                        act.wait_ge(o_mm, 2 * h + i // 4 + 1)
                        settle(act, g)
                        act.activation(g.omTh[orows(b), bass.ds(n, 1), (i - 3) * P:(i + 1) * P].rearrange("p a t -> p (a t)"),
                                       g.ps[orows(b), obank(i) * 512:obank(i) * 512 + 512], ACT.Copy).then_inc(oh_ok, 1)

            expo(0, 0)
            heads(act, body)

        @block.vector
        def _(dve):
            c = Steps(dve, dv)

            def stats(h, i):
                s, n = i % 2, META + P * (i + 1)
                dve.wait_ge(s_mm, TT * h + i + 1)
                d = g.ps[:, sbank(i) * 512 + P * i:sbank(i) * 512 + P * (i + 1)]
                c.link(dve.tensor_tensor(d, d, mask[:, :], ALU.add))
                dve.tensor_reduce(out=negmax[:, s:s + 1], in_=g.ps[:, sbank(i) * 512:sbank(i) * 512 + n], axis=AX.X,
                                  op=ALU.max, negate=True).then_inc(mx_ok, 1)

            def scaling(h, i):
                s = i % 2
                dve.wait_ge(exp_ok, TT * h + i + 1)
                c.link(dve.reciprocal(inv[:, s:s + 1], total[:, s:s + 1]))
                dve.tensor_scalar(diag[s][:, :], g.ident[:, :], inv[:, s:s + 1], None, ALU.mult).then_inc(dg_ok, 1)

            def body(h, n, b, nxt):
                for i in range(TT):
                    ahead = (h, i + 1) if i + 1 < TT else (h + 1, 0)
                    more = i + 1 < TT or nxt
                    if more:
                        stats(*ahead)
                    for gi, grp in enumerate(groups(i)):
                        m = before[i] + gi
                        if m % 2 == 1:
                            dve.wait_ge(p_tr, NG * h + m + 1)
                            for dst, src in taken(i, grp, 7):
                                ins = dve.tensor_copy(dst, src)
                            ins.then_inc(pd_ok, 1)
                    if more:
                        scaling(*ahead)
                    if i % 4 == 3:
                        dve.wait_ge(oh_ok, 2 * h + i // 4 + 1)
                        hi = g.omTh[orows(b), bass.ds(n, 1), (i - 3) * P:(i + 1) * P].rearrange("p a t -> p (a t)")
                        lo = g.omTl[orows(b), bass.ds(n, 1), (i - 3) * P:(i + 1) * P].rearrange("p a t -> p (a t)")
                        dve.tensor_tensor(lo, g.ps[orows(b), obank(i) * 512:obank(i) * 512 + 512], hi.bitcast(F32),
                                          ALU.subtract).then_inc(ol_ok, 1)

            dve.wait_ge(cst, 2)
            stats(0, 0)
            scaling(0, 0)
            with dve.Fori(0, HEADS // 2 - 1) as n:
                c.enter(n, 2 * 2 * TT)
                for b in range(2):
                    body(2 * n + b, n, b, True)
                c.leave(HEADS // 2 - 1)
            body(HEADS - 2, HEADS // 2 - 1, 0, True)
            body(HEADS - 1, HEADS // 2 - 1, 1, False)

        @block.tensor
        def _(pe):
            def scores(h, n, b, i):
                if i == 0:
                    pe.wait_ge(q_in[b], 16 * n + 16)
                if i == TT - 1:
                    pe.wait_ge(ol_ok, 2 * h + 1)
                base = sbank(i) * 512
                q = Q[b][:, i * P:(i + 1) * P]
                m = P * (i + 1)
                key = lambda c, k: g.KT[:, bass.ds(h, 1), c:c + k].rearrange("p a t -> p (a t)")
                for c in range(0, m, 512):
                    k = min(512, m - c)
                    pe.matmul(g.ps[:, base + c:base + c + k], q, key(c, k), start=True, stop=True)
                pe.matmul(g.ps[:, base + m:base + m + META], q, key(SEQ, META), start=True, stop=True).then_inc(s_mm, 1)

            def taken_by(h, m):
                half = m // 2 + 1
                wait(pe, pa_ok if m % 2 == 0 else pd_ok, HALF * h + half)

            def body(h, n, b, nxt):
                for i in range(TT):
                    s, gs = i % 2, groups(i)
                    pe.wait_ge(dg_ok, TT * h + i + 1)
                    if i == 0:
                        pe.wait_ge(v_in[b], 32 * n + 32)
                        pe.wait_ge(exp_ok, TT * h + 1)

                    def weighted(gi):
                        taken_by(h, before[i] + gi)
                        for t in gs[gi]:
                            k = META if t == TT else P
                            ins = pe.matmul(g.ps[0:VD + VD * b, obank(i) * 512 + (i % 4) * P:obank(i) * 512 + (i % 4 + 1) * P],
                                            V[b][0:k, t, :], PT[s][0:k, t, :], start=t == 0, stop=t == TT)
                        return ins

                    for gi, grp in enumerate(gs):
                        m = before[i] + gi
                        taken_by(h, m - 2)
                        for x, t in enumerate(grp):
                            if t == TT:
                                last = pe.matmul(g.ps[0:META, (6 + m % 2) * 512 + x * P:(6 + m % 2) * 512 + (x + 1) * P],
                                                 pr[s][:, P * (i + 1):P * (i + 1) + META], diag[s][:, :], start=True, stop=True)
                            else:
                                last = pe.matmul(bank(6 + m % 2, x * P, P), pr[s][:, t * P:(t + 1) * P], diag[s][:, :],
                                                 start=True, stop=True)
                        last.then_inc(p_tr, 1)
                        if gi == 0 and i + 2 < TT:
                            scores(h, n, b, i + 2)
                        elif gi == 0 and nxt:
                            scores(h + 1, n + b, 1 - b, i + 2 - TT)
                        if gi >= 1:
                            if gi == 1 and i == 4:
                                wait(pe, ol_ok, 2 * h)
                            weighted(gi - 1)
                    ins = weighted(len(gs) - 1)
                    if i % 4 == 3:
                        ins.then_inc(o_mm, 1)

            pe.wait_ge(cst, 2)
            scores(0, 0, 0, 0)
            scores(0, 0, 0, 1)
            body(0, 0, 0, True)
            body(1, 0, 1, True)
            with pe.Fori(1, HEADS // 2 - 1) as n:
                for b in range(2):
                    body(2 * n + b, n, b, True)
            body(HEADS - 2, HEADS // 2 - 1, 0, True)
            body(HEADS - 1, HEADS // 2 - 1, 1, False)


def expert_loaders(g):
    up = [a[0].rearrange("e (p j) f -> p e j f", j=DK) for a in (g.w1, g.w3)]
    down = g.w2[0].rearrange("e (p j) n -> p e j n", j=2)

    def load_up(eng, e, b):
        for r in range(2):
            eng.dma_start(g.r13[b][:, r, :, :], up[r][:, bass.ds(e, 1), :, :].rearrange("p a j f -> p (a j) f")
                          ).then_inc(g.w_up_in[b], 16)

    def load_down(eng, e, b):
        eng.dma_start(g.r2[b][:, :, :], down[:, bass.ds(e, 1), :, :].rearrange("p a j n -> p (a j) n")
                      ).then_inc(g.w_down_in[b], 16)

    return load_up, load_down


def phase_merge(nc, g):
    with ExitStack() as ph:
        sb = lambda n, s, d=F32: ph.enter_context(nc.sbuf_tensor(n, s, d))
        sem = semaphores(nc, ph)
        w = [sb(f"e_w{b}", [P, 2, 4, P]) for b in range(2)]
        wh = [sb(f"e_wh{b}", [P, 2, 4, P], F32R) for b in range(2)]
        wl = [sb(f"e_wl{b}", [P, 2, 4, P], F32R) for b in range(2)]
        gate = [sb(f"e_gate{b}", [P, 2, SEQ]) for b in range(2)]
        m = [sb(f"e_m{b}", [P, SEQ]) for b in range(2)]
        wo = [sb(f"e_wo{b}", [P, 2, D]) for b in range(2)]
        wo_in = [sem(f"e_wo_in{b}") for b in range(2)]
        woh_ok, wol_ok = sem("e_woh_ok"), sem("e_wol_ok")
        w_in = [sem(f"e_w_in{b}") for b in range(2)]
        gate_in = [sem(f"e_gate_in{b}") for b in range(2)]
        stored = [sem(f"e_stored{b}") for b in range(2)]
        wh_ok, wl_ok, mm_ok, m_ok, dv = sem("e_wh_ok"), sem("e_wl_ok"), sem("e_mm_ok"), sem("e_m_ok"), sem("e_dv")
        block = ph.enter_context(nc.Block())
        bank = lambda i: g.ps[:, i * 512:(i + 1) * 512]
        br = [a[0].rearrange("(j p) n -> p j n", p=P) for a in (g.w_br_mla, g.w_br_hgrn)]
        wo_src = g.w_out[0].rearrange("(j p) n -> p j n", p=P)

        @block.sync
        def _(sp):
            def load_w(n, b):
                for r in range(2):
                    sp.dma_start(w[b][:, r, :, :], br[r][:, :, bass.ds(n * P, P)]).then_inc(w_in[b], 16)

            def load_gates(n, b):
                for r in range(2):
                    sp.dma_start(gate[b][:, r, :], g.gates[bass.ds(n * P + r * D, P), :]).then_inc(gate_in[b], 16)

            def store(n, b):
                sp.wait_ge(m_ok, n + 1)
                sp.dma_start(g.merged[bass.ds(n * P, P), :], m[b][:, :]).then_inc(stored[b], 16)

            def load_out(n):
                if n >= 2:
                    sp.wait_ge(wol_ok, n - 1)
                sp.dma_start(wo[n % 2][:, :, :], wo_src[:, 2 * n:2 * n + 2, :]).then_inc(wo_in[n % 2], 16)

            def turn(n, b):
                sp.wait_ge(wl_ok, n + 1)
                load_w(n + 2, b)
                store(n, b)
                load_gates(n + 2, b)

            load_w(0, 0)
            load_w(1, 1)
            load_gates(0, 0)
            load_gates(1, 1)
            load_out(0)
            load_out(1)
            turn(0, 0)
            load_out(2)
            load_out(3)
            turn(1, 1)
            with sp.Fori(1, DK // 2 - 1) as i:
                for b in range(2):
                    turn(2 * i + b, b)
            for b in range(2):
                store(DK - 2 + b, b)
                sp.wait_ge(stored[b], 16 * (DK // 2))

        @block.scalar
        def _(act):
            def high(n, b, turn):
                wait(act, mm_ok, 4 * (n - 1))
                act.wait_ge(w_in[b], 32 * turn + 32)
                act.activation(wh[b][:, :, :, :], w[b][:, :, :, :], ACT.Copy).then_inc(wh_ok, 1)

            def high_out(n):
                act.wait_ge(wo_in[n % 2], 16 * (n // 2) + 16)
                act.activation(g.woh[:, 2 * n:2 * n + 2, :], wo[n % 2][:, :, :], ACT.Copy).then_inc(woh_ok, 1)

            high(0, 0, 0)
            high(1, 1, 0)
            for b in range(2):
                high_out(2 * b)
                high_out(2 * b + 1)
                high(2 + b, b, 1)
            with act.Fori(2, DK // 2) as i:
                for b in range(2):
                    high(2 * i + b, b, i)

        @block.vector
        def _(dve):
            c = Steps(dve, dv)

            def low(n, b):
                dve.wait_ge(wh_ok, n + 1)
                dve.tensor_tensor(wl[b][:, :, :, :], w[b][:, :, :, :], wh[b][:, :, :, :].bitcast(F32),
                                  ALU.subtract).then_inc(wl_ok, 1)

            def merge(n, b, turn, first):
                dve.wait_ge(gate_in[b], 32 * turn + 32)
                if not first:
                    dve.wait_ge(stored[b], 16 * turn)
                for r in range(2):
                    for q in range(2):
                        dve.wait_ge(mm_ok, 4 * n + 2 * r + q + 1)
                        cols = slice(q * 512, (q + 1) * 512)
                        c.mark(dve.tensor_tensor((m[b] if r == 0 else gate[b][:, 1, :])[:, cols], gate[b][:, r, cols],
                                                 bank(4 * b + 2 * r + q), ALU.mult))
                dve.wait_ge(dv, c.now())
                dve.tensor_tensor(m[b][:, :], m[b][:, :], gate[b][:, 1, :], ALU.add).then_inc(m_ok, 1)

            low(0, 0)
            for b in range(2):
                low(b + 1, 1 - b)
                merge(b, b, 0, True)
                for n in (2 * b, 2 * b + 1):
                    dve.wait_ge(woh_ok, n + 1)
                    dve.tensor_tensor(g.wol[:, 2 * n:2 * n + 2, :], wo[n % 2][:, :, :],
                                      g.woh[:, 2 * n:2 * n + 2, :].bitcast(F32), ALU.subtract).then_inc(wol_ok, 1)
            with dve.Fori(1, DK // 2 - 1) as i:
                c.enter(i - 1, 8)
                for b in range(2):
                    low(2 * i + b + 1, 1 - b)
                    merge(2 * i + b, b, i, False)
                c.leave(DK // 2 - 2)
            low(DK - 1, 1)
            merge(DK - 2, 0, DK // 2 - 1, False)
            merge(DK - 1, 1, DK // 2 - 1, False)

        @block.tensor
        def _(pe):
            def products(n, b):
                pe.wait_ge(wl_ok, n + 1)
                for r, (oh, ol) in enumerate([(g.omTh, g.omTl), (g.ohTh, g.ohTl)]):
                    for q in range(2):
                        cols = slice(q * 512, (q + 1) * 512)
                        for j in range(4):
                            last = mm3(pe, bank(4 * b + 2 * r + q), wh[b][:, r, j, :], wl[b][:, r, j, :],
                                       oh[:, j, cols], ol[:, j, cols], j == 0, j == 3)
                        last.then_inc(mm_ok, 1)

            for b in range(2):
                products(b, b)
            with pe.Fori(1, DK // 2) as i:
                for b in range(2):
                    pe.wait_ge(m_ok, 2 * i + b - 1)
                    products(2 * i + b, b)


def phase_output(nc, g):
    with ExitStack() as ph:
        sb = lambda n, s, d=F32: ph.enter_context(nc.sbuf_tensor(n, s, d))
        sem = semaphores(nc, ph)
        m = [sb(f"f_m{b}", [P, DK, P]) for b in range(2)]
        mh = [sb(f"f_mh{b}", [P, DK, P], F32R) for b in range(2)]
        ml = [sb(f"f_ml{b}", [P, DK, P], F32R) for b in range(2)]
        x = [sb(f"f_x{b}", [P, D]) for b in range(2)]
        u = [sb(f"f_u{b}", [P, D]) for b in range(2)]
        junk, gain, uT = sb("f_junk", [P, D]), sb("f_gain", [P, D]), sb("f_uT", [P, DK, P])
        R = GROUPS + EXPERTS
        FILLS = EXPERTS * SLOTS * ROWS // P // SLOTS
        wr, br = sb("f_wr", [P, DK, R]), sb("f_br", [P, R])
        st = sb("f_stat", [P, 4])
        lg, top, idx, ex8, oh8, sel, es = (sb("f_lg", [P, R]), sb("f_top", [P, 2, 8]), sb("f_idx", [P, 2, 8], U32),
                                           sb("f_ex8", [P, 8]), sb("f_oh8", [P, 8]), sb("f_sel", [P, 8, 8]), sb("f_es", [P, 8]))
        sc = sb("f_sc", [P, 16])
        M = [sb(f"f_M{b}", [P, 3, EXPERTS]) for b in range(2)]
        Mcum, R2, tmp = sb("f_Mcum", [P, EXPERTS]), sb("f_R2", [P, EXPERTS]), sb("f_tmp", [P, EXPERTS])
        slot = [sb(f"f_slot{b}", [P, 2], I32) for b in range(2)]
        slotf = sb("f_slotf", [P, 2])
        rec = [sb(f"f_rec{b}", [P, 2, ROWS]) for b in range(2)]
        io8, io64, off64, tok, upper = (sb("f_io8", [P, 8]), sb("f_io64", [P, EXPERTS]), sb("f_off64", [P, EXPERTS]),
                                        sb("f_tok", [P, 1]), sb("f_upper", [P, P]))
        fill = sb("f_fill", [P, SLOTS])
        rec_z = sem("f_rec_z")
        cst_in, cst, fill_ok, filled = sem("f_cst_in"), sem("f_cst"), sem("f_fill_ok"), sem("f_filled")
        m_in = [sem(f"f_m_in{b}") for b in range(2)]
        x_in = [sem(f"f_x_in{b}") for b in range(2)]
        h_out = [sem(f"f_h_out{b}") for b in range(2)]
        u_out = [sem(f"f_u_out{b}") for b in range(2)]
        rec_out, rec_free = sem("f_rec_out"), sem("f_rec_free")
        mh_ok, ml_ok, w_mm, h_ok, ss_ok, rt_ok, u_ok = (sem("f_mh_ok"), sem("f_ml_ok"), sem("f_w_mm"), sem("f_h_ok"),
                                                        sem("f_ss_ok"), sem("f_rt_ok"), sem("f_u_ok"))
        u_tr, uT_ok, lg_mm, lg_ok, eg_ok, d_ok, ed_ok, M_ok, rk_mm, cum_ok, dv = (
            sem("f_u_tr"), sem("f_uT_ok"), sem("f_lg_mm"), sem("f_lg_ok"), sem("f_eg_ok"), sem("f_d_ok"), sem("f_ed_ok"),
            sem("f_M_ok"), sem("f_rk_mm"), sem("f_cum_ok"), sem("f_dv"))
        block = ph.enter_context(nc.Block())
        bank = lambda i, a=0, n=512: g.ps[:, i * 512 + a:i * 512 + a + n]
        m_src = g.merged.rearrange("(j p) t -> p j t", p=P)

        def steps(body, eng, enter=None, leave=None):
            for t in range(-2, 2):
                body(t, t // 2, t % 2)
            with eng.Fori(1, TT // 2 - 1) as n:
                if enter:
                    enter(n)
                for b in range(2):
                    body(2 * n + b, n, b)
                if leave:
                    leave()
            for t in range(TT - 2, TT + 2):
                body(t, t // 2, t % 2)

        def has(t, d=0):
            return not isinstance(t, int) or 0 <= t + d < TT

        @block.sync
        def _(sp):
            for b in range(2):
                sp.dma_start(m[b][:, :, :], m_src[:, :, b * P:(b + 1) * P]).then_inc(m_in[b], 16)
                sp.dma_start(x[b][:, :], g.x[0, b * P:(b + 1) * P, :]).then_inc(x_in[b], 16)
            sp.dma_start(gain[:, :], g.ffn_norm[0:1, :].to_broadcast([P, D])).then_inc(cst_in, 16)
            sp.dma_start(wr[:, :, 0:GROUPS], g.w_group[0].rearrange("(j p) n -> p j n", p=P)).then_inc(cst_in, 16)
            sp.dma_start(wr[:, :, GROUPS:R], g.w_route[0].rearrange("(j p) n -> p j n", p=P)).then_inc(cst_in, 16)
            sp.dma_start(br[:, 0:GROUPS], g.b_group[0:1, :].to_broadcast([P, GROUPS])).then_inc(cst_in, 16)
            sp.dma_start(br[:, GROUPS:R], g.b_route[0:1, :].to_broadcast([P, EXPERTS])).then_inc(cst_in, 16)
            sp.wait_ge(fill_ok, 1)
            for n in range(FILLS):
                sp.dma_start(g.table.rearrange("(p s) r -> p (s r)", p=P)[:, n * SLOTS:(n + 1) * SLOTS],
                             fill[:, :]).then_inc(filled, 16)

            def load_m(t, b):
                sp.wait_ge(ml_ok, t - 1)
                sp.dma_start(m[b][:, :, :], m_src[:, :, bass.ds(t * P, P)]).then_inc(m_in[b], 16)

            def body(t, n, b, more):
                if more:
                    load_m(t + 3, 1 - b)
                sp.wait_ge(h_ok, t + 1)
                sp.dma_start(g.h[bass.ds(t * P, P), :], x[b][:, :]).then_inc(h_out[b], 16)
                sp.wait_ge(u_ok, t + 1)
                sp.dma_start(g.u2[bass.ds(t * P, P), :], u[b][:, :]).then_inc(u_out[b], 16)
                if has(t, 2):
                    sp.wait_ge(h_out[b], 16 * (n + 1))
                    sp.dma_start(x[b][:, :], g.x[0, bass.ds((t + 2) * P, P), :]).then_inc(x_in[b], 16)

            load_m(2, 0)
            body(0, 0, 0, True)
            for b in range(2):
                g.load_up(sp, b, b)
                g.load_down(sp, b, b)
            with sp.Fori(0, TT // 2 - 2) as n:
                body(2 * n + 1, n, 1, True)
                body(2 * n + 2, n + 1, 0, True)
            for t in range(TT - 3, TT):
                body(t, t // 2, t % 2, False)
            for b in range(2):
                sp.wait_ge(h_out[b], 16 * (TT // 2))
                sp.wait_ge(u_out[b], 16 * (TT // 2))

        @block.gpsimd
        def _(pool):
            pool.iota(io8[:, :], pattern=[[1, 8]], base=0, channel_multiplier=0,
                      allow_small_or_imprecise_dtypes=True).then_inc(cst, 1)
            pool.iota(io64[:, :], pattern=[[1, EXPERTS]], base=0, channel_multiplier=0,
                      allow_small_or_imprecise_dtypes=True).then_inc(cst, 1)
            pool.iota(off64[:, :], pattern=[[SLOTS, EXPERTS]], base=0, channel_multiplier=0,
                      allow_small_or_imprecise_dtypes=True).then_inc(cst, 1)
            pool.iota(tok[:, :], pattern=[[0, 1]], base=0, channel_multiplier=1,
                      allow_small_or_imprecise_dtypes=True).then_inc(cst, 1)
            pool.memset(Mcum[:, :], 0.0).then_inc(cst, 1)
            pool.affine_select(out=upper[:, :], in_=g.ones[:, :], compare_op=ALU.is_gt, fill=0.0, base=0,
                               pattern=[[1, P]], channel_multiplier=-1).then_inc(cst, 1)
            for b in range(2):
                pool.memset(rec[b][:, :, :], 0.0).then_inc(rec_z, 1)
            pool.memset(fill[:, :], SKIP).then_inc(fill_ok, 1)

            pool.wait_ge(filled, 16 * FILLS)
            pool.sem_inc(rec_free, 1)
            with pool.Fori(0, TT // 2) as i:
                for b in range(2):
                    pool.wait_ge(cum_ok, 2 * i + b + 1)
                    settle(pool, g)
                    for c in range(2):
                        pool.indirect_dma_start(out=g.table, out_offset=bass.IndirectOffsetOnAxis(ap=slot[b][:, c:c + 1], axis=0),
                                                in_=rec[b][:, c, :], in_offset=None).then_inc(rec_out, 16)
                    pool.wait_ge(rec_out, 32 * (2 * i + b + 1))
                    pool.sem_inc(rec_free, 1)

        @block.scalar
        def _(act):
            def split(t, b, n):
                act.wait_ge(m_in[b], 16 * n + 16)
                act.activation(mh[b][:, :, :], m[b][:, :, :], ACT.Copy).then_inc(mh_ok, 1)

            def body(t, n, b):
                if has(t):
                    act.wait_ge(h_ok, t + 1)
                    act.activation(junk[:, :], x[b][:, :], ACT.Square, accum_out=st[:, b:b + 1]).then_inc(ss_ok, 1)
                    act.wait_ge(ss_ok, t + 1)
                    act.activation(st[:, 2 + b:3 + b], st[:, b:b + 1], ACT.Sqrt, scale=1.0 / D,
                                   bias=g.eps[:, :]).then_inc(rt_ok, 1)
                if has(t, 2):
                    wait(act, w_mm, t + 1)
                    split(t + 2, b, n + 1)
                if has(t, -1):
                    act.wait_ge(lg_ok, t)
                    act.activation(ex8[:, :], lg[:, 0:8], ACT.Exp, bias=sc[:, 0:1], accum_out=sc[:, 1:2]).then_inc(eg_ok, 1)
                    act.wait_ge(d_ok, t)
                    act.activation(sc[:, 7:8], sc[:, 6:7], ACT.Exp).then_inc(ed_ok, 1)
                if has(t):
                    for q in range(2):
                        act.wait_ge(u_tr, 2 * t + q + 1)
                        act.activation(uT[:, 4 * q:4 * q + 4, :], bank(4 + q).rearrange("p (j t) -> p j t", j=4),
                                       ACT.Copy).then_inc(uT_ok, 1)

            steps(body, act)

        @block.vector
        def _(dve):
            c = Steps(dve, dv)

            def low(t, b):
                dve.wait_ge(mh_ok, t + 1)
                dve.tensor_tensor(ml[b][:, :, :], m[b][:, :, :], mh[b][:, :, :].bitcast(F32), ALU.subtract).then_inc(ml_ok, 1)

            def choose(t, b):
                dve.wait_ge(lg_mm, t + 1)
                c.link(dve.tensor_tensor(lg[:, :], bank(6, 0, R), br[:, :], ALU.add))
                settle(dve, g)
                c.link(dve.max(out=top[:, 0, :], in_=lg[:, 0:8]))
                dve.tensor_scalar(sc[:, 0:1], top[:, 0, 0:1], -1.0, None, ALU.mult).then_inc(lg_ok, 1)
                settle(dve, g)
                c.link(dve.max_index(out=idx[:, 0, :], in_max=top[:, 0, :], in_values=lg[:, 0:8]))
                c.link(dve.tensor_copy(sc[:, 2:3], idx[:, 0, 0:1]))
                c.link(dve.tensor_scalar(oh8[:, :], io8[:, :], sc[:, 2:3], None, ALU.is_equal))
                c.link(dve.tensor_tensor(sel[:, :, :], lg[:, 8:R].rearrange("p (g e) -> p g e", g=8),
                                         oh8[:, :].rearrange("p (g a) -> p g a", a=1).to_broadcast([P, 8, 8]), ALU.mult))
                c.link(dve.tensor_reduce(out=es[:, :], in_=sel[:, :, :].rearrange("p g e -> p e g"), axis=AX.X, op=ALU.add))
                settle(dve, g)
                c.link(dve.max(out=top[:, 1, :], in_=es[:, :]))
                dve.tensor_tensor(sc[:, 6:7], top[:, 1, 1:2], top[:, 1, 0:1], ALU.subtract).then_inc(d_ok, 1)
                settle(dve, g)
                c.link(dve.max_index(out=idx[:, 1, :], in_max=top[:, 1, :], in_values=es[:, :]))
                c.link(dve.tensor_copy(sc[:, 4:6], idx[:, 1, 0:2]))
                c.link(dve.tensor_scalar(sc[:, 3:4], sc[:, 2:3], 8.0, None, ALU.mult))
                c.link(dve.tensor_scalar(sc[:, 4:6], sc[:, 4:6], sc[:, 3:4], None, ALU.add))
                for k in range(2):
                    c.link(dve.tensor_scalar(M[b][:, k, :], io64[:, :], sc[:, 4 + k:5 + k], None, ALU.is_equal))
                dve.tensor_tensor(M[b][:, 2, :], M[b][:, 0, :], M[b][:, 1, :], ALU.add).then_inc(M_ok, 1)
                dve.wait_ge(eg_ok, t + 1)
                c.link(dve.reciprocal(sc[:, 8:9], sc[:, 1:2]))
                dve.wait_ge(ed_ok, t + 1)
                c.link(dve.tensor_scalar(sc[:, 9:10], sc[:, 7:8], 1.0, None, ALU.add))
                c.link(dve.reciprocal(sc[:, 9:10], sc[:, 9:10]))
                c.link(dve.tensor_tensor(sc[:, 10:11], sc[:, 8:9], sc[:, 9:10], ALU.mult))
                c.link(dve.tensor_tensor(sc[:, 11:12], sc[:, 10:11], sc[:, 7:8], ALU.mult))

            def place(t, b):
                dve.wait_ge(rk_mm, t + 1)
                c.link(dve.tensor_tensor(R2[:, :], bank(7, 0, EXPERTS), off64[:, :], ALU.add))
                for k in range(2):
                    c.link(dve.scalar_tensor_tensor(out=tmp[:, :], in0=M[b][:, k, :], scalar=1.0, in1=R2[:, :], op0=ALU.mult,
                                                    op1=ALU.mult, accum_out=slotf[:, k:k + 1]))
                dve.wait_ge(rec_free, t + 1)
                c.link(dve.tensor_copy(slot[b][:, :], slotf[:, :]))
                for k in range(2):
                    c.link(dve.tensor_scalar(rec[b][:, k, 0:1], tok[:, :], 2.0, float(k), ALU.mult, ALU.add))
                    c.link(dve.tensor_copy(rec[b][:, k, 1:2], sc[:, 10 + k:11 + k]))
                    c.link(dve.tensor_copy(rec[b][:, k, 2:3], tok[:, :]))
                c.link(dve.tensor_scalar(tok[:, :], tok[:, :], float(P), None, ALU.add))
                dve.tensor_tensor(Mcum[:, :], Mcum[:, :], M[b][:, 2, :], ALU.add).then_inc(cum_ok, 1)

            def body(t, n, b):
                if has(t):
                    if isinstance(t, int) and t == 0:
                        dve.wait_ge(cst_in, 80)
                        dve.wait_ge(cst, 6)
                        dve.wait_ge(rec_z, 2)
                    dve.wait_ge(x_in[b], 16 * n + 16)
                    dve.wait_ge(w_mm, t + 1)
                    for q in range(2):
                        ins = dve.tensor_tensor(x[b][:, q * 512:(q + 1) * 512], x[b][:, q * 512:(q + 1) * 512],
                                                bank(2 * b + q), ALU.add)
                    ins.then_inc(h_ok, 1)
                    dve.wait_ge(rt_ok, t + 1)
                    c.link(dve.reciprocal(st[:, 2 + b:3 + b], st[:, 2 + b:3 + b]))
                    wait(dve, u_out[b], 16 * n)
                    dve.scalar_tensor_tensor(out=u[b][:, :], in0=x[b][:, :], scalar=st[:, 2 + b:3 + b], in1=gain[:, :],
                                             op0=ALU.mult, op1=ALU.mult).then_inc(u_ok, 1)
                if has(t, 2):
                    low(t + 2, b)
                if has(t, -2):
                    place(t - 2, b)
                if has(t, -1):
                    choose(t - 1, 1 - b)

            per = 31
            steps(body, dve, lambda n: c.enter(n - 1, 2 * per), lambda: c.leave(TT // 2 - 2))
            dve.wait_ge(rk_mm, TT + 1)
            c.link(dve.tensor_reduce(out=sc[:, 12:13], in_=bank(7, 0, EXPERTS), axis=AX.X, op=ALU.max))
            c.link(dve.tensor_copy(g.most[:, :], sc[:, 12:13]))

        @block.tensor
        def _(pe):
            def times_out(b, q):
                for j in range(DK):
                    last = mm3(pe, bank(2 * b + q), mh[b][:, j, :], ml[b][:, j, :], g.woh[:, j, q * 512:(q + 1) * 512],
                               g.wol[:, j, q * 512:(q + 1) * 512], j == 0, j == DK - 1)
                return last

            def body(t, n, b):
                if has(t, 1):
                    pe.wait_ge(ml_ok, t + 2)
                    wait(pe, h_ok, t)
                    times_out(1 - b, 0)
                if has(t):
                    if isinstance(t, int) and t == 0:
                        pe.wait_ge(cst_in, 80)
                        pe.wait_ge(cst, 6)
                    pe.wait_ge(u_ok, t + 1)
                    for q in range(2):
                        for j in range(4):
                            last_i = pe.transpose(bank(4 + q, j * P, P), u[b][:, (4 * q + j) * P:(4 * q + j + 1) * P], g.ident[:, :])
                        last_i.then_inc(u_tr, 1)
                if has(t, 1):
                    times_out(1 - b, 1).then_inc(w_mm, 1)
                if has(t, -1):
                    pe.wait_ge(M_ok, t)
                    wait(pe, cum_ok, t - 1)
                    pe.matmul(bank(7, 0, EXPERTS), upper[:, :], M[1 - b][:, 2, :], start=True, stop=False)
                    pe.matmul(bank(7, 0, EXPERTS), g.ones[:, :], Mcum[:, :], start=False, stop=True).then_inc(rk_mm, 1)
                if has(t):
                    pe.wait_ge(uT_ok, 2 * t + 2)
                    for j in range(DK):
                        ins = pe.matmul(bank(6, 0, R), uT[:, j, :], wr[:, j, :], start=j == 0, stop=j == DK - 1)
                    ins.then_inc(lg_mm, 1)

            steps(body, pe)
            pe.wait_ge(cum_ok, TT)
            pe.matmul(bank(7, 0, EXPERTS), g.ones[:, :], Mcum[:, :], start=True, stop=True).then_inc(rk_mm, 1)


def inside(e, d=0):
    return not isinstance(e, int) or 0 <= e + d < EXPERTS


def each_expert(eng, body):
    for e in range(-2, 4):
        body(e, e // 2, e % 2)
    with eng.Fori(2, EXPERTS // 2 - 2) as n:
        for b in range(2):
            body(2 * n + b, n, b)
    for e in range(EXPERTS - 4, EXPERTS + 2):
        body(e, e // 2, e % 2)


def phase_experts(nc, g):
    with ExitStack() as ph:
        sb = lambda n, s, d=F32: ph.enter_context(nc.sbuf_tensor(n, s, d))
        sem = semaphores(nc, ph)
        up_h = [sb(f"m_up_h{b}", [P, 2, DK, DE], F32R) for b in range(2)]
        up_l = [sb(f"m_up_l{b}", [P, 2, DK, DE], F32R) for b in range(2)]
        dn_h = [sb(f"m_dn_h{b}", [P, 2, D], F32R) for b in range(2)]
        dn_l = [sb(f"m_dn_l{b}", [P, 2, D], F32R) for b in range(2)]
        x = [sb(f"m_x{b}", [CAP, D]) for b in range(2)]
        xT_h = [sb(f"m_xT_h{b}", [P, DK, WIDE], F32R) for b in range(2)]
        xT_l = [sb(f"m_xT_l{b}", [P, DK, WIDE], F32R) for b in range(2)]
        sig, prod, hid = sb("m_sig", [CAP, DE]), sb("m_prod", [CAP, DE]), sb("m_hid", [CAP, DE])
        hT_h, hT_l = sb("m_hT_h", [P, 2, WIDE], F32R), sb("m_hT_l", [P, 2, WIDE], F32R)
        zero = sb("m_zero", [P, DK, WIDE - CAP])
        y = [sb(f"m_y{b}", [CAP, D]) for b in range(2)]
        tab = sb("m_tab", [EXPERTS, CAP * ROWS])
        rows = sb("m_rows", [CAP, 2, EXPERTS], I32)
        gate = sb("m_gate", [CAP, EXPERTS])
        src_row = [sb(f"m_src_row{b}", [CAP, 1], I32) for b in range(2)]
        dst_row = [sb(f"m_dst_row{b}", [CAP, 1], I32) for b in range(2)]
        tab_in, tab_tr, rows_ok, x_zero, pad_ok = (sem("m_tab_in"), sem("m_tab_tr"), sem("m_rows_ok"), sem("m_x_zero"),
                                                   sem("m_pad_ok"))
        x_in = [sem(f"m_x_in{b}") for b in range(2)]
        y_out = [sem(f"m_y_out{b}") for b in range(2)]
        row_ok = sem("m_row_ok")
        up_h_ok, up_l_ok, dn_h_ok, dn_l_ok = sem("m_up_h_ok"), sem("m_up_l_ok"), sem("m_dn_h_ok"), sem("m_dn_l_ok")
        x_tr, xh_ok, xl_ok, up_mm, sig_ok, prod_ok, hid_ok = (sem("m_x_tr"), sem("m_xh_ok"), sem("m_xl_ok"), sem("m_up_mm"),
                                                              sem("m_sig_ok"), sem("m_prod_ok"), sem("m_hid_ok"))
        h_tr, hh_ok, hl_ok, dn_mm, y_ok = sem("m_h_tr"), sem("m_hh_ok"), sem("m_hl_ok"), sem("m_dn_mm"), sem("m_y_ok")
        block = ph.enter_context(nc.Block())
        bank = lambda i, a=0, n=512, rows=P: g.ps[0:rows, i * 512 + a:i * 512 + a + n]
        turned = lambda i, n: bank(i, 0, n * CAP).rearrange("p (j t) -> p j t", j=n)
        X_BANK, UP_BANK, Y_BANK, H_BANK = 0, 2, 4, 6
        first = lambda e: isinstance(e, int) and e == -1

        @block.sync
        def _(sp):
            sp.dma_start(tab[:, :], g.table.rearrange("(e s) r -> e s r", e=EXPERTS)[:, 0:CAP, :]
                         .rearrange("e s r -> e (s r)")).then_inc(tab_in, 16)

            def body(e, n, b):
                if inside(e, 3) and (not isinstance(e, int) or e > -2):
                    sp.wait_ge(up_l_ok, 2 * e + 4)
                    g.load_up(sp, e + 3, 1 - b)
                if inside(e, 2) and (not isinstance(e, int) or e > -1):
                    sp.wait_ge(dn_l_ok, e + 1)
                    g.load_down(sp, e + 2, b)

            each_expert(sp, body)

        @block.gpsimd
        def _(pool):
            k = [0]
            pool.memset(zero[:, :, :], 0.0).then_inc(x_zero, 1)
            for b in range(2):
                pool.memset(x[b][:, :], 0.0).then_inc(x_zero, 1)
            pool.wait_ge(x_zero, 3)
            pool.wait_ge(rows_ok, 3)

            def body(e, n, b):
                before = k[0] if isinstance(e, int) else 2 * e
                if inside(e, 2):
                    wait(pool, x_tr, 2 * e + 2)
                    settle(pool, g)
                    pool.tensor_copy(src_row[b][:, :], rows[:, 1, bass.ds(e + 2, 1)]).then_inc(row_ok, 1)
                    pool.wait_ge(row_ok, before + 1)
                    settle(pool, g)
                    pool.indirect_dma_start(out=x[b][:, :], out_offset=None, in_=g.u2,
                                            in_offset=bass.IndirectOffsetOnAxis(ap=src_row[b][:, 0:1], axis=0),
                                            bounds_check=SEQ - 1, oob_is_err=False).then_inc(x_in[b], 16)
                    before = before + 1
                if inside(e, -2):
                    pool.wait_ge(y_ok, 2 * e - 2)
                    settle(pool, g)
                    pool.tensor_copy(dst_row[b][:, :], rows[:, 0, bass.ds(e - 2, 1)]).then_inc(row_ok, 1)
                    pool.wait_ge(row_ok, before + 1)
                    settle(pool, g)
                    pool.indirect_dma_start(out=g.y, out_offset=bass.IndirectOffsetOnAxis(ap=dst_row[b][:, 0:1], axis=0),
                                            in_=y[b][:, :], in_offset=None,
                                            bounds_check=2 * SEQ - 1, oob_is_err=False).then_inc(y_out[b], 16)
                    before = before + 1
                k[0] = before if isinstance(e, int) else 2 * (EXPERTS - 4)

            each_expert(pool, body)
            for b in range(2):
                pool.wait_ge(y_out[b], 16 * (EXPERTS // 2))

        @block.scalar
        def _(act):
            def pad():
                act.wait_ge(x_zero, 3)
                for t in (*xT_h, *xT_l, hT_h, hT_l):
                    act.activation(t[:, :, CAP:WIDE], zero[:, 0:t.shape[1], :], ACT.Copy).then_inc(pad_ok, 1)


            def split_up(e, n, b, r):
                if r == 0:
                    act.wait_ge(g.w_up_in[1 - b], 32 * (n + b + 1))
                act.activation(up_h[1 - b][:, r, :, :], g.r13[1 - b][:, r, :, :], ACT.Copy).then_inc(up_h_ok, 1)

            def body(e, n, b):
                if inside(e, -1):
                    act.wait_ge(up_mm, e)
                    act.activation(sig[:, :], bank(UP_BANK + 1 - b, 0, DE, CAP), ACT.Sigmoid).then_inc(sig_ok, 1)
                if inside(e, 1):
                    split_up(e, n, b, 0)
                if first(e):
                    split_up(e, n, b, 1)
                    pad()
                    act.wait_ge(rows_ok, 3)
                if inside(e, -2):
                    if inside(e, -4):
                        act.wait_ge(y_out[b], 16 * (n - 1))
                    for q in range(2):
                        act.wait_ge(dn_mm, 2 * e + q - 3)
                        settle(act, g)
                        act.activation(y[b][:, q * 512:(q + 1) * 512], bank(Y_BANK + q, rows=CAP), ACT.Copy,
                                       scale=gate[:, bass.ds(e - 2, 1)]).then_inc(y_ok, 1)
                if inside(e):
                    act.wait_ge(g.w_down_in[b], 16 * (n + 1))
                    act.activation(dn_h[b][:, :, :], g.r2[b][:, :, :], ACT.Copy).then_inc(dn_h_ok, 1)
                if inside(e, -1):
                    act.wait_ge(h_tr, e)
                    act.activation(hT_h[:, :, 0:CAP], turned(H_BANK, 2), ACT.Copy).then_inc(hh_ok, 1)
                if inside(e, 1):
                    for q in range(2):
                        act.wait_ge(x_tr, 2 * e + q + 3)
                        act.activation(xT_h[1 - b][:, 4 * q:4 * q + 4, 0:CAP], turned(X_BANK + q, 4),
                                       ACT.Copy).then_inc(xh_ok, 1)
                    if not first(e):
                        split_up(e, n, b, 1)

            each_expert(act, body)

        @block.vector
        def _(dve):
            dve.wait_ge(tab_tr, 1)
            for c in range(2):
                dve.tensor_copy(rows[:, c, :], bank(H_BANK + 1, 2 * c * EXPERTS, EXPERTS, CAP)).then_inc(rows_ok, 1)
            dve.tensor_copy(gate[:, :], bank(H_BANK + 1, EXPERTS, EXPERTS, CAP)).then_inc(rows_ok, 1)

            def split_up(e, b, r):
                dve.wait_ge(up_h_ok, 2 * e + r + 3)
                dve.tensor_tensor(up_l[1 - b][:, r, :, :], g.r13[1 - b][:, r, :, :], up_h[1 - b][:, r, :, :].bitcast(F32),
                                  ALU.subtract).then_inc(up_l_ok, 1)

            def body(e, n, b):
                if inside(e, -1):
                    dve.wait_ge(sig_ok, e)
                    dve.tensor_tensor(prod[:, :], sig[:, :], bank(UP_BANK + 1 - b, 0, DE, CAP), ALU.mult).then_inc(prod_ok, 1)
                    dve.wait_ge(prod_ok, e)
                    dve.tensor_tensor(hid[:, :], prod[:, :], bank(UP_BANK + 1 - b, DE, DE, CAP), ALU.mult).then_inc(hid_ok, 1)
                if inside(e, 1):
                    split_up(e, b, 0)
                if first(e):
                    split_up(e, b, 1)
                if inside(e, -1):
                    dve.wait_ge(hh_ok, e)
                    dve.tensor_tensor(hT_l[:, :, 0:CAP], turned(H_BANK, 2), hT_h[:, :, 0:CAP].bitcast(F32),
                                      ALU.subtract).then_inc(hl_ok, 1)
                if inside(e, 1):
                    for q in range(2):
                        dve.wait_ge(xh_ok, 2 * e + q + 3)
                        dve.tensor_tensor(xT_l[1 - b][:, 4 * q:4 * q + 4, 0:CAP], turned(X_BANK + q, 4),
                                          xT_h[1 - b][:, 4 * q:4 * q + 4, 0:CAP].bitcast(F32), ALU.subtract).then_inc(xl_ok, 1)
                if inside(e):
                    dve.wait_ge(dn_h_ok, e + 1)
                    dve.tensor_tensor(dn_l[b][:, :, :], g.r2[b][:, :, :], dn_h[b][:, :, :].bitcast(F32),
                                      ALU.subtract).then_inc(dn_l_ok, 1)
                if inside(e, 1) and not first(e):
                    split_up(e, b, 1)

            each_expert(dve, body)

        @block.tensor
        def _(pe):
            pe.wait_ge(tab_in, 16)
            for c in range(3):
                ins = pe.transpose(bank(H_BANK + 1, c * EXPERTS, EXPERTS, CAP), tab[:, c::ROWS], g.ident[0:EXPERTS, 0:EXPERTS])
            ins.then_inc(tab_tr, 1)
            pe.wait_ge(rows_ok, 3)
            pe.wait_ge(pad_ok, 6)

            def up(b, js):
                for j in js:
                    ins = mm3(pe, bank(UP_BANK + b, rows=WIDE).rearrange("p (r f) -> p r f", r=2), xT_h[b][:, j, :], xT_l[b][:, j, :],
                              up_h[b][:, :, j, :], up_l[b][:, :, j, :], j == 0, j == DK - 1)
                return ins

            def body(e, n, b):
                if inside(e):
                    pe.wait_ge(up_l_ok, 2 * e + 2)
                    pe.wait_ge(xl_ok, 2 * e + 2)
                    up(b, range(DK // 2))
                if inside(e, -1):
                    pe.wait_ge(hid_ok, e)
                    settle(pe, g)
                    for j in range(2):
                        ins = pe.transpose(bank(H_BANK, j * CAP, CAP), hid[:, j::2], g.ident[0:CAP, 0:CAP])
                    ins.then_inc(h_tr, 1)
                if inside(e, 1):
                    pe.wait_ge(x_in[1 - b], 16 * (n + b + 1))
                    wait(pe, xl_ok, 2 * e + 2)
                    settle(pe, g)
                    for q in range(2):
                        for j in range(4):
                            ins = pe.transpose(bank(X_BANK + q, j * CAP, CAP), x[1 - b][:, 4 * q + j::DK], g.ident[0:CAP, 0:CAP])
                        ins.then_inc(x_tr, 1)
                if inside(e):
                    up(b, range(DK // 2, DK)).then_inc(up_mm, 1)
                if inside(e, -1):
                    pe.wait_ge(hl_ok, e)
                    pe.wait_ge(dn_l_ok, e)
                    if inside(e, -2):
                        pe.wait_ge(y_ok, 2 * e - 2)
                    for q in range(2):
                        for j in range(2):
                            ins = mm3(pe, bank(Y_BANK + q, rows=WIDE), hT_h[:, j, :], hT_l[:, j, :],
                                      dn_h[1 - b][:, j, q * 512:(q + 1) * 512], dn_l[1 - b][:, j, q * 512:(q + 1) * 512],
                                      j == 0, j == 1)
                        ins.then_inc(dn_mm, 1)

            each_expert(pe, body)


def phase_overflow(nc, g):
    with ExitStack() as ph:
        sb = lambda n, s, d=F32: ph.enter_context(nc.sbuf_tensor(n, s, d))
        sem = semaphores(nc, ph)
        x, xT = sb("v_x", [CAP, D]), sb("v_xT", [P, DK, CAP])
        sig, prod, hid, hT = sb("v_sig", [CAP, DE]), sb("v_prod", [CAP, DE]), sb("v_hid", [CAP, DE]), sb("v_hT", [P, 2, CAP])
        y = sb("v_y", [CAP, D])
        rec, rows = sb("v_rec", [CAP, ROWS]), sb("v_rows", [CAP, ROWS], I32)
        up_in, down_in, rec_in, x_zero = sem("v_up_in"), sem("v_down_in"), sem("v_rec_in"), sem("v_x_zero")
        rows_ok, x_in, x_tr, xT_ok, up_mm = sem("v_rows_ok"), sem("v_x_in"), sem("v_x_tr"), sem("v_xT_ok"), sem("v_up_mm")
        sig_ok, prod_ok, hid_ok, h_tr, hT_ok = sem("v_sig_ok"), sem("v_prod_ok"), sem("v_hid_ok"), sem("v_h_tr"), sem("v_hT_ok")
        dn_mm, y_ok, y_out, turn = sem("v_dn_mm"), sem("v_y_ok"), sem("v_y_out"), sem("v_turn")
        block = ph.enter_context(nc.Block())
        bank = lambda i, a=0, n=512, rows=P: g.ps[0:rows, i * 512 + a:i * 512 + a + n]
        turned = lambda i, n: bank(i, 0, n * CAP).rearrange("p (j t) -> p j t", j=n)
        X_BANK, UP_BANK, Y_BANK, H_BANK = 0, 2, 4, 6

        def blocks(eng, body):
            most = eng.value_load(g.most[0:1, 0:1], min_val=0, max_val=SLOTS)
            with eng.If(most > CAP):
                with eng.Fori(1, SLOTS // CAP) as c:
                    with eng.If(most > c * CAP):
                        with eng.Fori(0, EXPERTS) as e:
                            body((c - 1) * EXPERTS + e, e, c)
                        eng.sem_inc(g.settled, 1)
                    with eng.Else():
                        eng.sem_inc(g.settled, 1)
                    eng.sem_inc(g.settled, 1)
                eng.sem_inc(g.settled, 1)
            with eng.Else():
                eng.sem_inc(g.settled, 1)

        @block.sync
        def _(sp):
            table = g.table.rearrange("(e b s) r -> e b s r", e=EXPERTS, s=CAP)
            up = [a[0].rearrange("e (p j) f -> p e j f", j=DK) for a in (g.w1, g.w3)]
            down = g.w2[0].rearrange("e (p j) n -> p e j n", j=2)

            def body(k, e, c):
                sp.wait_ge(turn, k + 1)
                sp.dma_start(rec[:, :], table[bass.ds(e, 1), bass.ds(c, 1), :, :].rearrange("a b s r -> (a b s) r")
                             ).then_inc(rec_in, 16)
                for r in range(2):
                    sp.dma_start(g.r13[0][:, r, :, :], up[r][:, bass.ds(e, 1), :, :].rearrange("p a j f -> p (a j) f")
                                 ).then_inc(up_in, 16)
                sp.dma_start(g.r2[0][:, :, :], down[:, bass.ds(e, 1), :, :].rearrange("p a j n -> p (a j) n")
                             ).then_inc(down_in, 16)

            blocks(sp, body)

        @block.gpsimd
        def _(pool):
            pool.memset(x[:, :], 0.0).then_inc(x_zero, 1)
            pool.sem_inc(turn, 1)
            pool.wait_ge(x_zero, 1)

            def body(k, e, c):
                pool.wait_ge(rows_ok, k + 1)
                settle(pool, g)
                pool.indirect_dma_start(out=x[:, :], out_offset=None, in_=g.u2,
                                        in_offset=bass.IndirectOffsetOnAxis(ap=rows[:, 2:3], axis=0),
                                        bounds_check=SEQ - 1, oob_is_err=False).then_inc(x_in, 16)
                pool.wait_ge(y_ok, 2 * k + 2)
                settle(pool, g)
                pool.indirect_dma_start(out=g.y, out_offset=bass.IndirectOffsetOnAxis(ap=rows[:, 0:1], axis=0),
                                        in_=y[:, :], in_offset=None,
                                        bounds_check=2 * SEQ - 1, oob_is_err=False).then_inc(y_out, 16)
                pool.wait_ge(y_out, 16 * k + 16)
                pool.sem_inc(turn, 1)

            blocks(pool, body)

        @block.scalar
        def _(act):
            def body(k, e, c):
                for q in range(2):
                    act.wait_ge(x_tr, 2 * k + q + 1)
                    act.activation(xT[:, 4 * q:4 * q + 4, :], turned(X_BANK + q, 4), ACT.Copy).then_inc(xT_ok, 1)
                act.wait_ge(up_mm, k + 1)
                act.activation(sig[:, :], bank(UP_BANK, 0, DE, CAP), ACT.Sigmoid).then_inc(sig_ok, 1)
                act.wait_ge(h_tr, k + 1)
                act.activation(hT[:, :, :], turned(H_BANK, 2), ACT.Copy).then_inc(hT_ok, 1)
                for q in range(2):
                    act.wait_ge(dn_mm, 2 * k + q + 1)
                    act.activation(y[:, q * 512:(q + 1) * 512], bank(Y_BANK + q, rows=CAP), ACT.Copy,
                                   scale=rec[:, 1:2]).then_inc(y_ok, 1)

            blocks(act, body)

        @block.vector
        def _(dve):
            def body(k, e, c):
                dve.wait_ge(rec_in, 16 * k + 16)
                dve.tensor_copy(rows[:, :], rec[:, :]).then_inc(rows_ok, 1)
                dve.wait_ge(sig_ok, k + 1)
                dve.tensor_tensor(prod[:, :], sig[:, :], bank(UP_BANK, 0, DE, CAP), ALU.mult).then_inc(prod_ok, 1)
                dve.wait_ge(prod_ok, k + 1)
                dve.tensor_tensor(hid[:, :], prod[:, :], bank(UP_BANK, DE, DE, CAP), ALU.mult).then_inc(hid_ok, 1)

            blocks(dve, body)

        @block.tensor
        def _(pe):
            def body(k, e, c):
                pe.wait_ge(x_in, 16 * k + 16)
                settle(pe, g)
                for q in range(2):
                    for j in range(4):
                        ins = pe.transpose(bank(X_BANK + q, j * CAP, CAP), x[:, 4 * q + j::DK], g.ident[0:CAP, 0:CAP])
                    ins.then_inc(x_tr, 1)
                pe.wait_ge(up_in, 32 * k + 32)
                pe.wait_ge(xT_ok, 2 * k + 2)
                for j in range(DK):
                    ins = pe.matmul(bank(UP_BANK, rows=CAP).rearrange("p (r f) -> p r f", r=2), xT[:, j, :],
                                    g.r13[0][:, :, j, :], start=j == 0, stop=j == DK - 1)
                ins.then_inc(up_mm, 1)
                pe.wait_ge(hid_ok, k + 1)
                settle(pe, g)
                for j in range(2):
                    ins = pe.transpose(bank(H_BANK, j * CAP, CAP), hid[:, j::2], g.ident[0:CAP, 0:CAP])
                ins.then_inc(h_tr, 1)
                pe.wait_ge(down_in, 16 * k + 16)
                pe.wait_ge(hT_ok, k + 1)
                for q in range(2):
                    for j in range(2):
                        ins = pe.matmul(bank(Y_BANK + q, rows=CAP), hT[:, j, :], g.r2[0][:, j, q * 512:(q + 1) * 512],
                                        start=j == 0, stop=j == 1)
                    ins.then_inc(dn_mm, 1)

            blocks(pe, body)


def phase_final(nc, g):
    with ExitStack() as ph:
        sb = lambda n, s, d=F32: ph.enter_context(nc.sbuf_tensor(n, s, d))
        sem = semaphores(nc, ph)
        NB = 4
        h = [sb(f"z_h{b}", [P, D]) for b in range(NB)]
        y = [sb(f"z_y{b}", [P, 2, D]) for b in range(NB)]
        o = [sb(f"z_o{b}", [P, D]) for b in range(NB)]
        gain, junk = sb("z_gain", [P, D]), sb("z_junk", [P, D])
        st = [sb(f"z_stat{b}", [P, 2]) for b in range(NB)]
        gain_in = sem("z_gain_in")
        t_in = [sem(f"z_t_in{b}") for b in range(NB)]
        stored = [sem(f"z_stored{b}") for b in range(NB)]
        s0_ok, s1_ok, ss_ok, rt_ok, rc_ok, o_ok = (sem("z_s0_ok"), sem("z_s1_ok"), sem("z_ss_ok"), sem("z_rt_ok"),
                                                   sem("z_rc_ok"), sem("z_o_ok"))
        block = ph.enter_context(nc.Block())
        y_src = g.y.rearrange("(t c) d -> t c d", c=2)

        def rounds(eng, body):
            with eng.Fori(0, TT // NB) as i:
                for b in range(NB):
                    body(NB * i + b, b, i)

        @block.sync
        def _(sp):
            def load(t, b):
                sp.dma_start(h[b][:, :], g.h[bass.ds(t * P, P), :]).then_inc(t_in[b], 16)
                sp.dma_start(y[b][:, :, :], y_src[bass.ds(t * P, P), :, :]).then_inc(t_in[b], 16)

            load(0, 0)
            sp.dma_start(gain[:, :], g.final_norm[None, :].to_broadcast([P, D])).then_inc(gain_in, 16)
            for b in range(1, NB):
                load(b, b)
            with sp.Fori(0, TT // NB - 1) as i:
                for b in range(NB):
                    sp.wait_ge(o_ok, NB * i + b + 1)
                    load(NB * i + NB + b, b)

        @block.gpsimd
        def _(pool):
            def body(t, b, i):
                pool.wait_ge(o_ok, t + 1)
                settle(pool, g)
                pool.dma_start(g.out[0, bass.ds(t * P, P), :], o[b][:, :]).then_inc(stored[b], 16)

            rounds(pool, body)
            for b in range(NB):
                pool.wait_ge(stored[b], 16 * (TT // NB))

        @block.scalar
        def _(act):
            def body(t, b, i):
                act.wait_ge(s1_ok, t + 1)
                act.activation(junk[:, :], h[b][:, :], ACT.Square, accum_out=st[b][:, 0:1]).then_inc(ss_ok, 1)
                act.wait_ge(ss_ok, t + 1)
                act.activation(st[b][:, 1:2], st[b][:, 0:1], ACT.Sqrt, scale=1.0 / D, bias=g.eps[:, :]).then_inc(rt_ok, 1)

            rounds(act, body)

        @block.vector
        def _(dve):
            dve.wait_ge(gain_in, 16)

            def body(t, b, i):
                dve.wait_ge(t_in[b], 32 * i + 32)
                for c, done in ((0, s0_ok), (1, s1_ok)):
                    dve.tensor_tensor(h[b][:, :], h[b][:, :], y[b][:, c, :], ALU.add).then_inc(done, 1)
                    dve.wait_ge(done, t + 1)
                dve.wait_ge(rt_ok, t + 1)
                dve.reciprocal(st[b][:, 1:2], st[b][:, 1:2]).then_inc(rc_ok, 1)
                dve.wait_ge(rc_ok, t + 1)
                wait(dve, stored[b], 16 * i)
                dve.scalar_tensor_tensor(out=o[b][:, :], in0=h[b][:, :], scalar=st[b][:, 1:2], in1=gain[:, :],
                                         op0=ALU.mult, op1=ALU.mult).then_inc(o_ok, 1)

            for b in range(NB):
                body(b, b, 0)
            with dve.Fori(1, TT // NB) as i:
                for b in range(NB):
                    body(NB * i + b, b, i)


def program(nc, a, out):
    g = Ctx(a, out)
    g.gates = nc.dram_tensor("gates", [2 * D, SEQ], F32, kind="Internal").ap()
    g.merged = nc.dram_tensor("merged", [D, SEQ], F32, kind="Internal").ap()
    g.h = nc.dram_tensor("h_mid", [SEQ, D], F32, kind="Internal").ap()
    g.u2 = nc.dram_tensor("u_moe", [SEQ, D], F32, kind="Internal").ap()
    g.y = nc.dram_tensor("y_moe", [2 * SEQ, D], F32, kind="Internal").ap()
    g.table = nc.dram_tensor("slots", [EXPERTS * SLOTS, ROWS], F32, kind="Internal").ap()
    with ExitStack() as keep:
        g.most = keep.enter_context(nc.sbuf_tensor("most", [P, 1], I32))
        g.ident = keep.enter_context(nc.sbuf_tensor("ident", [P, P], F32))
        g.ones = keep.enter_context(nc.sbuf_tensor("ones", [P, P], F32))
        g.eps = keep.enter_context(nc.sbuf_tensor("eps", [P, 1], F32))
        g.settled = keep.enter_context(nc.semaphore("settled"))
        g.ps = keep.enter_context(nc.psum_tensor("ps", [P, 8 * 512], F32))
        left = lambda st, n, sh, d=F32: st.enter_context(nc.sbuf_tensor(n, sh, d))
        oh = ExitStack()
        g.ohTh, g.ohTl = left(oh, "ohTh", [P, HG, SEQ], F32R), left(oh, "ohTl", [P, HG, SEQ], F32R)
        with ExitStack() as ust:
            g.uTh = ust.enter_context(nc.sbuf_tensor("uTh", [P, DK, NT], F32R, side="right"))
            g.uTl = ust.enter_context(nc.sbuf_tensor("uTl", [P, DK, NT], F32R, side="right"))
            phase_norm_in(nc, g)
            phase_gates(nc, g)
            phase_hgrn(nc, g)
            lat = ExitStack()
            g.cqh, g.cql = left(lat, "cqh", [P, 3, SEQ], F32R), left(lat, "cql", [P, 3, SEQ], F32R)
            g.ckh, g.ckl = left(lat, "ckh", [P, 2, NT], F32R), left(lat, "ckl", [P, 2, NT], F32R)
            g.kpe = left(lat, "kpe", [QH, NT])
            g.cos, g.sin = left(lat, "cos", [QH, NT]), left(lat, "sin", [QH, NT])
            phase_latents(nc, g)
        with ExitStack() as qkv:
            right = lambda n, sh: qkv.enter_context(nc.sbuf_tensor(n, sh, F32, side="right"))
            g.QT, g.KT = right("QT", [QH, HEADS, SEQ]), right("KT", [QH, HEADS, NT])
            g.V = right("V", [P, HEADS // 2, TT + 1, VD + P])
            phase_heads(nc, g)
            lat.close()
            om = ExitStack()
            g.omTh, g.omTl = left(om, "omTh", [P, 4, SEQ], F32R), left(om, "omTl", [P, 4, SEQ], F32R)
            phase_attention(nc, g)
        wo = ExitStack()
        g.woh = wo.enter_context(nc.sbuf_tensor("woh", [P, DK, D], F32R, side="right"))
        g.wol = wo.enter_context(nc.sbuf_tensor("wol", [P, DK, D], F32R, side="right"))
        phase_merge(nc, g)
        om.close()
        oh.close()
        wraw = ExitStack()
        g.r13 = [left(wraw, f"r13_{b}", [P, 2, DK, DE]) for b in range(2)]
        g.r2 = [left(wraw, f"r2_{b}", [P, 2, D]) for b in range(2)]
        g.w_up_in = [keep.enter_context(nc.semaphore(f"w_up_in{b}")) for b in range(2)]
        g.w_down_in = [keep.enter_context(nc.semaphore(f"w_down_in{b}")) for b in range(2)]
        g.load_up, g.load_down = expert_loaders(g)
        phase_output(nc, g)
        wo.close()
        phase_experts(nc, g)
        phase_overflow(nc, g)
        wraw.close()
        phase_final(nc, g)

_INPUTS = ["x", "meta_tokens", "attn_norm", "w_in", "q_norm", "w_uq", "kv_norm", "w_ukv", "lb_table", "hg_norm",
           "w_br_mla", "w_br_hgrn", "b_gate", "w_out", "ffn_norm", "w_group", "b_group", "w_route", "b_route",
           "w1", "w3", "w2", "final_norm"]


def rotary():
    inv = (np.float32(10000.0) ** (-np.arange(0, ROPE, 2, dtype=np.float32) / np.float32(ROPE))).astype(np.float32)
    pos = np.concatenate([np.arange(META, META + SEQ), np.arange(META)]).astype(np.float32)
    ang = (inv[:, None] * pos[None, :]).astype(np.float32)
    cos, sin = np.cos(ang), np.sin(ang)
    return (np.concatenate([cos, cos], 0).astype(np.float32), np.concatenate([-sin, sin], 0).astype(np.float32))


def kernel(**inputs):
    import concourse.bacc as bacc
    from concourse.bass_utils import run_bass_kernel_spmd

    nc = bacc.Bacc("TRN2", target_bir_lowering=False, num_devices=1)
    arrays, aps = {}, {}
    cos, sin = rotary()
    for name in _INPUTS + ["rope_cos", "rope_sin"]:
        a = cos if name == "rope_cos" else sin if name == "rope_sin" else np.ascontiguousarray(inputs[name])
        arrays["in_" + name] = a
        aps[name] = nc.dram_tensor("in_" + name, a.shape, mybir.dt.from_np(a.dtype), kind="ExternalInput").ap()
    out = nc.dram_tensor("out_0", (1, SEQ, D), F32, kind="ExternalOutput").ap()
    program(nc, aps, out)
    r = run_bass_kernel_spmd(nc, [arrays], core_ids=[0])
    return r.results[0]["out_0"]
```
